# Optimizing a Trainium2 kernel written in Bass

```python
import jax, jax.numpy as jnp
from jax import lax
import numpy as np

D_MODEL = 2048
BATCH = 1
SEQ = 512
DEPTH = 1

NSA_HEADS = 16
NSA_GROUPS = 4
NSA_HPG = NSA_HEADS // NSA_GROUPS
NSA_DIM = 64
NSA_WIDTH = NSA_HEADS * NSA_DIM
KV_WIDTH = NSA_GROUPS * NSA_DIM
N_KV_STREAMS = 6
CMP_BLOCK = 32
CMP_STRIDE = 16
CMP_HIDDEN = 256
SEL_BLOCK = 64
SEL_TOPK = 16
WINDOW = 512
QUERY_BLOCK = 128
SGU_GROUPS = 8
SGU_GROUP_DIM = 128
SGU_WIDTH = SGU_GROUPS * SGU_GROUP_DIM
SGU_CHUNK = 128
N_BRANCHES = 2
MEM_TOKENS = 256
MEM_HEADS = 4
MEM_DIM = 128
MEM_WIDTH = MEM_HEADS * MEM_DIM
FFN_HIDDEN = (8 * D_MODEL + 3 * 256 - 1) // (3 * 256) * 256

NORM_EPS = 1e-6
MASK_VALUE = -1e30
FORCED_SCORE = 1e6
IN_SPLITS = (NSA_WIDTH, N_KV_STREAMS * KV_WIDTH, NSA_HEADS * 3, SGU_WIDTH, SGU_WIDTH, N_BRANCHES * D_MODEL)
IN_WIDTH = sum(IN_SPLITS)

kernel_name = "hybrid_nsa_sgu_gated_block"

def rmsnorm(x, g):
    xf = x.astype(jnp.float32)
    y = xf * lax.rsqrt(jnp.mean(xf * xf, axis=-1, keepdims=True) + NORM_EPS)
    return (y * g.astype(jnp.float32)).astype(x.dtype)

def layernorm(x, g, b):
    xf = x.astype(jnp.float32)
    mu = jnp.mean(xf, axis=-1, keepdims=True)
    var = jnp.mean(jnp.square(xf - mu), axis=-1, keepdims=True)
    y = (xf - mu) * lax.rsqrt(var + NORM_EPS)
    return (y * g.astype(jnp.float32) + b.astype(jnp.float32)).astype(x.dtype)

def masked_softmax(s, mask):
    s = jnp.where(mask, s.astype(jnp.float32), MASK_VALUE)
    p = jax.nn.softmax(s, axis=-1)
    return jnp.where(mask, p, 0.0)

def compress_blocks(kv, pe, w1, b1, w2):
    b, s = kv.shape[:2]
    nc = (s - CMP_BLOCK) // CMP_STRIDE + 1
    idx = jnp.arange(nc)[:, None] * CMP_STRIDE + jnp.arange(CMP_BLOCK)[None, :]
    blocks = kv[:, idx] + pe[None, None, :, None, :]
    blocks = blocks.transpose(0, 3, 1, 2, 4).reshape(b, NSA_GROUPS, nc, CMP_BLOCK * NSA_DIM)
    hid = jax.nn.gelu(blocks @ w1 + b1)
    return hid @ w2

def block_coverage(nc, nb):
    cs = np.arange(nc)[:, None] * CMP_STRIDE
    ss = np.arange(nb)[None, :] * SEL_BLOCK
    cov = np.clip(np.minimum(cs + CMP_BLOCK, ss + SEL_BLOCK) - np.maximum(cs, ss), 0, None) / CMP_BLOCK
    return jnp.asarray(cov, dtype=jnp.float32)

def nsa_attention(q, kc, vc, ks, vs, kw, vw, gates):
    b, s = q.shape[:2]
    nqb = s // QUERY_BLOCK
    nc = kc.shape[2]
    nb = s // SEL_BLOCK
    topk = min(SEL_TOPK, nb)
    cov = block_coverage(nc, nb)
    q_blocks = (q * (NSA_DIM ** -0.5)).reshape(b, nqb, QUERY_BLOCK, NSA_GROUPS, NSA_HPG, NSA_DIM)
    q_blocks = q_blocks.transpose(1, 0, 3, 4, 2, 5)
    ks_blocks = ks.transpose(0, 2, 1, 3).reshape(b, NSA_GROUPS, nb, SEL_BLOCK, NSA_DIM)
    vs_blocks = vs.transpose(0, 2, 1, 3).reshape(b, NSA_GROUPS, nb, SEL_BLOCK, NSA_DIM)
    pad = ((0, 0), (WINDOW, 0), (0, 0), (0, 0))
    kw_pad = jnp.pad(kw, pad).transpose(0, 2, 1, 3)
    vw_pad = jnp.pad(vw, pad).transpose(0, 2, 1, 3)
    cmp_end = jnp.arange(nc) * CMP_STRIDE + CMP_BLOCK - 1
    blk = jnp.arange(nb)
    b_idx = jnp.arange(b)[:, None, None, None]
    g_idx = jnp.arange(NSA_GROUPS)[None, :, None, None]
    sel_off = jnp.arange(SEL_BLOCK)
    win_off = jnp.arange(QUERY_BLOCK + WINDOW)

    def block_fn(args):
        qb, i = args
        start = i * QUERY_BLOCK
        t = start + jnp.arange(QUERY_BLOCK)
        s_c = jnp.einsum('bghqd,bgnd->bghqn', qb, kc)
        p_c = masked_softmax(s_c, cmp_end[None, :] <= t[:, None])
        o_c = jnp.einsum('bghqn,bgnd->bghqd', p_c.astype(vc.dtype), vc)
        imp = jnp.einsum('bghqn,nj->bgqj', p_c, cov)
        jt = (t // SEL_BLOCK)[:, None]
        forced = (blk == 0) | (blk == jt) | (blk == jt - 1)
        score = jnp.where(forced, FORCED_SCORE, jnp.where(blk <= jt, imp, -1.0))
        _, idx = lax.top_k(score, topk)
        k_sel = ks_blocks[b_idx, g_idx, idx].reshape(b, NSA_GROUPS, QUERY_BLOCK, topk * SEL_BLOCK, NSA_DIM)
        v_sel = vs_blocks[b_idx, g_idx, idx].reshape(b, NSA_GROUPS, QUERY_BLOCK, topk * SEL_BLOCK, NSA_DIM)
        pos = (idx[..., None] * SEL_BLOCK + sel_off).reshape(b, NSA_GROUPS, QUERY_BLOCK, topk * SEL_BLOCK)
        mask_s = pos <= t[:, None]
        s_s = jnp.einsum('bghqd,bgqkd->bghqk', qb, k_sel)
        p_s = masked_softmax(s_s, mask_s[:, :, None])
        o_s = jnp.einsum('bghqk,bgqkd->bghqd', p_s.astype(v_sel.dtype), v_sel)
        k_w = lax.dynamic_slice_in_dim(kw_pad, start, QUERY_BLOCK + WINDOW, axis=2)
        v_w = lax.dynamic_slice_in_dim(vw_pad, start, QUERY_BLOCK + WINDOW, axis=2)
        kpos = start - WINDOW + win_off
        mask_w = (kpos[None, :] <= t[:, None]) & (kpos[None, :] > t[:, None] - WINDOW) & (kpos[None, :] >= 0)
        s_w = jnp.einsum('bghqd,bgkd->bghqk', qb, k_w)
        p_w = masked_softmax(s_w, mask_w)
        o_w = jnp.einsum('bghqk,bgkd->bghqd', p_w.astype(v_w.dtype), v_w)
        return (o_c, o_s, o_w)

    o_c, o_s, o_w = lax.map(block_fn, (q_blocks, jnp.arange(nqb, dtype=jnp.int32)))

    def unblock(o):
        return o.transpose(1, 0, 4, 2, 3, 5).reshape(b, s, NSA_HEADS, NSA_DIM)

    out = gates[..., 0:1] * unblock(o_c) + gates[..., 1:2] * unblock(o_s) + gates[..., 2:3] * unblock(o_w)
    return out.reshape(b, s, NSA_WIDTH)

def spatial_gating(u, v, ln_g, ln_b, ws, bs):
    b, s, _ = v.shape
    v = layernorm(v, ln_g, ln_b)
    vc = v.reshape(b, s // SGU_CHUNK, SGU_CHUNK, SGU_GROUPS, SGU_GROUP_DIM)
    tri = jnp.tril(jnp.ones((SGU_CHUNK, SGU_CHUNK), dtype=bool))
    w = jnp.where(tri, ws, 0.0)
    mixed = jnp.einsum('gts,bcsgd->bctgd', w, vc) + bs.T[None, None, :, :, None]
    return u * mixed.reshape(b, s, SGU_WIDTH)

def setup_inputs(seed: int = 0) -> dict:
    key = jax.random.key(seed)
    ks = jax.random.split(key, 32)

    def nrm(k, shape, scale):
        return jax.random.normal(k, shape, jnp.float32) * scale

    def gain(k, shape):
        return 1.0 + 0.1 * jax.random.normal(k, shape, jnp.float32)

    L = DEPTH
    return {
        "x": nrm(ks[0], (BATCH, SEQ, D_MODEL), 1.0),
        "mem": nrm(ks[1], (BATCH, MEM_TOKENS, D_MODEL), 1.0),
        "norm_mix_g": gain(ks[2], (L, D_MODEL)),
        "w_in": nrm(ks[3], (L, D_MODEL, IN_WIDTH), D_MODEL ** -0.5),
        "cmp_pe_k": nrm(ks[4], (L, CMP_BLOCK, NSA_DIM), 0.5),
        "cmp_k_w1": nrm(ks[5], (L, CMP_BLOCK * NSA_DIM, CMP_HIDDEN), (CMP_BLOCK * NSA_DIM) ** -0.5),
        "cmp_k_b1": nrm(ks[6], (L, CMP_HIDDEN), 0.01),
        "cmp_k_w2": nrm(ks[7], (L, CMP_HIDDEN, NSA_DIM), CMP_HIDDEN ** -0.5),
        "cmp_pe_v": nrm(ks[8], (L, CMP_BLOCK, NSA_DIM), 0.5),
        "cmp_v_w1": nrm(ks[9], (L, CMP_BLOCK * NSA_DIM, CMP_HIDDEN), (CMP_BLOCK * NSA_DIM) ** -0.5),
        "cmp_v_b1": nrm(ks[10], (L, CMP_HIDDEN), 0.01),
        "cmp_v_w2": nrm(ks[11], (L, CMP_HIDDEN, NSA_DIM), CMP_HIDDEN ** -0.5),
        "sgu_ln_g": gain(ks[12], (L, SGU_WIDTH)),
        "sgu_ln_b": nrm(ks[13], (L, SGU_WIDTH), 0.01),
        "sgu_ws": nrm(ks[14], (L, SGU_GROUPS, SGU_CHUNK, SGU_CHUNK), SGU_CHUNK ** -0.5),
        "sgu_b": gain(ks[15], (L, SGU_GROUPS, SGU_CHUNK)),
        "w_proj_a": nrm(ks[16], (L, NSA_WIDTH, D_MODEL), NSA_WIDTH ** -0.5),
        "w_proj_b": nrm(ks[17], (L, SGU_WIDTH, D_MODEL), SGU_WIDTH ** -0.5),
        "w_mix_out": nrm(ks[18], (L, D_MODEL, D_MODEL), D_MODEL ** -0.5),
        "norm_cross_g": gain(ks[19], (L, D_MODEL)),
        "norm_mem_g": gain(ks[20], (L, D_MODEL)),
        "w_mq": nrm(ks[21], (L, D_MODEL, MEM_WIDTH), D_MODEL ** -0.5),
        "w_mkv": nrm(ks[22], (L, D_MODEL, 2 * MEM_WIDTH), D_MODEL ** -0.5),
        "w_mo": nrm(ks[23], (L, MEM_WIDTH, D_MODEL), MEM_WIDTH ** -0.5),
        "norm_ffn_g": gain(ks[24], (L, D_MODEL)),
        "w_ffn_in": nrm(ks[25], (L, D_MODEL, 2 * FFN_HIDDEN), D_MODEL ** -0.5),
        "w_ffn_out": nrm(ks[26], (L, FFN_HIDDEN, D_MODEL), FFN_HIDDEN ** -0.5),
        "norm_final_g": gain(ks[27], (D_MODEL,)),
    }

def reference(x, mem, norm_mix_g, w_in, cmp_pe_k, cmp_k_w1, cmp_k_b1, cmp_k_w2, cmp_pe_v, cmp_v_w1, cmp_v_b1, cmp_v_w2,
              sgu_ln_g, sgu_ln_b, sgu_ws, sgu_b, w_proj_a, w_proj_b, w_mix_out, norm_cross_g, norm_mem_g,
              w_mq, w_mkv, w_mo, norm_ffn_g, w_ffn_in, w_ffn_out, norm_final_g):
    b, s, _ = x.shape
    split_points = np.cumsum(IN_SPLITS)[:-1].tolist()
    for l in range(DEPTH):
        h = rmsnorm(x, norm_mix_g[l])
        proj = h @ w_in[l]
        q, kv, nsa_g, u, v, merge_g = jnp.split(proj, split_points, axis=-1)
        q = q.reshape(b, s, NSA_HEADS, NSA_DIM)
        kv = kv.reshape(b, s, N_KV_STREAMS, NSA_GROUPS, NSA_DIM)
        kc = compress_blocks(kv[:, :, 0], cmp_pe_k[l], cmp_k_w1[l], cmp_k_b1[l], cmp_k_w2[l])
        vc = compress_blocks(kv[:, :, 1], cmp_pe_v[l], cmp_v_w1[l], cmp_v_b1[l], cmp_v_w2[l])
        nsa_gates = jax.nn.sigmoid(nsa_g.reshape(b, s, NSA_HEADS, 3))
        o_a = nsa_attention(q, kc, vc, kv[:, :, 2], kv[:, :, 3], kv[:, :, 4], kv[:, :, 5], nsa_gates)
        o_b = spatial_gating(jax.nn.gelu(u), jax.nn.gelu(v), sgu_ln_g[l], sgu_ln_b[l], sgu_ws[l], sgu_b[l])
        g = jax.nn.sigmoid(merge_g).reshape(b, s, N_BRANCHES, D_MODEL)
        merged = g[:, :, 0] * (o_a @ w_proj_a[l]) + g[:, :, 1] * (o_b @ w_proj_b[l])
        x = x + merged @ w_mix_out[l]
        hx = rmsnorm(x, norm_cross_g[l])
        hm = rmsnorm(mem, norm_mem_g[l])
        mq = (hx @ w_mq[l]).reshape(b, s, MEM_HEADS, MEM_DIM) * (MEM_DIM ** -0.5)
        mk, mv = jnp.split(hm @ w_mkv[l], 2, axis=-1)
        mk = mk.reshape(b, -1, MEM_HEADS, MEM_DIM)
        mv = mv.reshape(b, -1, MEM_HEADS, MEM_DIM)
        sc = jnp.einsum('bshd,bmhd->bhsm', mq, mk).astype(jnp.float32)
        p = jax.nn.softmax(sc, axis=-1)
        mo = jnp.einsum('bhsm,bmhd->bshd', p.astype(mv.dtype), mv).reshape(b, s, MEM_WIDTH)
        x = x + mo @ w_mo[l]
        hf = rmsnorm(x, norm_ffn_g[l])
        gt, up = jnp.split(hf @ w_ffn_in[l], 2, axis=-1)
        x = x + (jax.nn.silu(gt) * up) @ w_ffn_out[l]
    return rmsnorm(x, norm_final_g)


_drawn_inputs = setup_inputs


def setup_inputs(seed=0):
    import zlib

    import numpy as np

    out = dict(_drawn_inputs(seed))
    spreads = {}
    factors = {'cmp_pe_k': 5.584,
     'cmp_k_b1': 64.0,
     'cmp_v_b1': 8.0,
     'sgu_ln_b': 8.0,
     'norm_cross_g': 5.395,
     'norm_mem_g': 3.731}
    for name, (base, spread) in spreads.items():
        noise = np.random.default_rng([zlib.crc32(name.encode()), seed]).standard_normal(out[name].shape)
        drawn = base * np.exp(spread * noise) if base else spread * noise
        out[name] = __import__('jax').numpy.asarray(drawn.astype(out[name].dtype))
    for name, factor in factors.items():
        out[name] = (out[name] * factor).astype(out[name].dtype)
    return out
```

```python
import concourse.bass as bass
from concourse import mybir
from contextlib import ExitStack

F32 = mybir.dt.float32
F32R = mybir.dt.float32r
BF16 = mybir.dt.bfloat16
ACT = mybir.ActivationFunctionType
ALU = mybir.AluOpType
AX = mybir.AxisListType

P = 128
T = 512
TC = T // P
D = 2048
DK = D // P
MEM = 256
MC = MEM // P
HEADS, GROUPS, HD = 16, 4, 64
HPG = HEADS // GROUPS
CMP_LEN, CMP_STEP = 32, 16
NCMP = (T - CMP_LEN) // CMP_STEP + 1
CMP_HID = 256
SG = 8
MH = 4
FF = (8 * D + 3 * 256 - 1) // (3 * 256) * 256
FK = FF // P
FFN_CHUNKS = (16, 16, 12)
EPS = 1e-6
MASKED = -1e30
KIB = 1024

C_Q, C_KV = 0, 1024
C_NSA_GATE = C_KV + 6 * 256
C_U = C_NSA_GATE + 48
C_V = C_U + 1024
C_MERGE = C_V + 1024

assert sum(FFN_CHUNKS) == FK and T // 64 <= 16 and T <= 512


class Phase:

    def __init__(self, prev, panels, quarters=4, groups=1, dmas=1):
        self.n, self.nq, self.ng, self.nd = panels, quarters, groups, dmas
        if prev is None:
            self.panel0 = self.quarter0 = self.group0 = 0
            self.landed0 = (0, 0)
        else:
            self.panel0 = prev.panel0 + prev.n
            self.quarter0 = prev.quarter0 + prev.n * prev.nq
            self.group0 = prev.group0 + prev.n * prev.ng
            used = [sum(1 for k in range(prev.n) if (prev.panel0 + k) % 2 == s) for s in (0, 1)]
            self.landed0 = tuple(prev.landed0[s] + 16 * prev.nd * used[s] for s in (0, 1))
        self.first = prev is None

    def slot(self, u):
        return (self.panel0 + u) % 2

    def landed(self, i, u):
        return self.landed0[self.slot(u)] + 16 * self.nd * (i + 1)

    def quarter(self, i, u):
        return self.quarter0 + self.nq * (2 * i + u)

    def group(self, i, u):
        return self.group0 + self.ng * (2 * i + u)

    def end(self):
        return self.quarter0 + self.n * self.nq

    def groups_end(self):
        return self.group0 + self.n * self.ng


def plan():
    ph, prev = {}, None
    for name, args in (
        ("merge", (32,)), ("sv", (8,)), ("su", (8,)), ("q", (8,)), ("c", (4,)), ("k", (4,)),
        ("v", (4,)), ("g", (1,)), ("ab", (16, 4, 2, 2)), ("wo", (16,)), ("mk", (4,)), ("mv", (4,)),
        ("mq", (4,)), ("mo", (4, 4, 4, 4)),
    ):
        prev = ph[name] = Phase(prev, *args)
    for c, nk in enumerate(FFN_CHUNKS):
        prev = ph[f"f{c}"] = Phase(prev, 2 * nk)
        prev = ph[f"o{c}"] = Phase(prev, DK, nk // 4)
    return ph


def build(nc, x, mem, norm_mix_g, w_in, cmp_pe_k, cmp_k_w1, cmp_k_b1, cmp_k_w2, cmp_pe_v, cmp_v_w1,
          cmp_v_b1, cmp_v_w2, sgu_ln_g, sgu_ln_b, sgu_ws, sgu_b, w_proj_a, w_proj_b, w_mix_out,
          norm_cross_g, norm_mem_g, w_mq, w_mkv, w_mo, norm_ffn_g, w_ffn_in, w_ffn_out,
          norm_final_g, out):
    PH = plan()
    ds = bass.ds
    with ExitStack() as ctx:
        def sem(name):
            return ctx.enter_context(nc.semaphore(name))

        base = (nc.sbuf_base + 63) // 64 * 64
        A = base + 32 * KIB
        B = A + 64 * KIB
        B2 = B + 32 * KIB
        C = B + 64 * KIB
        K = C + 40 * KIB

        def at(name, shape, dt, offset):
            return nc.alloc_sbuf_tensor_at(name, shape, dt, offset=offset)

        raw = at("raw", [P, 2, 16, P], F32, base)
        w_hi = at("w_hi", [P, 4, 4, P], F32R, base + 16 * KIB)
        w_lo = at("w_lo", [P, 4, 4, P], F32R, base + 24 * KIB)

        act_hi = at("act_hi", [P, DK, T], F32R, A)
        act_lo = at("act_lo", [P, DK, T], F32R, A + 32 * KIB)

        x_rows = at("x_rows", [P, TC, D], F32, B)
        junk = at("junk", [P, D], F32, B2)
        small_rows = at("small_rows", [116, P], F32, C)
        v_rows = at("v_rows", [P, TC, 1024], F32, C)
        ln_g_bc = at("ln_g_bc", [P, 1024], F32, C + 16 * KIB)
        ln_b_bc = at("ln_b_bc", [P, 1024], F32, C + 20 * KIB)
        ws_rows = at("ws_rows", [P, SG, P], F32, C + 24 * KIB)
        gate_out = at("gate_out", [P, 2, T], F32, C + 28 * KIB)
        vt = at("vt", [P, 2, T], F32, B2)
        ut = at("ut", [P, 2, T], F32, B2 + 4 * KIB)
        vz = at("vz", [P, 2, TC, P], F32, B2 + 8 * KIB)
        vn = at("vn", [P, 2, TC, P], F32, B2 + 12 * KIB)
        mixed = at("mixed", [P, 2, TC, P], F32, B2 + 16 * KIB)
        ob = at("ob", [P, 2, T], F32, B2 + 20 * KIB)
        ws_t = at("ws_t", [P, SG, P], F32, B2 + 24 * KIB)
        sgu_b_bc = at("sgu_b_bc", [P, SG, P], F32, B2 + 28 * KIB)
        ob_hi = at("ob_hi", [P, SG, T], F32R, B)
        ob_lo = at("ob_lo", [P, SG, T], F32R, B + 16 * KIB)
        q_t = at("q_t", [P, 8, T], F32, C)
        k_t = at("k_t", [P, 2, 2, T], F32, C + 16 * KIB)
        v_kv = at("v_kv", [P, 2, TC, 256], F32, C + 24 * KIB)
        kv_src = at("kv_src", [P, 2, GROUPS, T], F32, B2 + 8 * KIB)
        gate_t = at("gate_t", [48, T], F32, B2 + 24 * KIB)
        w1 = [at(f"w1_{s}", [P, 16, CMP_HID], F32, A + 16 * KIB * s) for s in range(2)]
        blocks = [at(f"blocks_{s}", [P, 16, GROUPS, NCMP], F32, A + 32 * KIB + 8 * KIB * s) for s in range(2)]
        hid_t = [at(f"hid_t_{s}", [P, 2, GROUPS * NCMP], F32, A + 48 * KIB + KIB * s) for s in range(2)]
        qs = at("qs", [HD, 2, HPG, T], F32, A)
        kg = at("kg", [HD, 2, 2, T], F32, A + 16 * KIB)
        vg = at("vg", [P, 2, 2, TC, HD], F32, A + 24 * KIB)
        prob = at("prob", [P, 3, T], F32, A + 28 * KIB)
        prob_t = at("prob_t", [P, 3, TC, P], F32, A + 34 * KIB)
        o_rows = at("o_rows", [P, 2, P], F32, A + 40 * KIB)
        o_parts = at("o_parts", [P, 2, 2, 3, HD], F32, A + 41 * KIB)
        kcg = at("kcg", [HD, 2, NCMP], F32, A + 44 * KIB)
        vcg = at("vcg", [NCMP, 2, HD], F32, A + 45 * KIB)
        oa_hi = at("oa_hi", [P, 8, T], F32R, B2)
        oa_lo = at("oa_lo", [P, 8, T], F32R, B2 + 16 * KIB)
        gate_in = at("gate_in", [P, 2, 2, T], F32, C)
        pa = at("pa", [P, 2, T], F32, C + 8 * KIB)
        pb = at("pb", [P, 2, T], F32, C + 12 * KIB)
        merged = at("merged", [P, 2, T], F32, C + 16 * KIB)
        mem_rows = at("mem_rows", [P, MC, D], F32, C + 20 * KIB)
        x_cols = at("x_cols", [P, 2, TC, P], F32, C + 36 * KIB)
        xt = at("xt", [P, DK, T], F32, B)
        sq = at("sq", [P, 2, T], F32, C)
        sumsq = at("sumsq", [P, T], F32, C + 4 * KIB)
        rms_bc = at("rms_bc", [P, T], F32, C + 6 * KIB)
        xg = at("xg", [P, 2, T], F32, C + 8 * KIB)
        hm_hi = at("hm_hi", [P, DK, MEM], F32R, B2)
        hm_lo = at("hm_lo", [P, DK, MEM], F32R, B2 + 16 * KIB)
        mq_t = at("mq_t", [P, MH, T], F32, C + 12 * KIB)
        mk_t = at("mk_t", [P, MH, MEM], F32, C + 20 * KIB)
        mv_rows = at("mv_rows", [P, MC, 512], F32, C + 24 * KIB)
        mv_t = at("mv_t", [P, 2, MEM], F32, C + 28 * KIB)
        add_in = at("add_in", [P, 2, T], F32, C + 32 * KIB)
        mo_hi = at("mo_hi", [P, MH, T], F32R, A)
        mo_lo = at("mo_lo", [P, MH, T], F32R, A + 8 * KIB)
        mem_junk = at("mem_junk", [P, D], F32, A + 48 * KIB)
        m_prob = at("m_prob", [P, 3, MEM], F32, A + 16 * KIB)
        m_prob_n = at("m_prob_n", [P, 3, MEM], F32, A + 20 * KIB)
        m_prob_t = at("m_prob_t", [P, 3, MC, P], F32, A + 24 * KIB)
        ff_hi = at("ff_hi", [P, 16, T], F32R, B2)
        ff_lo = at("ff_lo", [P, 16, T], F32R, C)
        gated = at("gated", [P, T], F32, C + 32 * KIB)
        up = at("up", [P, T], F32, C + 34 * KIB)
        ff = at("ff", [P, T], F32, C + 36 * KIB)
        sumsq_f = at("sumsq_f", [P, T], F32, C + 38 * KIB)
        rms_f = at("rms_f", [P, T], F32, C)
        y_t = at("y_t", [P, DK, T], F32, A)
        y_rows = at("y_rows", [P, TC, D], F32, A + 32 * KIB)

        spot = [K]

        def const(name, shape, dt=F32):
            size = mybir.dt.size(dt)
            for n in shape[1:]:
                size *= n
            t = at(name, shape, dt, spot[0])
            spot[0] += (size + 31) // 32 * 32
            return t

        ident = const("ident", [P, P])
        ones = const("ones", [P, P])
        ident_b = const("ident_b", [P, P], BF16)
        causal_b = const("causal_b", [P, P], BF16)
        cmp_mask_b = const("cmp_mask_b", [P, TC, NCMP], BF16)
        valid = const("valid", [P, 1])
        eps = const("eps", [P, 1])
        cols = const("cols", [P, 116])
        ss = const("ss", [P, TC])
        rstd = const("rstd", [P, TC])
        bn = const("bn", [P, TC, 2, 6])
        mv_stat = const("mv_stat", [P, TC, 2])
        ln_rstd = const("ln_rstd", [P, TC])
        ln_shift = const("ln_shift", [P, TC])
        gates = const("gates", [P, TC, 48])
        gg = const("gg", [P, 2, TC, 12])
        kc_t = const("kc_t", [HD, GROUPS * NCMP])
        vc = const("vc", [NCMP, GROUPS, HD])
        w2 = const("w2", [P, 2, 2, HD])
        neg_max = const("neg_max", [P, 4])
        den = const("den", [P, 2, 6])
        coef = const("coef", [P, 2, 6])
        assert spot[0] <= nc.sbuf_usable_end, spot[0]
        G_MIX, G_CROSS, G_MEM, G_FFN, G_FINAL, PE_K, PE_V, B1_K, B1_V = 0, 16, 32, 48, 64, 80, 96, 112, 114

        bank = [ctx.enter_context(nc.psum_tensor(f"bank{b}", [P, T], F32)) for b in range(8)]
        merge_dram = nc.dram_tensor("merge_gates", [2 * DK * P, T], F32, kind="Internal").ap()

        raw_landed = [sem("raw_landed0"), sem("raw_landed1")]
        hi_done = sem("hi_done")
        split_done = sem("split_done")
        quarters_done = sem("quarters_done")
        banks_read = sem("banks_read")
        ones_made = sem("ones_made")
        ident_zero = sem("ident_zero")
        ident_made = sem("ident_made")
        masks_zero = sem("masks_zero")
        masks_made = sem("masks_made")
        x_landed = [sem(f"x_landed{c}") for c in range(TC)]
        small_landed = sem("small_landed")
        sgu_landed = sem("sgu_landed")
        sq_done = sem("sq_done")
        rms_done = sem("rms_done")
        rstd_done = sem("rstd_done")
        x_scaled = sem("x_scaled")
        turned = sem("turned")
        turned_hi = sem("turned_hi")
        turned_lo = sem("turned_lo")
        cols_turned = sem("cols_turned")
        cols_ready = sem("cols_ready")
        ws_masked = sem("ws_masked")
        ws_turned = sem("ws_turned")
        ws_ready = sem("ws_ready")
        gate_stored = [sem("gate_stored0"), sem("gate_stored1")]
        v_turned = sem("v_turned")
        v_rows_done = sem("v_rows_done")
        ln_stats = sem("ln_stats")
        ln_sqrt = sem("ln_sqrt")
        ln_ready = sem("ln_ready")
        vz_done = sem("vz_done")
        vn_step = sem("vn_step")
        vn_done = sem("vn_done")
        mix_done = sem("mix_done")
        mix_copied = sem("mix_copied")
        ob_step = sem("ob_step")
        ob_done = sem("ob_done")
        ob_hi_done = sem("ob_hi_done")
        ob_lo_done = sem("ob_lo_done")
        kv_turned = sem("kv_turned")
        kv_rows_done = sem("kv_rows_done")
        gates_done = sem("gates_done")
        gates_masked = sem("gates_masked")
        w1_landed = sem("w1_landed")
        blocks_done = sem("blocks_done")
        hid_done = sem("hid_done")
        hid_act = sem("hid_act")
        cmp_out = sem("cmp_out")
        cmp_ready = sem("cmp_ready")
        staged_qk = sem("staged_qk")
        staged_v = sem("staged_v")
        sumsq_zero = sem("sumsq_zero")
        qk_done = sem("qk_done")
        max_done = sem("max_done")
        exp_done = sem("exp_done")
        pt_done = sem("pt_done")
        pt_copied = sem("pt_copied")
        pv_done = sem("pv_done")
        coef_step = sem("coef_step")
        o_summed = sem("o_summed")
        o_turned = sem("o_turned")
        oa_hi_done = sem("oa_hi_done")
        oa_lo_done = sem("oa_lo_done")
        gates_landed = [sem("gates_landed0"), sem("gates_landed1")]
        merge_step = sem("merge_step")
        merge_done = sem("merge_done")
        merge_hi_done = sem("merge_hi_done")
        merge_lo_done = sem("merge_lo_done")
        mem_landed = sem("mem_landed")
        mem_sq = sem("mem_sq")
        mem_rms = sem("mem_rms")
        mem_rstd = sem("mem_rstd")
        mem_scaled = sem("mem_scaled")
        mem_turned = sem("mem_turned")
        mem_hi = sem("mem_hi")
        mem_lo = sem("mem_lo")
        xcol_landed = [sem("xcol_landed0"), sem("xcol_landed1")]
        squared = sem("squared")
        summed = sem("summed")
        norm_sum = sem("norm_sum")
        norm_root = sem("norm_root")
        norm_inv = sem("norm_inv")
        xg_done = sem("xg_done")
        xg_hi = sem("xg_hi")
        xg_lo = sem("xg_lo")
        mvt_turned = sem("mvt_turned")
        mv_ready = sem("mv_ready")
        m_qk = sem("m_qk")
        m_max = sem("m_max")
        m_exp = sem("m_exp")
        m_inv = sem("m_inv")
        m_norm = sem("m_norm")
        m_pt = sem("m_pt")
        m_ptc = sem("m_ptc")
        m_pv = sem("m_pv")
        mo_hi_done = sem("mo_hi_done")
        mo_lo_done = sem("mo_lo_done")
        copied = sem("copied")
        added = sem("added")
        gated_done = sem("gated_done")
        ff_done = sem("ff_done")
        ff_hi_done = sem("ff_hi_done")
        ff_lo_done = sem("ff_lo_done")
        y_done = sem("y_done")
        y_turned = sem("y_turned")
        y_copied = sem("y_copied")
        stored = sem("stored")

        block = ctx.enter_context(nc.Block())

        def wait(eng, s, value):
            if not isinstance(value, int) or value > 0:
                eng.wait_ge(s, value)

        def runs(eng, n, body, peel=False):
            if peel:
                body(0)
            if n - peel > 0:
                with eng.Fori(1 if peel else 0, n) as i:
                    body(i)

        ITEMS = 96
        items = [(f, pr, qi, e, b) for f in range(2) for pr in range(2) for qi in range(TC)
                 for e in range(2) for b in (1, 2, 0)]

        w_in_v = w_in[0].rearrange("(k p) n -> p k n", p=P)
        wa_v = w_proj_a[0].rearrange("(k p) n -> p k n", p=P)
        wb_v = w_proj_b[0].rearrange("(k p) n -> p k n", p=P)
        wo_v = w_mix_out[0].rearrange("(k p) n -> p k n", p=P)
        mq_v = w_mq[0].rearrange("(k p) n -> p k n", p=P)
        mkv_v = w_mkv[0].rearrange("(k p) n -> p k n", p=P)
        mo_v = w_mo[0].rearrange("(k p) n -> p k n", p=P)
        fi_v = w_ffn_in[0].rearrange("(k p) n -> p k n", p=P)
        fo_v = w_ffn_out[0].rearrange("(k p) n -> p k n", p=P)
        x_v = x[0].rearrange("(c p) n -> p c n", p=P)
        out_v = out[0].rearrange("(c p) n -> p c n", p=P)

        @block.sync
        def _(sp):
            def panel(ph, i, u, parts):
                s = ph.slot(u)
                wait(sp, split_done, ph.quarter(i, u) - ph.nq)
                for k0, k1, src in parts:
                    sp.dma_start(raw[:, s, k0:k1, 0:src.shape[2]], src).then_inc(raw_landed[s], 16)

            def columns(ph, view, col, width=P, step=2 * P, apart=P, n=None, peel=False):
                def body(i):
                    for u in range(min(2, ph.n)):
                        panel(ph, i, u, [(0, 16, view[:, :, ds(i * step + u * apart + col, width)])])
                runs(sp, n or ph.n // 2, body, peel)

            for c in range(0, TC, 2):
                sp.dma_start(x_rows[:, c], x_v[:, c]).then_inc(x_landed[c], 16)
            columns(PH["merge"], w_in_v, C_MERGE, peel=True)
            columns(PH["sv"], w_in_v, C_V)
            columns(PH["su"], w_in_v, C_U)
            columns(PH["q"], w_in_v, C_Q)
            columns(PH["c"], w_in_v, C_KV)
            columns(PH["k"], w_in_v, C_KV + 2 * 256, step=2 * 256)
            columns(PH["v"], w_in_v, C_KV + 3 * 256, step=2 * 256)
            panel(PH["g"], 0, 0, [(0, 16, w_in_v[:, :, C_NSA_GATE:C_NSA_GATE + 48])])
            sp.wait_ge(quarters_done, PH["g"].end())
            for s, w in enumerate((cmp_k_w1, cmp_v_w1)):
                sp.dma_start(w1[s][:], w[0].rearrange("(k p) n -> p k n", p=P)).then_inc(w1_landed, 16)

            ph = PH["ab"]
            def ab(i):
                for u in range(2):
                    n = i * 2 + u
                    panel(ph, i, u, [(0, 8, wa_v[:, :, ds(n * P, P)]), (8, 16, wb_v[:, :, ds(n * P, P)])])
                    if isinstance(i, int) and i == 0 and u == 0:
                        sp.wait_ge(o_summed, 32)
                        sp.wait_ge(pv_done, 192)
                        sp.wait_ge(staged_qk, 24)
                        sp.wait_ge(staged_v, 20)
                        for b in range(2):
                            sp.wait_ge(gate_stored[b], 16 * DK)
                        sp.dma_start(mem_rows[:], mem[0].rearrange("(c p) n -> p c n", p=P)).then_inc(mem_landed, 16)
                    wait(sp, merge_done, n - 1)
                    for b in range(2):
                        sp.dma_start(gate_in[:, u, b], merge_dram[ds(n * P + b * DK * P, P), :]).then_inc(gates_landed[u], 16)
            runs(sp, ph.n // 2, ab, peel=True)

            ph = PH["wo"]
            def wo(i):
                for u in range(2):
                    n = i * 2 + u
                    panel(ph, i, u, [(0, 16, wo_v[:, :, ds(n * P, P)])])
                    wait(sp, quarters_done, ph.quarter(i, u) - ph.nq)
                    sp.dma_start(x_cols[:, u], x_v[:, :, ds(n * P, P)]).then_inc(xcol_landed[u], 16)
            runs(sp, ph.n // 2, wo, peel=True)
            columns(PH["mk"], mkv_v, 0)
            columns(PH["mv"], mkv_v, 512)
            columns(PH["mq"], mq_v, 0)
            ph = PH["mo"]
            def mo(i):
                for u in range(2):
                    panel(ph, i, u, [(4 * j, 4 * j + 4, mo_v[:, :, ds((i * 2 + u) * 512 + j * P, P)]) for j in range(4)])
            runs(sp, ph.n // 2, mo)
            t0 = 0
            for c, nk in enumerate(FFN_CHUNKS):
                columns(PH[f"f{c}"], fi_v, t0 * P, step=P, apart=FF)
                ph = PH[f"o{c}"]
                def fo(i, ph=ph, t0=t0, nk=nk):
                    for u in range(2):
                        panel(ph, i, u, [(0, nk, fo_v[:, t0:t0 + nk, ds((i * 2 + u) * P, P)])])
                runs(sp, ph.n // 2, fo)
                t0 += nk
            for c in range(TC):
                sp.wait_ge(y_copied, DK)
                sp.dma_start(out_v[:, c], y_rows[:, c]).then_inc(stored, 16)
            sp.wait_ge(stored, 16 * TC)

        @block.tensor
        def _(pe):
            def quarter(ph, i, u, q, dst, hi, lo, first, last, k0, m=P):
                pe.wait_ge(split_done, ph.quarter(i, u) + q + 1)
                for j in range(4):
                    k = k0 + j
                    pe.matmul(dst, w_hi[:, q, j, 0:m], hi(k), start=first and j == 0, stop=False)
                    pe.matmul(dst, w_hi[:, q, j, 0:m], lo(k), start=False, stop=False)
                    mm = pe.matmul(dst, w_lo[:, q, j, 0:m], hi(k), start=False, stop=last and j == 3)
                mm.then_inc(quarters_done, 1)

            def acts(k):
                return act_hi[:, k], act_lo[:, k]

            def group(ph, i, u, hi, lo, n=T, m=P, extra=None, ready=None):
                g = ph.group(i, u)
                b = (ph.group0 + u) % 2
                wait(pe, banks_read, g - 1)
                dst = bank[b][0:m, 0:n]
                for q in range(ph.nq):
                    if extra and q == ph.nq - 1:
                        extra(dst)
                    if ready:
                        pe.wait_ge(ready[0], ready[1] + 4 * q + 4)
                    quarter(ph, i, u, q, dst, hi, lo, q == 0, q == ph.nq - 1, 4 * q, m)

            hi16, lo16 = (lambda k: act_hi[:, k]), (lambda k: act_lo[:, k])

            pe.wait_ge(small_landed, 16 * 9)
            pe.wait_ge(ident_made, 2)
            pe.transpose(bank[0][:, 0:116], small_rows[:], ident[0:116, 0:116]).then_inc(cols_turned, 1)
            for k in range(DK):
                if k == 0:
                    pe.wait_ge(x_scaled, TC)
                wait(pe, turned_lo, k - 3)
                for c in range(TC):
                    mm = pe.transpose(bank[4 + k % 4][:, c * P:(c + 1) * P], x_rows[:, c, k * P:(k + 1) * P], ident[:])
                mm.then_inc(turned, 1)
            pe.wait_ge(ws_masked, 1)
            for g in range(SG):
                if g == 0:
                    pe.wait_ge(turned_lo, DK)
                mm = pe.transpose(bank[4 + g // 4][:, (g % 4) * P:(g % 4 + 1) * P], ws_rows[:, g], ident[:])
            mm.then_inc(ws_turned, 1)
            pe.wait_ge(cols_ready, 1)
            pe.wait_ge(turned_hi, DK)

            ph = PH["merge"]
            def merge_gates(i):
                for u in range(2):
                    group(ph, i, u, hi16, lo16)
            runs(pe, ph.n // 2, merge_gates, peel=True)

            ph = PH["sv"]
            def turn_v(n, u):
                pe.wait_ge(banks_read, ph.group0 + n + 1)
                wait(pe, v_rows_done, n - 1)
                for c in range(TC):
                    mm = pe.transpose(bank[2 + u][:, c * P:(c + 1) * P], vt[:, u, c * P:(c + 1) * P], ident[:])
                mm.then_inc(v_turned, 1)
            def sgu_v(i):
                for u in range(2):
                    group(ph, i, u, hi16, lo16)
                    if not (isinstance(i, int) and i == 0 and u == 0):
                        turn_v(i * 2 + u - 1, 1 - u)
            runs(pe, ph.n // 2, sgu_v, peel=True)
            turn_v(ph.n - 1, 1)

            ph = PH["su"]
            pe.wait_ge(ws_ready, 2)
            def mix(n, u):
                pe.wait_ge(vn_done, n + 1)
                wait(pe, mix_copied, n - 1)
                if isinstance(n, int) and n < 2:
                    pe.wait_ge(v_rows_done, SG)
                for c in range(TC):
                    mm = pe.matmul(bank[2 + u][:, c * P:(c + 1) * P], vn[:, u, c], ws_t[:, ds(n, 1), :],
                                   start=True, stop=True)
                mm.then_inc(mix_done, 1)
            def sgu_u(i):
                for u in range(2):
                    group(ph, i, u, hi16, lo16)
                    if not (isinstance(i, int) and i == 0 and u == 0):
                        mix(i * 2 + u - 1, 1 - u)
            runs(pe, ph.n // 2, sgu_u, peel=True)
            mix(ph.n - 1, 1)

            for name in ("q", "c", "k"):
                ph = PH[name]
                def plain(i):
                    for u in range(2):
                        group(ph, i, u, hi16, lo16)
                runs(pe, ph.n // 2, plain)
            ph = PH["v"]
            pe.wait_ge(mix_copied, SG)
            def kv_values(i):
                for u in range(2):
                    n = i * 2 + u
                    group(ph, i, u, hi16, lo16)
                    pe.wait_ge(banks_read, ph.group(i, u) + 1)
                    wait(pe, kv_rows_done, n - 1)
                    for c in range(TC):
                        mm = pe.transpose(bank[2 + u][:, c * P:(c + 1) * P], vt[:, u, c * P:(c + 1) * P], ident[:])
                    mm.then_inc(kv_turned, 1)
            runs(pe, ph.n // 2, kv_values, peel=True)
            ph = PH["g"]
            group(ph, 0, 0, hi16, lo16, m=48)
            pe.wait_ge(banks_read, ph.groups_end())
            pe.wait_ge(kv_rows_done, 4)
            for c in range(TC):
                mm = pe.transpose(bank[2][:, c * 48:(c + 1) * 48], gate_t[:, c * P:(c + 1) * P], ident[0:48, 0:48])
            mm.then_inc(kv_turned, 1)

            pe.wait_ge(w1_landed, 32)
            for s in range(2):
                pe.wait_ge(blocks_done, s + 1)
                for hh in range(2):
                    for k in range(16):
                        mm = pe.matmul(bank[4 + 2 * s + hh][:, 0:GROUPS * NCMP], w1[s][:, k, hh * P:(hh + 1) * P],
                                       blocks[s][:, k].rearrange("p g n -> p (g n)"), start=k == 0, stop=k == 15)
                    mm.then_inc(hid_done, 1)
            pe.wait_ge(hid_act, 2)
            pe.wait_ge(gates_done, 1)
            for hh in range(2):
                mm = pe.matmul(bank[2][0:HD, 0:GROUPS * NCMP], w2[:, 0, hh], hid_t[0][:, hh], start=hh == 0, stop=hh == 1)
            mm.then_inc(cmp_out, 1)
            pe.wait_ge(hid_act, 4)
            for g in range(GROUPS):
                for hh in range(2):
                    mm = pe.matmul(bank[3][0:NCMP, g * HD:(g + 1) * HD], hid_t[1][:, hh, g * NCMP:(g + 1) * NCMP],
                                   w2[:, 1, hh], start=hh == 0, stop=hh == 1)
            mm.then_inc(cmp_out, 1)

            pe.wait_ge(cmp_ready, 2)
            def attention(j):
                n0 = j * ITEMS
                for step in range(ITEMS + 6):
                    if step < ITEMS:
                        f, pr, qi, e, b = items[step]
                        if step % 48 == 0:
                            pe.wait_ge(staged_qk, j * 12 + f * 6 + 6)
                            pe.wait_ge(staged_v, j * 10 + f * 5 + 5)
                        if step >= 3:
                            pe.wait_ge(exp_done, n0 + step - 2)
                        s = bank[step % 3]
                        q = qs[:, f, 2 * pr + e, qi * P:(qi + 1) * P]
                        if b == 0:
                            pe.matmul(s[:, 0:NCMP], q, kcg[:, f], start=True, stop=False)
                            pe.matmul(s[:, 0:NCMP], ident_b[:], cmp_mask_b[:, qi], start=False, stop=True).then_inc(qk_done, 1)
                        else:
                            pe.matmul(s[:, 0:(qi + 1) * P], q, kg[:, f, b - 1, 0:(qi + 1) * P], start=True, stop=False)
                            pe.matmul(s[:, qi * P:(qi + 1) * P], ident_b[:], causal_b[:], start=False, stop=True).then_inc(qk_done, 1)
                    if 0 <= step - 2 < ITEMS:
                        t = step - 2
                        f, pr, qi, e, b = items[t]
                        pe.wait_ge(exp_done, n0 + t + 1)
                        if t >= 2:
                            pe.wait_ge(pt_copied, n0 + t - 1)
                        tb = bank[3 + t % 2]
                        if b == 0:
                            mm = pe.transpose(tb[0:NCMP, 0:P], prob[:, t % 3, 0:NCMP], ident[:])
                        else:
                            for kj in range(qi + 1):
                                mm = pe.transpose(tb[:, kj * P:(kj + 1) * P], prob[:, t % 3, kj * P:(kj + 1) * P], ident[:])
                        mm.then_inc(pt_done, 1)
                    if 0 <= step - 3 < ITEMS:
                        t = step - 3
                        f, pr, qi, e, b = items[t]
                        unit = t // 6
                        pe.wait_ge(pt_copied, n0 + t + 1)
                        if t % 6 == 0 and unit >= 2:
                            pe.wait_ge(o_summed, j * 16 + unit - 1)
                        o = bank[5 + unit % 2][:, (e * 3 + b) * HD:(e * 3 + b + 1) * HD]
                        if b == 0:
                            mm = pe.matmul(o, prob_t[0:NCMP, t % 3, 0], vcg[:, f], start=True, stop=True)
                        else:
                            for kj in range(qi + 1):
                                mm = pe.matmul(o, prob_t[:, t % 3, kj], vg[:, f, b - 1, kj], start=kj == 0, stop=kj == qi)
                        mm.then_inc(pv_done, 1)
                    if step >= 11 and (step - 11) % 6 == 0:
                            unit = (step - 11) // 6
                            qi = unit % TC
                            pe.wait_ge(o_summed, j * 16 + unit + 1)
                            if qi == 0 and unit >= TC:
                                pe.wait_ge(oa_lo_done, j * 4 + unit // TC)
                            pe.transpose(bank[7][:, qi * P:(qi + 1) * P], o_rows[:, unit % 2], ident[:]).then_inc(o_turned, 1)
            runs(pe, 2, attention, peel=False)

            pe.wait_ge(exp_done, 192)
            pe.wait_ge(oa_lo_done, 8)
            pe.wait_ge(oa_hi_done, 8)
            pe.wait_ge(ob_lo_done, SG)
            ph = PH["ab"]
            def ab(i):
                for u in range(2):
                    for a, (h, l) in enumerate(((oa_hi, oa_lo), (ob_hi, ob_lo))):
                        wait(pe, banks_read, ph.group(i, u) + a - 1)
                        dst = bank[(ph.group0 + a) % 2][:]
                        for q in range(2):
                            quarter(ph, i, u, 2 * a + q, dst, lambda k: h[:, k], lambda k: l[:, k], q == 0, q == 1, 4 * q)
            runs(pe, ph.n // 2, ab)

            for k2 in range(DK // 2):
                if k2 == 0:
                    pe.wait_ge(mem_scaled, MC)
                wait(pe, mem_lo, k2 - 1)
                wait(pe, mem_hi, k2 - 1)
                for kk in range(2):
                    for c in range(MC):
                        k = 2 * k2 + kk
                        mm = pe.transpose(bank[2 + k2 % 2][:, (kk * MC + c) * P:(kk * MC + c + 1) * P],
                                          mem_rows[:, c, k * P:(k + 1) * P], ident[:])
                mm.then_inc(mem_turned, 1)

            ph = PH["wo"]
            pe.wait_ge(merge_hi_done, DK)
            pe.wait_ge(merge_lo_done, DK)
            def wo(i):
                for u in range(2):
                    def residual(dst):
                        pe.wait_ge(xcol_landed[u], i * 16 + 16)
                        for c in range(TC):
                            pe.matmul(dst[:, c * P:(c + 1) * P], x_cols[:, u, c], ident[:], start=False, stop=False)
                    group(ph, i, u, hi16, lo16, extra=residual)
            runs(pe, ph.n // 2, wo)

            def norm_total(src, tiles, n):
                pe.wait_ge(summed, tiles)
                pe.matmul(bank[4][:], ones[:], src[:], start=True, stop=True).then_inc(norm_sum, 1)

            norm_total(sumsq, DK, 0)
            pe.wait_ge(mem_hi, DK // 2)
            pe.wait_ge(mem_lo, DK // 2)
            hm_h, hm_l = (lambda k: hm_hi[:, k]), (lambda k: hm_lo[:, k])
            ph = PH["mk"]
            def mem_keys(i):
                for u in range(2):
                    group(ph, i, u, hm_h, hm_l, n=MEM)
            runs(pe, ph.n // 2, mem_keys)
            ph = PH["mv"]
            def mem_values(i):
                for u in range(2):
                    group(ph, i, u, hm_h, hm_l, n=MEM)
                    pe.wait_ge(banks_read, ph.group(i, u) + 1)
                    wait(pe, mv_ready, i * 2 + u - 1)
                    for c in range(MC):
                        mm = pe.transpose(bank[2 + u][:, c * P:(c + 1) * P], mv_t[:, u, c * P:(c + 1) * P], ident[:])
                    mm.then_inc(mvt_turned, 1)
            runs(pe, ph.n // 2, mem_values, peel=True)
            ph = PH["mq"]
            pe.wait_ge(xg_hi, DK)
            pe.wait_ge(xg_lo, DK)
            def mem_queries(i):
                for u in range(2):
                    group(ph, i, u, hi16, lo16)
            runs(pe, ph.n // 2, mem_queries)

            pe.wait_ge(banks_read, ph.groups_end())
            pe.wait_ge(mv_ready, 4)
            N = MH * TC
            for step in range(N + 3):
                if step < N:
                    h, qi = divmod(step, TC)
                    wait(pe, m_exp, step - 2)
                    pe.matmul(bank[step % 3][:, 0:MEM], mq_t[:, h, qi * P:(qi + 1) * P], mk_t[:, h], start=True, stop=True).then_inc(m_qk, 1)
                if 0 <= step - 2 < N:
                    t = step - 2
                    pe.wait_ge(m_norm, t + 1)
                    wait(pe, m_ptc, t - 1)
                    for c in range(MC):
                        mm = pe.transpose(bank[3 + t % 2][:, c * P:(c + 1) * P], m_prob_n[:, t % 3, c * P:(c + 1) * P], ident[:])
                    mm.then_inc(m_pt, 1)
                if 0 <= step - 3 < N:
                    t = step - 3
                    h, qi = divmod(t, TC)
                    pe.wait_ge(m_ptc, t + 1)
                    if qi == 0:
                        wait(pe, mo_lo_done, h - 1)
                    for c in range(MC):
                        mm = pe.matmul(bank[5 + h % 2][:, qi * P:(qi + 1) * P], mv_rows[:, c, h * P:(h + 1) * P],
                                       m_prob_t[:, t % 3, c], start=c == 0, stop=c == MC - 1)
                    mm.then_inc(m_pv, 1)
            pe.wait_ge(mo_lo_done, MH)
            pe.wait_ge(mo_hi_done, MH)
            ph = PH["mo"]
            def mo(i):
                for u in range(2):
                    for j in range(4):
                        wait(pe, banks_read, ph.group(i, u) + j - 1)
                        quarter(ph, i, u, j, bank[(ph.group0 + j) % 2][:], lambda k: mo_hi[:, k], lambda k: mo_lo[:, k], True, True, 0)
            runs(pe, ph.n // 2, mo)
            norm_total(sumsq, 2 * DK, 1)

            tiles = 0
            for c, nk in enumerate(FFN_CHUNKS):
                ph = PH[f"f{c}"]
                def fi(i):
                    for u in range(2):
                        group(ph, i, u, hi16, lo16, ready=(xg_lo, DK) if c == 0 and u == 0 and isinstance(i, int) else None)
                runs(pe, ph.n // 2, fi, peel=c == 0)
                tiles += nk
                pe.wait_ge(ff_hi_done, tiles)
                pe.wait_ge(ff_lo_done, tiles)
                ph = PH[f"o{c}"]
                def fo(i):
                    for u in range(2):
                        group(ph, i, u, lambda k: ff_hi[:, k], lambda k: ff_lo[:, k])
                runs(pe, ph.n // 2, fo)
            norm_total(sumsq_f, 3 * DK, 2)
            for k in range(DK):
                pe.wait_ge(y_done, k + 1)
                wait(pe, y_copied, k - 3)
                for c in range(TC):
                    mm = pe.transpose(bank[(5, 6, 7, 3)[k % 4]][:, c * P:(c + 1) * P], y_t[:, k, c * P:(c + 1) * P], ident[:])
                mm.then_inc(y_turned, 1)

        @block.vector
        def _(dve):
            def split(ph, i, u, width=P):
                s = ph.slot(u)
                dve.wait_ge(raw_landed[s], ph.landed(i, u))
                for q in range(ph.nq):
                    n = ph.quarter(i, u) + q
                    wait(dve, quarters_done, n - ph.nq + 1)
                    src = raw[:, s, 4 * q:4 * q + 4, 0:width]
                    dve.tensor_copy(w_hi[:, q, :, 0:width], src).then_inc(hi_done, 1)
                    dve.wait_ge(hi_done, n + 1)
                    dve.tensor_tensor(w_lo[:, q, :, 0:width], src, w_hi[:, q, :, 0:width].bitcast(F32), ALU.subtract).then_inc(split_done, 1)

            def split_all(ph, start=0, peel=False):
                def body(i):
                    for u in range(2):
                        split(ph, i, u)
                if start == 0:
                    runs(dve, ph.n // 2, body, peel)
                else:
                    with dve.Fori(start, ph.n // 2) as i:
                        body(i)

            dve.memset(ones[:], 1.0).then_inc(ones_made, 1)
            dve.memset(eps[:], EPS).then_inc(ones_made, 1)
            for c in range(TC):
                dve.wait_ge(rms_done, c + 1)
                dve.reciprocal(rstd[:, c:c + 1], ss[:, c:c + 1]).then_inc(rstd_done, 1)
                dve.wait_ge(rstd_done, c + 1)
                dve.tensor_scalar(x_rows[:, c], x_rows[:, c], rstd[:, c:c + 1], None, ALU.mult).then_inc(x_scaled, 1)
            dve.wait_ge(cols_ready, 1)
            for k in range(DK):
                dve.wait_ge(turned_hi, k + 1)
                dve.scalar_tensor_tensor(out=act_lo[:, k], in0=bank[4 + k % 4][:], scalar=cols[:, G_MIX + k:G_MIX + k + 1],
                                         in1=act_hi[:, k].bitcast(F32), op0=ALU.mult, op1=ALU.subtract).then_inc(turned_lo, 1)
            split_all(PH["merge"], peel=True)
            split_all(PH["sv"])
            ph = PH["su"]
            split(ph, 0, 0)
            dve.wait_ge(v_rows_done, SG)
            for c in range(TC):
                for h in range(2):
                    dve.bn_stats(bn[:, c, h], v_rows[:, c, h * 512:(h + 1) * 512]).then_inc(ln_stats, 1)
            dve.wait_ge(ln_stats, 2 * TC)
            for c in range(TC):
                dve.bn_aggr(mv_stat[:, c], bn[:, c].rearrange("p a b -> p (a b)")).then_inc(ln_stats, 1)
            dve.wait_ge(ln_sqrt, 1)
            dve.reciprocal(ln_rstd[:], ln_shift[:]).then_inc(ln_ready, 1)
            dve.wait_ge(ln_ready, 1)
            dve.scalar_tensor_tensor(out=ln_shift[:], in0=mv_stat[:, :, 0], scalar=-1.0, in1=ln_rstd[:],
                                     op0=ALU.mult, op1=ALU.mult).then_inc(ln_ready, 1)
            split(ph, 0, 1)
            split_all(ph, start=1)
            for name in ("q", "c", "k", "v"):
                split_all(PH[name])
            split(PH["g"], 0, 0, width=48)

            def stage(j, f):
                for b in range(2):
                    dve.tensor_copy(vg[:, f, b], v_kv[:, b, :, ds(j * P + f * HD, HD)]).then_inc(staged_v, 1)
                dve.tensor_copy(kcg[:, f], kc_t[:, ds((j * 2 + f) * NCMP, NCMP)]).then_inc(staged_v, 1)
                dve.tensor_copy(vcg[:, f], vc[:, ds(j * 2 + f, 1), :]).then_inc(staged_v, 1)
                dve.tensor_copy(gg[:, f], gates[:, :, ds(j * 24 + f * 12, 12)]).then_inc(staged_v, 1)
                dve.wait_ge(staged_v, j * 10 + f * 5 + 5)
            def attention(j):
                n0 = j * ITEMS
                for step in range(ITEMS + 7):
                    if step in (0, 24):
                        stage(j, step // 24)
                    if step < ITEMS:
                        f, pr, qi, e, b = items[step]
                        n = NCMP if b == 0 else (qi + 1) * P
                        dve.wait_ge(qk_done, n0 + step + 1)
                        if step >= 4:
                            dve.wait_ge(exp_done, n0 + step - 3)
                        dve.tensor_reduce(neg_max[:, step % 4:step % 4 + 1], bank[step % 3][:, 0:n], AX.X, ALU.max, negate=True).then_inc(max_done, 1)
                    if 0 <= step - 2 < ITEMS:
                        t = step - 2
                        f, pr, qi, e, b = items[t]
                        dve.wait_ge(pt_done, n0 + t + 1)
                        if t >= 3:
                            dve.wait_ge(pv_done, n0 + t - 2)
                        if b == 0:
                            dve.tensor_copy(prob_t[0:NCMP, t % 3, 0], bank[3 + t % 2][0:NCMP, 0:P]).then_inc(pt_copied, 1)
                        else:
                            dve.tensor_copy(prob_t[:, t % 3, 0:qi + 1].rearrange("p k q -> p (k q)"),
                                            bank[3 + t % 2][:, 0:(qi + 1) * P]).then_inc(pt_copied, 1)
                    if step >= 9 and (step - 9) % 6 == 0:
                        unit = (step - 9) // 6
                        if unit < 16:
                            f, pr, qi = unit // 8, unit // TC % 2, unit % TC
                            un = j * 16 + unit
                            ub = unit % 2
                            dve.wait_ge(exp_done, n0 + 6 * unit + 6)
                            dve.reciprocal(coef[:, ub], den[:, ub]).then_inc(coef_step, 1)
                            dve.wait_ge(coef_step, un * 3 + 1)
                            dve.tensor_tensor(coef[:, ub], coef[:, ub], gg[:, f, qi, 6 * pr:6 * pr + 6], ALU.mult).then_inc(coef_step, 1)
                            dve.wait_ge(coef_step, un * 3 + 2)
                            dve.wait_ge(pv_done, n0 + 6 * unit + 6)
                            dve.tensor_tensor(o_parts[:, ub].rearrange("p e b d -> p (e b) d"),
                                              bank[5 + ub][:, 0:6 * HD].rearrange("p (s d) -> p s d", d=HD),
                                              coef[:, ub].unsqueeze(2).broadcast_to([P, 6, HD]), ALU.mult).then_inc(coef_step, 1)
                            dve.wait_ge(coef_step, un * 3 + 3)
                            if unit >= 2:
                                dve.wait_ge(o_turned, un - 1)
                            dve.tensor_reduce(o_rows[:, ub].rearrange("p (e d) -> p e d", e=2), o_parts[:, ub].rearrange("p e b d -> p e d b"),
                                              AX.X, ALU.add).then_inc(o_summed, 1)
                    if step >= 30 and (step - 30) % 24 == 0:
                        pair = (step - 30) // 24
                        pn = j * 4 + pair
                        dve.wait_ge(oa_hi_done, pn + 1)
                        dve.tensor_tensor(oa_lo[:, ds(pn, 1), :], bank[7][:], oa_hi[:, ds(pn, 1), :].bitcast(F32), ALU.subtract).then_inc(oa_lo_done, 1)
            dve.wait_ge(gates_masked, 1)
            dve.wait_ge(cmp_ready, 2)
            runs(dve, 2, attention)

            ph = PH["ab"]
            split(ph, 0, 0)
            dve.wait_ge(mem_rms, 1)
            dve.reciprocal(rstd[:, 0:MC], rstd[:, 0:MC]).then_inc(mem_rstd, 1)
            split(ph, 0, 1)
            split_all(ph, start=1)
            ph = PH["wo"]
            split(ph, 0, 0)
            for k2 in range(DK // 2):
                dve.wait_ge(mem_hi, k2 + 1)
                for kk in range(2):
                    k = 2 * k2 + kk
                    mm = dve.scalar_tensor_tensor(out=hm_lo[:, k], in0=bank[2 + k2 % 2][:, kk * MEM:(kk + 1) * MEM],
                                                  scalar=cols[:, G_MEM + k:G_MEM + k + 1], in1=hm_hi[:, k].bitcast(F32),
                                                  op0=ALU.mult, op1=ALU.subtract)
                mm.then_inc(mem_lo, 1)
            split(ph, 0, 1)
            split_all(ph, start=1)

            def inverse(n, buf):
                dve.wait_ge(norm_root, n + 1)
                dve.reciprocal(buf[:], buf[:]).then_inc(norm_inv, 1)
                dve.wait_ge(norm_inv, n + 1)

            def normed(k, done, gain):
                wait(dve, xg_hi, done + k - 1)
                wait(dve, xg_lo, done + k - 1)
                dve.scalar_tensor_tensor(out=xg[:, k % 2], in0=xt[:, k], scalar=cols[:, gain + k:gain + k + 1],
                                         in1=rms_bc[:], op0=ALU.mult, op1=ALU.mult).then_inc(xg_done, 1)

            split(PH["mk"], 0, 0)
            inverse(0, rms_bc)
            k = 0
            for n in range(1, 8):
                for _ in range(3 if n < 3 else 2):
                    normed(k, 0, G_CROSS)
                    k += 1
                split(PH["mk" if n < 4 else "mv"], n % 4 // 2, n % 2)
            assert k == DK
            split_all(PH["mq"])

            N = MH * TC
            for step in range(N + 5):
                if step < N:
                    dve.wait_ge(m_qk, step + 1)
                    wait(dve, m_exp, step - 3)
                    dve.tensor_reduce(neg_max[:, step % 4:step % 4 + 1], bank[step % 3][:, 0:MEM], AX.X, ALU.max, negate=True).then_inc(m_max, 1)
                if 0 <= step - 1 < N:
                    t = step - 1
                    dve.wait_ge(m_exp, t + 1)
                    dve.reciprocal(coef[:, 0, t % 3:t % 3 + 1], den[:, 0, t % 3:t % 3 + 1]).then_inc(m_inv, 1)
                    dve.wait_ge(m_inv, t + 1)
                    wait(dve, m_pt, t - 2)
                    dve.tensor_scalar(m_prob_n[:, t % 3], m_prob[:, t % 3], coef[:, 0, t % 3:t % 3 + 1], None, ALU.mult).then_inc(m_norm, 1)
                if 0 <= step - 2 < N:
                    t = step - 2
                    dve.wait_ge(m_pt, t + 1)
                    wait(dve, m_pv, t - 2)
                    dve.tensor_copy(m_prob_t[:, t % 3].rearrange("p c q -> p (c q)"), bank[3 + t % 2][:, 0:MEM]).then_inc(m_ptc, 1)
                if step >= 4 and (step - 4) % TC == TC - 1 or step == N + 4:
                    h = (step - 4) // TC if step < N + 4 else MH
                    if h < MH:
                        dve.wait_ge(mo_hi_done, h + 1)
                        dve.tensor_tensor(mo_lo[:, h], bank[5 + h % 2][:], mo_hi[:, h].bitcast(F32), ALU.subtract).then_inc(mo_lo_done, 1)
            split_all(PH["mo"])
            split(PH["f0"], 0, 0)
            inverse(1, rms_bc)
            for k in range(DK):
                normed(k, DK, G_FFN)
            split(PH["f0"], 0, 1)
            split_all(PH["f0"], start=1)
            for name in ("o0", "f1", "o1", "f2", "o2"):
                split_all(PH[name])
            inverse(2, rms_f)
            for k in range(DK):
                dve.scalar_tensor_tensor(out=y_t[:, k], in0=xt[:, k], scalar=cols[:, G_FINAL + k:G_FINAL + k + 1],
                                         in1=rms_f[:], op0=ALU.mult, op1=ALU.mult).then_inc(y_done, 1)

        @block.scalar
        def _(act):
            for c in range(1, TC, 2):
                act.dma_start(x_rows[:, c], x_v[:, c]).then_inc(x_landed[c], 16)
            row = 0
            for g in (norm_mix_g[0], norm_cross_g[0], norm_mem_g[0], norm_ffn_g[0], norm_final_g):
                act.dma_start(small_rows[row:row + 16], g.rearrange("(k p) -> k p", p=P)).then_inc(small_landed, 16)
                row += 16
            for g in (cmp_pe_k[0], cmp_pe_v[0]):
                act.dma_start(small_rows[row:row + 16], g.rearrange("(k a) d -> k (a d)", a=2)).then_inc(small_landed, 16)
                row += 16
            for g in (cmp_k_b1[0], cmp_v_b1[0]):
                act.dma_start(small_rows[row:row + 2], g.rearrange("(k p) -> k p", p=P)).then_inc(small_landed, 16)
                row += 2
            act.dma_start(ws_rows[:], sgu_ws[0].rearrange("g t s -> t g s")).then_inc(sgu_landed, 16)
            act.dma_start(sgu_b_bc[:].rearrange("p g t -> p (g t)"), sgu_b[0].rearrange("g t -> (g t)").partition_broadcast(P)).then_inc(sgu_landed, 16)
            act.dma_start(ln_g_bc[:], sgu_ln_g[0].partition_broadcast(P)).then_inc(sgu_landed, 16)
            act.dma_start(ln_b_bc[:], sgu_ln_b[0].partition_broadcast(P)).then_inc(sgu_landed, 16)
            for s, w in enumerate((cmp_k_w2, cmp_v_w2)):
                act.dma_start(w2[:, s], w[0].rearrange("(k p) n -> p k n", p=P)).then_inc(sgu_landed, 16)

            for c in range(TC):
                act.wait_ge(x_landed[c], 16)
                wait(act, sq_done, c)
                act.activation(junk[:], x_rows[:, c], ACT.Square,
                               accum_out=ss[:, c:c + 1]).then_inc(sq_done, 1)
            act.wait_ge(ones_made, 2)
            for c in range(TC):
                act.wait_ge(sq_done, c + 1)
                act.activation(ss[:, c:c + 1], ss[:, c:c + 1], ACT.Sqrt, scale=1.0 / D, bias=eps[:]).then_inc(rms_done, 1)
            act.wait_ge(cols_turned, 1)
            act.activation(cols[:], bank[0][:, 0:116], ACT.Copy).then_inc(cols_ready, 1)
            act.wait_ge(cols_ready, 1)
            for k in range(DK):
                act.wait_ge(turned, k + 1)
                act.activation(act_hi[:, k], bank[4 + k % 4][:], ACT.Copy, scale=cols[:, G_MIX + k:G_MIX + k + 1]).then_inc(turned_hi, 1)
            act.wait_ge(ws_turned, 1)
            for h in range(2):
                act.activation(ws_t[:, 4 * h:4 * h + 4].rearrange("p g t -> p (g t)"), bank[4 + h][:], ACT.Copy).then_inc(ws_ready, 1)

            def result(ph, i, u, g=0, upto=None):
                q = ph.nq if upto is None else upto
                act.wait_ge(quarters_done, ph.quarter(i, u) + q)
                return bank[(ph.group0 + ph.ng * u + g) % 2]

            ph = PH["merge"]
            def merge_gates(i):
                for u in range(2):
                    src = result(ph, i, u)
                    wait(act, gate_stored[u], i * 16)
                    act.activation(gate_out[:, u], src[:], ACT.Sigmoid).then_inc(banks_read, 1)
                    act.wait_ge(banks_read, ph.group(i, u) + 1)
                    act.dma_start(merge_dram[ds((i * 2 + u) * P, P), :], gate_out[:, u]).then_inc(gate_stored[u], 16)
            runs(act, ph.n // 2, merge_gates, peel=True)

            ph = PH["sv"]
            def v_out(n, u):
                act.wait_ge(v_turned, n + 1)
                act.activation(v_rows[:, :, ds(n * P, P)], bank[2 + u][:].rearrange("p (c f) -> p c f", c=TC), ACT.Copy).then_inc(v_rows_done, 1)
            def sgu_v(i):
                for u in range(2):
                    n = i * 2 + u
                    src = result(ph, i, u)
                    wait(act, v_turned, n - 1)
                    act.activation(vt[:, u], src[:], ACT.Gelu_apprx_tanh).then_inc(banks_read, 1)
                    if not (isinstance(i, int) and n == 0):
                        v_out(n - 1, 1 - u)
            runs(act, ph.n // 2, sgu_v, peel=True)
            v_out(ph.n - 1, 1)
            act.wait_ge(ln_stats, 3 * TC)
            act.activation(ln_shift[:], mv_stat[:, :, 1], ACT.Sqrt, bias=eps[:]).then_inc(ln_sqrt, 1)
            act.wait_ge(ln_ready, 2)

            ph = PH["su"]
            def mix_out(n, u):
                act.wait_ge(mix_done, n + 1)
                wait(act, ob_done, n - 1)
                act.activation(mixed[:, u].rearrange("p c t -> p (c t)"), bank[2 + u][:], ACT.Copy).then_inc(mix_copied, 1)
                act.wait_ge(ob_done, n + 1)
                act.activation(ob_hi[:, ds(n, 1), :], ob[:, u], ACT.Copy).then_inc(ob_hi_done, 1)
            def sgu_u(i):
                for u in range(2):
                    n = i * 2 + u
                    wait(act, vn_done, n - 1)
                    for c in range(TC):
                        a = act.activation(vz[:, u, c], v_rows[:, c, ds(n * P, P)], ACT.Identity,
                                           scale=ln_rstd[:, c:c + 1], bias=ln_shift[:, c:c + 1])
                    a.then_inc(vz_done, 1)
                    src = result(ph, i, u)
                    wait(act, ob_done, n - 1)
                    act.activation(ut[:, u], src[:], ACT.Gelu_apprx_tanh).then_inc(banks_read, 1)
                    if not (isinstance(i, int) and n == 0):
                        mix_out(n - 1, 1 - u)
            runs(act, ph.n // 2, sgu_u, peel=True)
            mix_out(ph.n - 1, 1)

            ph = PH["q"]
            def queries(i):
                for u in range(2):
                    act.activation(q_t[:, ds(i * 2 + u, 1), :], result(ph, i, u)[:], ACT.Copy, scale=HD ** -0.5).then_inc(banks_read, 1)
            runs(act, ph.n // 2, queries)
            ph = PH["c"]
            act.wait_ge(ob_lo_done, SG)
            def cmp_streams(i):
                for u in range(2):
                    src = result(ph, i, u)
                    for g in range(2):
                        act.activation(kv_src[0:HD, ds(i, 1), 2 * u + g, :], src[g * HD:(g + 1) * HD, :], ACT.Copy)
                        a = act.activation(kv_src[HD:P, ds(i, 1), 2 * u + g, 0:T - 1], src[g * HD:(g + 1) * HD, 1:T], ACT.Copy)
                    a.then_inc(banks_read, 1)
            runs(act, ph.n // 2, cmp_streams)
            ph = PH["k"]
            def keys(i):
                for u in range(2):
                    act.activation(k_t[:, ds(i, 1), u, :], result(ph, i, u)[:], ACT.Copy).then_inc(banks_read, 1)
            runs(act, ph.n // 2, keys)
            ph = PH["v"]
            for b in range(2):
                act.wait_ge(gate_stored[b], 16 * DK)
            def values(i):
                for u in range(2):
                    n = i * 2 + u
                    src = result(ph, i, u)
                    wait(act, kv_turned, n - 1)
                    act.activation(vt[:, u], src[:], ACT.Copy).then_inc(banks_read, 1)
                    act.wait_ge(kv_turned, n + 1)
                    act.activation(v_kv[:, ds(i, 1), :, u * P:(u + 1) * P], bank[2 + u][:].rearrange("p (c f) -> p c f", c=TC), ACT.Copy).then_inc(kv_rows_done, 1)
            runs(act, ph.n // 2, values, peel=True)
            ph = PH["g"]
            act.activation(gate_t[:], result(ph, 0, 0)[0:48, :], ACT.Copy).then_inc(banks_read, 1)
            act.wait_ge(kv_turned, 5)
            act.activation(gates[:].rearrange("p c g -> p (c g)"), bank[2][:, 0:TC * 48], ACT.Sigmoid).then_inc(gates_done, 1)

            for s in range(2):
                for hh in range(2):
                    act.wait_ge(hid_done, 2 * s + hh + 1)
                    act.activation(hid_t[s][:, hh], bank[4 + 2 * s + hh][:, 0:GROUPS * NCMP], ACT.Gelu_apprx_tanh,
                                   bias=cols[:, B1_K + 2 * s + hh:B1_K + 2 * s + hh + 1]).then_inc(hid_act, 1)
            act.wait_ge(cmp_out, 1)
            act.activation(kc_t[:], bank[2][0:HD, 0:GROUPS * NCMP], ACT.Copy).then_inc(cmp_ready, 1)
            act.wait_ge(cmp_out, 2)
            act.activation(vc[:].rearrange("n g d -> n (g d)"), bank[3][0:NCMP, 0:GROUPS * HD], ACT.Copy).then_inc(cmp_ready, 1)

            def stage(j, f):
                for pr in range(2):
                    for e in range(2):
                        act.activation(qs[:, f, 2 * pr + e], q_t[e * HD:(e + 1) * HD, ds(j * 4 + 2 * f + pr, 1), :], ACT.Copy).then_inc(staged_qk, 1)
                for b in range(2):
                    act.activation(kg[:, f, b], k_t[f * HD:(f + 1) * HD, b, ds(j, 1), :], ACT.Copy).then_inc(staged_qk, 1)
            def attention(j):
                n0 = j * ITEMS
                for step in range(ITEMS + 6):
                    if step in (0, 24):
                        stage(j, step // 24)
                    if step < ITEMS:
                        f, pr, qi, e, b = items[step]
                        n = NCMP if b == 0 else (qi + 1) * P
                        unit = step // 6
                        act.wait_ge(max_done, n0 + step + 1)
                        if step >= 3:
                            act.wait_ge(pt_done, n0 + step - 2)
                        if step % 6 == 0 and unit >= 2:
                            act.wait_ge(o_summed, j * 16 + unit - 1)
                        act.activation(prob[:, step % 3, 0:n], bank[step % 3][:, 0:n], ACT.Exp,
                                       bias=neg_max[:, step % 4:step % 4 + 1],
                                       accum_out=den[:, unit % 2, e * 3 + b:e * 3 + b + 1]).then_inc(exp_done, 1)
                    if step >= 29 and (step - 29) % 24 == 0:
                        pair = (step - 29) // 24
                        pn = j * 4 + pair
                        act.wait_ge(o_turned, 4 * pn + 4)
                        act.activation(oa_hi[:, ds(pn, 1), :], bank[7][:], ACT.Copy).then_inc(oa_hi_done, 1)
            runs(act, 2, attention)

            act.wait_ge(mem_landed, 16)
            for c in range(MC):
                wait(act, mem_sq, c)
                act.activation(mem_junk[:], mem_rows[:, c], ACT.Square, accum_out=ss[:, c:c + 1]).then_inc(mem_sq, 1)
            act.wait_ge(mem_sq, MC)
            act.activation(rstd[:, 0:MC], ss[:, 0:MC], ACT.Sqrt, scale=1.0 / D, bias=eps[:]).then_inc(mem_rms, 1)

            ph = PH["ab"]
            def merge_hi(n, u):
                act.wait_ge(merge_done, n + 1)
                act.activation(act_hi[:, ds(n, 1), :], merged[:, u], ACT.Copy).then_inc(merge_hi_done, 1)
            def ab(i):
                for u in range(2):
                    n = i * 2 + u
                    src = result(ph, i, u, 0, 2)
                    wait(act, merge_done, n - 1)
                    act.activation(pa[:, u], src[:], ACT.Copy).then_inc(banks_read, 1)
                    if not (isinstance(i, int) and n == 0):
                        merge_hi(n - 1, 1 - u)
                    src = result(ph, i, u, 1, 4)
                    act.activation(pb[:, u], src[:], ACT.Copy).then_inc(banks_read, 1)
            runs(act, ph.n // 2, ab, peel=True)
            merge_hi(ph.n - 1, 1)

            for k2 in range(DK // 2):
                act.wait_ge(mem_turned, k2 + 1)
                for kk in range(2):
                    k = 2 * k2 + kk
                    a = act.activation(hm_hi[:, k], bank[2 + k2 % 2][:, kk * MEM:(kk + 1) * MEM], ACT.Copy,
                                       scale=cols[:, G_MEM + k:G_MEM + k + 1])
                a.then_inc(mem_hi, 1)

            ph = PH["wo"]
            def wo(i):
                for u in range(2):
                    n = i * 2 + u
                    src = result(ph, i, u)
                    wait(act, summed, n - 1)
                    act.activation(sq[:, u], src[:], ACT.Square).then_inc(squared, 1)
                    act.activation(xt[:, ds(n, 1), :], src[:], ACT.Copy).then_inc(banks_read, 1)
            runs(act, ph.n // 2, wo, peel=True)

            def root(n, buf):
                act.wait_ge(norm_sum, n + 1)
                act.activation(buf[:], bank[4][:], ACT.Sqrt, scale=1.0 / D, bias=eps[:]).then_inc(norm_root, 1)

            def split_hi(k, done):
                act.wait_ge(xg_done, done + k + 1)
                act.activation(act_hi[:, k], xg[:, k % 2], ACT.Copy).then_inc(xg_hi, 1)

            root(0, rms_bc)
            k = 0
            for n in range(8):
                if n > 0:
                    for _ in range(3 if n < 3 else 2):
                        split_hi(k, 0)
                        k += 1
                ph = PH["mk" if n < 4 else "mv"]
                i, u = n % 4 // 2, n % 2
                src = result(ph, i, u)
                if n < 4:
                    act.activation(mk_t[:, n], src[:, 0:MEM], ACT.Copy).then_inc(banks_read, 1)
                else:
                    wait(act, mvt_turned, n - 5)
                    act.activation(mv_t[:, u], src[:, 0:MEM], ACT.Copy).then_inc(banks_read, 1)
                    act.wait_ge(mvt_turned, n - 3)
                    act.activation(mv_rows[:, :, (n - 4) * P:(n - 3) * P], bank[2 + u][:, 0:MEM].rearrange("p (c f) -> p c f", c=MC), ACT.Copy).then_inc(mv_ready, 1)
            ph = PH["mq"]
            def mem_queries(i):
                for u in range(2):
                    act.activation(mq_t[:, ds(i * 2 + u, 1), :], result(ph, i, u)[:], ACT.Copy, scale=P ** -0.5).then_inc(banks_read, 1)
            runs(act, ph.n // 2, mem_queries)

            N = MH * TC
            for step in range(N + 4):
                if step < N:
                    act.wait_ge(m_max, step + 1)
                    wait(act, m_norm, step - 2)
                    act.activation(m_prob[:, step % 3], bank[step % 3][:, 0:MEM], ACT.Exp, bias=neg_max[:, step % 4:step % 4 + 1],
                                   accum_out=den[:, 0, step % 3:step % 3 + 1]).then_inc(m_exp, 1)
                if step >= 3 and (step - 3) % TC == TC - 1:
                    h = (step - 3) // TC
                    act.wait_ge(m_pv, TC * (h + 1))
                    act.activation(mo_hi[:, h], bank[5 + h % 2][:], ACT.Copy).then_inc(mo_hi_done, 1)

            def add_out(ph, i, u, g, n, tile, total):
                src = result(ph, i, u, g, g + 1 if ph.ng > 1 else None)
                wait(act, added, n - 1)
                act.activation(add_in[:, g % 2 if ph.ng > 1 else u], src[:], ACT.Copy).then_inc(banks_read, 1)

            def square(n, tile, b, buf, sq0):
                act.wait_ge(added, n + 1)
                wait(act, summed, sq0 - 1)
                act.activation(buf, xt[:, ds(tile, 1), :], ACT.Square).then_inc(squared, 1)

            ph = PH["mo"]
            def mo(i):
                for u in range(2):
                    for j in range(4):
                        n = (i * 2 + u) * 4 + j
                        add_out(ph, i, u, j, n, n, DK)
                        if not (isinstance(i, int) and n == 0):
                            square(n - 1, n - 1, 1 - j % 2, sq[:, 1 - j % 2], DK + n - 1)
            runs(act, ph.n // 2, mo, peel=True)
            square(DK - 1, DK - 1, 1, sq[:, 1], 2 * DK - 1)
            root(1, rms_bc)
            for k in range(DK):
                split_hi(k, DK)
            tiles = 0
            n_add = DK
            for c, nk in enumerate(FFN_CHUNKS):
                ph = PH[f"f{c}"]
                act.wait_ge(added, n_add)
                def fi(i):
                    src = result(ph, i, 0)
                    wait(act, ff_done, tiles + i)
                    act.activation(gated[:], src[:], ACT.Silu).then_inc(banks_read, 1)
                    src = result(ph, i, 1)
                    act.activation(up[:], src[:], ACT.Copy).then_inc(banks_read, 1)
                    act.wait_ge(ff_done, tiles + i + 1)
                    act.activation(ff_hi[:, ds(i, 1), :], ff[:], ACT.Copy).then_inc(ff_hi_done, 1)
                runs(act, nk, fi, peel=c == 0)
                tiles += nk
                ph = PH[f"o{c}"]
                last = c == len(FFN_CHUNKS) - 1
                def fo(i):
                    for u in range(2):
                        n = i * 2 + u
                        src = result(ph, i, u)
                        wait(act, added, n_add + n - 1)
                        act.activation(add_in[:, u], src[:], ACT.Copy).then_inc(banks_read, 1)
                        if last:
                            act.wait_ge(added, n_add + n + 1)
                            wait(act, summed, 2 * DK + n)
                            act.activation(ff[:], xt[:, ds(n, 1), :], ACT.Square).then_inc(squared, 1)
                runs(act, ph.n // 2, fo)
                n_add += DK
            root(2, rms_f)
            for k in range(DK):
                act.wait_ge(y_turned, k + 1)
                act.activation(y_rows[:, :, k * P:(k + 1) * P], bank[(5, 6, 7, 3)[k % 4]][:].rearrange("p (c f) -> p c f", c=TC), ACT.Copy).then_inc(y_copied, 1)

        @block.gpsimd
        def _(pool):
            pool.memset(ident[:], 0.0).then_inc(ident_zero, 1)
            pool.memset(ident_b[:], 0.0).then_inc(ident_zero, 1)
            pool.wait_ge(ident_zero, 2)
            for m in (ident, ident_b):
                pool.affine_select(out=m[:], in_=m[:], compare_op=ALU.not_equal, fill=1.0, base=0,
                                   pattern=[[-1, P]], channel_multiplier=1).then_inc(ident_made, 1)
            pool.memset(causal_b[:], 0.0).then_inc(masks_zero, 1)
            pool.memset(cmp_mask_b[:], 0.0).then_inc(masks_zero, 1)
            pool.memset(valid[:], 1.0).then_inc(masks_zero, 1)
            pool.wait_ge(masks_zero, 3)
            pool.affine_select(out=causal_b[:], in_=causal_b[:], compare_op=ALU.is_ge, fill=MASKED, base=0,
                               pattern=[[-1, P]], channel_multiplier=1).then_inc(masks_made, 1)
            pool.affine_select(out=cmp_mask_b[:], in_=cmp_mask_b[:], compare_op=ALU.is_ge, fill=MASKED, base=1 - CMP_LEN,
                               pattern=[[P, TC], [-CMP_STEP, NCMP]], channel_multiplier=1).then_inc(masks_made, 1)
            pool.affine_select(out=valid[:], in_=valid[:], compare_op=ALU.is_ge, fill=0.0, base=1 - CMP_LEN,
                               pattern=[[0, 1]], channel_multiplier=1).then_inc(masks_made, 1)
            pool.wait_ge(sgu_landed, 16 * 6)
            pool.affine_select(out=ws_rows[:], in_=ws_rows[:], compare_op=ALU.is_ge, fill=0.0, base=0,
                               pattern=[[0, SG], [-1, P]], channel_multiplier=1).then_inc(ws_masked, 1)

            ph = PH["su"]
            def gate_out_tile(n, u):
                pool.wait_ge(mix_copied, n + 1)
                mx = mixed[:, u]
                pool.tensor_tensor(mx, mx, sgu_b_bc[:, ds(n, 1), :].broadcast_to([P, TC, P]), ALU.add).then_inc(ob_step, 1)
                pool.wait_ge(ob_step, n + 1)
                pool.tensor_tensor(ob[:, u], mx.rearrange("p c t -> p (c t)"), ut[:, u], ALU.mult).then_inc(ob_done, 1)
                pool.wait_ge(ob_hi_done, n + 1)
                pool.tensor_tensor(ob_lo[:, ds(n, 1), :], ob[:, u], ob_hi[:, ds(n, 1), :].bitcast(F32), ALU.subtract).then_inc(ob_lo_done, 1)
            def sgu_u(i):
                for u in range(2):
                    n = i * 2 + u
                    pool.wait_ge(vz_done, n + 1)
                    wait(pool, mix_done, n - 1)
                    pool.tensor_tensor(vz[:, u], vz[:, u], ln_g_bc[:, ds(n * P, P)].unsqueeze(1).broadcast_to([P, TC, P]), ALU.mult).then_inc(vn_step, 1)
                    pool.wait_ge(vn_step, n + 1)
                    pool.tensor_tensor(vn[:, u], vz[:, u], ln_b_bc[:, ds(n * P, P)].unsqueeze(1).broadcast_to([P, TC, P]), ALU.add).then_inc(vn_done, 1)
                    if not (isinstance(i, int) and n == 0):
                        gate_out_tile(n - 1, 1 - u)
            runs(pool, ph.n // 2, sgu_u, peel=True)
            gate_out_tile(ph.n - 1, 1)

            pool.wait_ge(banks_read, PH["c"].groups_end())
            pool.wait_ge(quarters_done, PH["g"].end())
            for s in range(2):
                for g in range(GROUPS):
                    src = kv_src[:, s, g].rearrange("p (n k a) -> p a k n", k=8, a=2)[:, 0]
                    for h in range(2):
                        pe_col = (PE_K, PE_V)[s] + 8 * h
                        a = pool.tensor_tensor(blocks[s][:, 8 * h:8 * h + 8, g], src[:, :, h:h + NCMP],
                                               cols[:, pe_col:pe_col + 8].unsqueeze(2).broadcast_to([P, 8, NCMP]), ALU.add)
                a.then_inc(blocks_done, 1)
            pool.wait_ge(gates_done, 1)
            g0 = gates[:, 0].rearrange("p (h b) -> p b h", b=3)[:, 0]
            pool.tensor_scalar(g0, g0, valid[:], None, ALU.mult).then_inc(gates_masked, 1)

            pool.wait_ge(mem_rstd, 1)
            for c in range(MC):
                pool.tensor_scalar(mem_rows[:, c], mem_rows[:, c], rstd[:, c:c + 1], None, ALU.mult).then_inc(mem_scaled, 1)

            ph = PH["ab"]
            def ab(i):
                for u in range(2):
                    n = i * 2 + u
                    pool.wait_ge(gates_landed[u], i * 32 + 32)
                    pool.wait_ge(banks_read, ph.group(i, u) + 2)
                    pool.tensor_tensor(pa[:, u], pa[:, u], gate_in[:, u, 0], ALU.mult).then_inc(merge_step, 1)
                    pool.tensor_tensor(pb[:, u], pb[:, u], gate_in[:, u, 1], ALU.mult).then_inc(merge_step, 1)
                    pool.wait_ge(merge_step, n * 2 + 2)
                    pool.tensor_tensor(merged[:, u], pa[:, u], pb[:, u], ALU.add).then_inc(merge_done, 1)
                    pool.wait_ge(merge_hi_done, n + 1)
                    pool.tensor_tensor(act_lo[:, ds(n, 1), :], merged[:, u], act_hi[:, ds(n, 1), :].bitcast(F32), ALU.subtract).then_inc(merge_lo_done, 1)
            runs(pool, ph.n // 2, ab)

            def clear(buf, n):
                pool.memset(buf[:], 0.0).then_inc(sumsq_zero, 1)
                pool.wait_ge(sumsq_zero, n)

            def total(buf, sqr, n):
                pool.wait_ge(squared, n + 1)
                wait(pool, summed, n)
                pool.tensor_tensor(buf[:], buf[:], sqr, ALU.add).then_inc(summed, 1)

            def split_lo(k, done):
                pool.wait_ge(xg_hi, done + k + 1)
                pool.tensor_tensor(act_lo[:, k], xg[:, k % 2], act_hi[:, k].bitcast(F32), ALU.subtract).then_inc(xg_lo, 1)

            clear(sumsq, 1)
            def wo(i):
                for u in range(2):
                    total(sumsq, sq[:, u], i * 2 + u)
            runs(pool, DK // 2, wo, peel=True)
            for k in range(DK):
                split_lo(k, 0)

            pool.wait_ge(norm_sum, 1)
            clear(sumsq, 2)
            ph = PH["mo"]
            def mo(i):
                for u in range(2):
                    for j in range(4):
                        n = (i * 2 + u) * 4 + j
                        pool.wait_ge(banks_read, ph.group(i, u) + j + 1)
                        pool.tensor_tensor(xt[:, ds(n, 1), :], xt[:, ds(n, 1), :], add_in[:, j % 2], ALU.add).then_inc(added, 1)
                        if not (isinstance(i, int) and n == 0):
                            total(sumsq, sq[:, 1 - j % 2], n - 1 + DK)
            runs(pool, ph.n // 2, mo, peel=True)
            total(sumsq, sq[:, 1], 2 * DK - 1)
            for k in range(DK):
                split_lo(k, DK)

            clear(sumsq_f, 3)
            tiles = 0
            for c, nk in enumerate(FFN_CHUNKS):
                ph = PH[f"f{c}"]
                def fi(i):
                    pool.wait_ge(banks_read, ph.group(i, 1) + 1)
                    wait(pool, ff_lo_done, i + tiles)
                    pool.tensor_tensor(ff[:], gated[:], up[:], ALU.mult).then_inc(ff_done, 1)
                    pool.wait_ge(ff_hi_done, i + tiles + 1)
                    pool.tensor_tensor(ff_lo[:, ds(i, 1), :], ff[:], ff_hi[:, ds(i, 1), :].bitcast(F32), ALU.subtract).then_inc(ff_lo_done, 1)
                runs(pool, nk, fi, peel=c == 0)
                tiles += nk
                ph = PH[f"o{c}"]
                last = c == len(FFN_CHUNKS) - 1
                def fo(i):
                    for u in range(2):
                        n = i * 2 + u
                        pool.wait_ge(banks_read, ph.group(i, u) + 1)
                        pool.tensor_tensor(xt[:, ds(n, 1), :], xt[:, ds(n, 1), :], add_in[:, u], ALU.add).then_inc(added, 1)
                        if last:
                            total(sumsq_f, ff[:], n + 2 * DK)
                runs(pool, ph.n // 2, fo)


_INS = ["x", "mem", "norm_mix_g", "w_in", "cmp_pe_k", "cmp_k_w1", "cmp_k_b1", "cmp_k_w2", "cmp_pe_v", "cmp_v_w1",
        "cmp_v_b1", "cmp_v_w2", "sgu_ln_g", "sgu_ln_b", "sgu_ws", "sgu_b", "w_proj_a", "w_proj_b", "w_mix_out",
        "norm_cross_g", "norm_mem_g", "w_mq", "w_mkv", "w_mo", "norm_ffn_g", "w_ffn_in", "w_ffn_out", "norm_final_g"]
_OUTS = [((1, T, D), "float32")]


def kernel(**inputs):
    import numpy as _np
    import concourse.bacc as _bacc
    from concourse import mybir as _mybir
    from concourse.bass_utils import run_bass_kernel_spmd as _run

    nc = _bacc.Bacc("TRN2", target_bir_lowering=False, num_devices=1)
    arrays, args = {}, []
    for name in _INS:
        a = _np.ascontiguousarray(inputs[name])
        arrays[f"in_{name}_dram"] = a
        args.append(nc.dram_tensor(f"in_{name}_dram", a.shape, _mybir.dt.from_np(a.dtype), kind="ExternalInput").ap())
    for i, (shape, dtype) in enumerate(_OUTS):
        dt = _mybir.dt.from_np(_np.dtype(dtype))
        args.append(nc.dram_tensor(f"out_{i}_dram", shape, dt, kind="ExternalOutput").ap())
    build(nc, *args)
    r = _run(nc, [arrays], core_ids=[0])
    got = tuple(r.results[0][f"out_{i}_dram"] for i in range(len(_OUTS)))
    return got[0]
```

```python
import concourse.bass as bass
from concourse import mybir
from contextlib import ExitStack

F32 = mybir.dt.float32
F32R = mybir.dt.float32r
BF16 = mybir.dt.bfloat16
ACT = mybir.ActivationFunctionType
ALU = mybir.AluOpType
AX = mybir.AxisListType

P = 128
T = 512
TC = T // P
D = 2048
DK = D // P
MEM = 256
MC = MEM // P
HEADS, GROUPS, HD = 16, 4, 64
HPG = HEADS // GROUPS
CMP_LEN, CMP_STEP = 32, 16
NCMP = (T - CMP_LEN) // CMP_STEP + 1
CMP_HID = 256
SG = 8
MH = 4
FF = (8 * D + 3 * 256 - 1) // (3 * 256) * 256
FK = FF // P
FFN_CHUNKS = (16, 16, 12)
EPS = 1e-6
MASKED = -1e30
KIB = 1024

C_Q, C_KV = 0, 1024
C_NSA_GATE = C_KV + 6 * 256
C_U = C_NSA_GATE + 48
C_V = C_U + 1024
C_MERGE = C_V + 1024

assert sum(FFN_CHUNKS) == FK and T // 64 <= 16 and T <= 512


class Phase:

    def __init__(self, prev, panels, quarters=4, groups=1, dmas=1):
        self.n, self.nq, self.ng, self.nd = panels, quarters, groups, dmas
        if prev is None:
            self.panel0 = self.quarter0 = self.group0 = 0
            self.landed0 = (0, 0)
        else:
            self.panel0 = prev.panel0 + prev.n
            self.quarter0 = prev.quarter0 + prev.n * prev.nq
            self.group0 = prev.group0 + prev.n * prev.ng
            used = [sum(1 for k in range(prev.n) if (prev.panel0 + k) % 2 == s) for s in (0, 1)]
            self.landed0 = tuple(prev.landed0[s] + 16 * prev.nd * used[s] for s in (0, 1))
        self.first = prev is None

    def slot(self, u):
        return (self.panel0 + u) % 2

    def landed(self, i, u):
        return self.landed0[self.slot(u)] + 16 * self.nd * (i + u // 2 + 1)

    def quarter(self, i, u):
        return self.quarter0 + self.nq * (2 * i + u)

    def group(self, i, u):
        return self.group0 + self.ng * (2 * i + u)

    def at(self, p):
        return p // 2, p % 2

    def end(self):
        return self.quarter0 + self.n * self.nq

    def groups_end(self):
        return self.group0 + self.n * self.ng


def plan():
    ph, prev = {}, None
    for name, args in (
        ("c", (4,)), ("q", (8,)), ("k", (4,)), ("v", (4,)), ("g", (1,)), ("merge", (32,)),
        ("sv", (8,)), ("su", (8,)), ("ab", (16, 4, 2, 2)), ("wo", (16,)), ("mk", (4,)), ("mv", (4,)),
        ("mq", (4,)), ("mo", (4, 4, 4, 4)),
    ):
        prev = ph[name] = Phase(prev, *args)
    for c, nk in enumerate(FFN_CHUNKS):
        prev = ph[f"f{c}"] = Phase(prev, 2 * nk)
        prev = ph[f"o{c}"] = Phase(prev, DK, nk // 4)
    return ph


def build(nc, x, mem, norm_mix_g, w_in, cmp_pe_k, cmp_k_w1, cmp_k_b1, cmp_k_w2, cmp_pe_v, cmp_v_w1,
          cmp_v_b1, cmp_v_w2, sgu_ln_g, sgu_ln_b, sgu_ws, sgu_b, w_proj_a, w_proj_b, w_mix_out,
          norm_cross_g, norm_mem_g, w_mq, w_mkv, w_mo, norm_ffn_g, w_ffn_in, w_ffn_out,
          norm_final_g, out):
    PH = plan()
    ds = bass.ds
    with ExitStack() as ctx:
        def sem(name):
            return ctx.enter_context(nc.semaphore(name))

        base = (nc.sbuf_base + 63) // 64 * 64
        A = base + 32 * KIB
        B = A + 64 * KIB
        B2 = B + 32 * KIB
        C = B + 64 * KIB
        K = C + 40 * KIB

        def at(name, shape, dt, offset):
            return nc.alloc_sbuf_tensor_at(name, shape, dt, offset=offset)

        raw = at("raw", [P, 2, 16, P], F32, base)
        w_hi = at("w_hi", [P, 4, 4, P], F32R, base + 16 * KIB)
        w_lo = at("w_lo", [P, 4, 4, P], F32R, base + 24 * KIB)

        act_hi = at("act_hi", [P, DK, T], F32R, A)
        act_lo = at("act_lo", [P, DK, T], F32R, A + 32 * KIB)

        x_rows = at("x_rows", [P, TC, D], F32, B)
        junk = at("junk", [P, D], F32, B2)
        small_rows = at("small_rows", [116, P], F32, C)
        kv_src = at("kv_src", [P, 2, GROUPS, T], F32, B2)
        blocks = [at(f"blocks_{s}", [P, 16, GROUPS, NCMP], F32, B2 + (16 + 8 * s) * KIB) for s in range(2)]
        w1 = [at(f"w1_{s}", [P, 16, CMP_HID], F32, B + 16 * KIB * s) for s in range(2)]
        hid_t = [at(f"hid_t_{s}", [P, 2, GROUPS * NCMP], F32, C + (16 + s) * KIB) for s in range(2)]
        vt = at("vt", [P, 2, T], F32, B2)
        gate_t = at("gate_t", [48, T], F32, B2 + 4 * KIB)
        q_t = at("q_t", [P, 8, T], F32, C)
        v_kv = at("v_kv", [P, 2, TC, 256], F32, C + 16 * KIB)
        k_t = at("k_t", [HD, 2, GROUPS, T], F32, C + 24 * KIB)
        qs = at("qs", [HD, HPG, T], F32, B)
        prob = at("prob", [P, 3, T], F32, B + 8 * KIB)
        prob_t = at("prob_t", [P, 3, TC, P], F32, B + 14 * KIB)
        gate_out = at("gate_out", [P, 2, T], F32, B + 20 * KIB)
        o_parts = at("o_parts", [P, 2, 2, 3, HD], F32, B + 24 * KIB)
        o_rows = at("o_rows", [P, 2, P], F32, B + 27 * KIB)
        oa_hi = at("oa_hi", [P, 8, T], F32R, B2)
        oa_lo = at("oa_lo", [P, 8, T], F32R, B2 + 16 * KIB)
        ws_rows = at("ws_rows", [P, SG, P], F32, B)
        ob_hi = at("ob_hi", [P, SG, T], F32R, B)
        ob_lo = at("ob_lo", [P, SG, T], F32R, B + 16 * KIB)
        v_rows = at("v_rows", [P, TC, 1024], F32, C)
        sv_t = at("sv_t", [P, 2, T], F32, C + 16 * KIB)
        ut = at("ut", [P, 2, T], F32, C + 16 * KIB)
        vz = at("vz", [P, 2, TC, P], F32, C + 20 * KIB)
        vn = at("vn", [P, 2, TC, P], F32, C + 24 * KIB)
        mixed = at("mixed", [P, TC, P], F32, C + 28 * KIB)
        ob = at("ob", [P, T], F32, C + 30 * KIB)
        ws_t = at("ws_t", [P, SG, P], F32, C + 32 * KIB)
        rows_bc = at("rows_bc", [P, 2, 3, P], F32, C + 36 * KIB)
        gate_in = at("gate_in", [P, 2, 2, T], F32, C)
        pa = at("pa", [P, 2, T], F32, C + 8 * KIB)
        pb = at("pb", [P, 2, T], F32, C + 12 * KIB)
        merged = at("merged", [P, 2, T], F32, C + 16 * KIB)
        mem_rows = at("mem_rows", [P, MC, D], F32, C + 20 * KIB)
        x_cols = at("x_cols", [P, 2, TC, P], F32, C + 36 * KIB)
        mem_cols = at("mem_cols", [P, 2, MC, P], F32, C + 8 * KIB)
        xt = at("xt", [P, DK, T], F32, B)
        sq = at("sq", [P, 2, T], F32, C)
        sumsq = at("sumsq", [P, T], F32, C + 4 * KIB)
        rms_bc = at("rms_bc", [P, T], F32, C + 6 * KIB)
        xg = at("xg", [P, 2, T], F32, C + 8 * KIB)
        hm_hi = at("hm_hi", [P, DK, MEM], F32R, B2)
        hm_lo = at("hm_lo", [P, DK, MEM], F32R, B2 + 16 * KIB)
        mq_t = at("mq_t", [P, MH, T], F32, C + 12 * KIB)
        mk_t = at("mk_t", [P, MH, MEM], F32, C + 20 * KIB)
        mv_rows = at("mv_rows", [P, MC, 512], F32, C + 24 * KIB)
        mv_t = at("mv_t", [P, 2, MEM], F32, C + 28 * KIB)
        add_in = at("add_in", [P, 2, T], F32, C + 32 * KIB)
        mo_hi = at("mo_hi", [P, MH, T], F32R, B2)
        mo_lo = at("mo_lo", [P, MH, T], F32R, B2 + 8 * KIB)
        mem_junk = at("mem_junk", [P, D], F32, A + 48 * KIB)
        m_prob = at("m_prob", [P, 3, MEM], F32, B2 + 16 * KIB)
        m_prob_n = at("m_prob_n", [P, 3, MEM], F32, B2 + 20 * KIB)
        m_prob_t = at("m_prob_t", [P, 3, MC, P], F32, B2 + 24 * KIB)
        ff_hi = at("ff_hi", [P, 16, T], F32R, B2)
        ff_lo = at("ff_lo", [P, 16, T], F32R, C)
        gated = at("gated", [P, T], F32, C + 32 * KIB)
        up = at("up", [P, T], F32, C + 34 * KIB)
        ff = at("ff", [P, T], F32, C + 36 * KIB)
        sumsq_f = at("sumsq_f", [P, T], F32, C + 38 * KIB)
        y_rows = at("y_rows", [P, TC, D], F32, A)
        final_g_bc = at("final_g_bc", [P, D], F32, A + 32 * KIB)
        x_out = at("x_out", [P, 2, T], F32, A + 40 * KIB)

        spot = [K]

        def const(name, shape, dt=F32):
            size = mybir.dt.size(dt)
            for n in shape[1:]:
                size *= n
            t = at(name, shape, dt, spot[0])
            spot[0] += (size + 31) // 32 * 32
            return t

        ident = const("ident", [P, P])
        ones = const("ones", [P, P])
        ident_b = const("ident_b", [P, P], BF16)
        causal_b = const("causal_b", [P, P], BF16)
        cmp_mask_b = const("cmp_mask_b", [P, TC, NCMP], BF16)
        valid = const("valid", [P, 1])
        eps = const("eps", [P, 1])
        cols = const("cols", [P, 116])
        ss = const("ss", [P, TC])
        rstd = const("rstd", [P, TC])
        bn = const("bn", [P, TC, 2, 6])
        mv_stat = const("mv_stat", [P, TC, 2])
        ln_rstd = const("ln_rstd", [P, TC])
        ln_shift = const("ln_shift", [P, TC])
        gates = const("gates", [P, TC, 48])
        kc_t = const("kc_t", [HD, GROUPS * NCMP])
        vc = const("vc", [NCMP, GROUPS, HD])
        vcg = const("vcg", [NCMP, HD])
        w2 = const("w2", [P, 2, 2, HD])
        neg_max = const("neg_max", [P, 4])
        den = const("den", [P, 2, 6])
        coef = const("coef", [P, 2, 6])
        assert spot[0] <= nc.sbuf_usable_end, spot[0]
        G_MIX, G_CROSS, G_MEM, G_FFN, G_FINAL, PE_K, PE_V, B1_K, B1_V = 0, 16, 32, 48, 64, 80, 96, 112, 114

        bank = [ctx.enter_context(nc.psum_tensor(f"bank{b}", [P, T], F32)) for b in range(8)]
        merge_dram = nc.dram_tensor("merge_gates", [2 * DK * P, T], F32, kind="Internal").ap()

        raw_landed = [sem("raw_landed0"), sem("raw_landed1")]
        hi_done = sem("hi_done")
        split_done = sem("split_done")
        quarters_done = sem("quarters_done")
        banks_read = sem("banks_read")
        ones_made = sem("ones_made")
        ident_zero = sem("ident_zero")
        ident_made = sem("ident_made")
        masks_zero = sem("masks_zero")
        masks_made = sem("masks_made")
        x_landed = [sem(f"x_landed{c}") for c in range(TC)]
        small_landed = sem("small_landed")
        sgu_landed = sem("sgu_landed")
        sq_done = sem("sq_done")
        rms_done = sem("rms_done")
        rstd_done = sem("rstd_done")
        x_scaled = sem("x_scaled")
        turned = sem("turned")
        turned_hi = sem("turned_hi")
        turned_lo = sem("turned_lo")
        cols_turned = sem("cols_turned")
        cols_ready = sem("cols_ready")
        ws_masked = sem("ws_masked")
        ws_turned = sem("ws_turned")
        ws_ready = sem("ws_ready")
        gate_stored = [sem("gate_stored0"), sem("gate_stored1")]
        v_turned = sem("v_turned")
        v_rows_done = sem("v_rows_done")
        ln_stats = sem("ln_stats")
        ln_sqrt = sem("ln_sqrt")
        ln_ready = sem("ln_ready")
        vz_done = sem("vz_done")
        vn_step = sem("vn_step")
        vn_done = sem("vn_done")
        mix_done = sem("mix_done")
        mix_copied = sem("mix_copied")
        ob_step = sem("ob_step")
        ob_done = sem("ob_done")
        ob_hi_done = sem("ob_hi_done")
        ob_lo_done = sem("ob_lo_done")
        kv_turned = sem("kv_turned")
        kv_rows_done = sem("kv_rows_done")
        gates_done = sem("gates_done")
        gates_masked = sem("gates_masked")
        w1_landed = sem("w1_landed")
        blocks_done = sem("blocks_done")
        hid_done = sem("hid_done")
        hid_act = sem("hid_act")
        cmp_out = sem("cmp_out")
        cmp_ready = sem("cmp_ready")
        staged = sem("staged")
        rows_landed = [sem("rows_landed0"), sem("rows_landed1")]
        ws_landed = sem("ws_landed")
        mem_cols_done = sem("mem_cols_done")
        gates_open = sem("gates_open")
        final_g_landed = sem("final_g_landed")
        sumsq_zero = sem("sumsq_zero")
        qk_done = sem("qk_done")
        max_done = sem("max_done")
        exp_done = sem("exp_done")
        pt_done = sem("pt_done")
        pt_copied = sem("pt_copied")
        pv_done = sem("pv_done")
        coef_step = sem("coef_step")
        o_scaled = sem("o_scaled")
        o_summed = sem("o_summed")
        o_turned = sem("o_turned")
        oa_hi_done = sem("oa_hi_done")
        oa_lo_done = sem("oa_lo_done")
        gates_landed = [sem("gates_landed0"), sem("gates_landed1")]
        merge_step = sem("merge_step")
        merge_done = sem("merge_done")
        merge_hi_done = sem("merge_hi_done")
        merge_lo_done = sem("merge_lo_done")
        mem_landed = sem("mem_landed")
        mem_sq = sem("mem_sq")
        mem_rms = sem("mem_rms")
        mem_rstd = sem("mem_rstd")
        mem_scaled = sem("mem_scaled")
        mem_turned = sem("mem_turned")
        mem_hi = sem("mem_hi")
        mem_lo = sem("mem_lo")
        xcol_landed = [sem("xcol_landed0"), sem("xcol_landed1")]
        squared = sem("squared")
        summed = sem("summed")
        norm_sum = sem("norm_sum")
        norm_root = sem("norm_root")
        norm_inv = sem("norm_inv")
        xg_done = sem("xg_done")
        xg_hi = sem("xg_hi")
        xg_lo = sem("xg_lo")
        mvt_turned = sem("mvt_turned")
        mv_ready = sem("mv_ready")
        m_qk = sem("m_qk")
        m_max = sem("m_max")
        m_exp = sem("m_exp")
        m_inv = sem("m_inv")
        m_norm = sem("m_norm")
        m_pt = sem("m_pt")
        m_ptc = sem("m_ptc")
        m_pv = sem("m_pv")
        mo_hi_done = sem("mo_hi_done")
        mo_lo_done = sem("mo_lo_done")
        copied = sem("copied")
        added = sem("added")
        gated_done = sem("gated_done")
        ff_done = sem("ff_done")
        ff_hi_done = sem("ff_hi_done")
        ff_lo_done = sem("ff_lo_done")
        y_done = sem("y_done")
        y_turned = sem("y_turned")
        y_copied = sem("y_copied")
        stored = sem("stored")

        block = ctx.enter_context(nc.Block())

        def wait(eng, s, value):
            if not isinstance(value, int) or value > 0:
                eng.wait_ge(s, value)

        def runs(eng, n, body, peel=False):
            if peel:
                body(0)
            if n - peel > 0:
                with eng.Fori(1 if peel else 0, n) as i:
                    body(i)

        items = [(pr, qi, e, b) for pr in range(2) for qi in range(TC) for e in range(2) for b in (1, 2, 0)]
        ITEMS = len(items)
        UNITS = ITEMS // 6
        SUM_LAG, OT_LAG = 8, 9
        STEPS = ITEMS - 6 + OT_LAG + 2
        QUARTERS_AT = [[k for k in range(32) if k * STEPS // 32 == step] for step in range(STEPS)]
        AHEAD = 3
        M_ITEMS, M_LAG = MH * TC, 5
        M_STEPS = M_ITEMS + M_LAG + 3

        w_in_v = w_in[0].rearrange("(k p) n -> p k n", p=P)
        wa_v = w_proj_a[0].rearrange("(k p) n -> p k n", p=P)
        wb_v = w_proj_b[0].rearrange("(k p) n -> p k n", p=P)
        wo_v = w_mix_out[0].rearrange("(k p) n -> p k n", p=P)
        mq_v = w_mq[0].rearrange("(k p) n -> p k n", p=P)
        mkv_v = w_mkv[0].rearrange("(k p) n -> p k n", p=P)
        mo_v = w_mo[0].rearrange("(k p) n -> p k n", p=P)
        fi_v = w_ffn_in[0].rearrange("(k p) n -> p k n", p=P)
        fo_v = w_ffn_out[0].rearrange("(k p) n -> p k n", p=P)
        x_v = x[0].rearrange("(c p) n -> p c n", p=P)
        out_v = out[0].rearrange("(c p) n -> p c n", p=P)

        @block.sync
        def _(sp):
            def panel(ph, i, u, parts):
                s = ph.slot(u)
                wait(sp, split_done, ph.quarter(i, u) - ph.nq)
                for k0, k1, src in parts:
                    sp.dma_start(raw[:, s, k0:k1, 0:src.shape[2]], src).then_inc(raw_landed[s], 16)

            def columns(ph, view, col, width=P, step=2 * P, apart=P, n=None, peel=False):
                def body(i):
                    for u in range(min(2, ph.n)):
                        panel(ph, i, u, [(0, 16, view[:, :, ds(i * step + u * apart + col, width)])])
                runs(sp, n or ph.n // 2, body, peel)

            for c in range(0, TC, 2):
                sp.dma_start(x_rows[:, c], x_v[:, c]).then_inc(x_landed[c], 16)
            columns(PH["c"], w_in_v, C_KV, peel=True)
            sp.wait_ge(turned, DK)
            for s, w in enumerate((cmp_k_w1, cmp_v_w1)):
                sp.dma_start(w1[s][:], w[0].rearrange("(k p) n -> p k n", p=P)).then_inc(w1_landed, 16)
            columns(PH["q"], w_in_v, C_Q)
            columns(PH["k"], w_in_v, C_KV + 2 * 256, step=2 * 256)
            columns(PH["v"], w_in_v, C_KV + 3 * 256, step=2 * 256)
            panel(PH["g"], 0, 0, [(0, 16, w_in_v[:, :, C_NSA_GATE:C_NSA_GATE + 48])])
            columns(PH["merge"], w_in_v, C_MERGE)
            columns(PH["sv"], w_in_v, C_V)
            columns(PH["su"], w_in_v, C_U)

            ph = PH["ab"]
            def ab(i):
                for u in range(2):
                    n = i * 2 + u
                    panel(ph, i, u, [(0, 8, wa_v[:, :, ds(n * P, P)]), (8, 16, wb_v[:, :, ds(n * P, P)])])
                    if isinstance(i, int) and i == 0 and u == 0:
                        sp.wait_ge(ob_lo_done, SG)
                        for b in range(2):
                            sp.wait_ge(gate_stored[b], 16 * DK)
                        sp.dma_start(mem_rows[:], mem[0].rearrange("(c p) n -> p c n", p=P)).then_inc(mem_landed, 16)
                    wait(sp, merge_done, n - 1)
                    for b in range(2):
                        sp.dma_start(gate_in[:, u, b], merge_dram[ds(n * P + b * DK * P, P), :]).then_inc(gates_landed[u], 16)
            runs(sp, ph.n // 2, ab, peel=True)

            ph = PH["wo"]
            def wo(i):
                for u in range(2):
                    n = i * 2 + u
                    panel(ph, i, u, [(0, 16, wo_v[:, :, ds(n * P, P)])])
                    wait(sp, quarters_done, ph.quarter(i, u) - ph.nq)
                    sp.dma_start(x_cols[:, u], x_v[:, :, ds(n * P, P)]).then_inc(xcol_landed[u], 16)
            runs(sp, ph.n // 2, wo, peel=True)
            columns(PH["mk"], mkv_v, 0)
            columns(PH["mv"], mkv_v, 512)
            columns(PH["mq"], mq_v, 0)
            ph = PH["mo"]
            def mo(i):
                for u in range(2):
                    panel(ph, i, u, [(4 * j, 4 * j + 4, mo_v[:, :, ds((i * 2 + u) * 512 + j * P, P)]) for j in range(4)])
            runs(sp, ph.n // 2, mo)
            t0 = 0
            for c, nk in enumerate(FFN_CHUNKS):
                columns(PH[f"f{c}"], fi_v, t0 * P, step=P, apart=FF)
                ph = PH[f"o{c}"]
                def fo(i, ph=ph, t0=t0, nk=nk):
                    for u in range(2):
                        panel(ph, i, u, [(0, nk, fo_v[:, t0:t0 + nk, ds((i * 2 + u) * P, P)])])
                runs(sp, ph.n // 2, fo)
                t0 += nk
            for c in range(TC):
                sp.wait_ge(y_done, c + 1)
                sp.dma_start(out_v[:, c], y_rows[:, c]).then_inc(stored, 16)
            sp.wait_ge(stored, 16 * TC)

        @block.tensor
        def _(pe):
            def quarter(ph, i, u, q, dst, hi, lo, first, last, k0, m=P):
                pe.wait_ge(split_done, ph.quarter(i, u) + q + 1)
                for j in range(4):
                    k = k0 + j
                    pe.matmul(dst, w_hi[:, q, j, 0:m], hi(k), start=first and j == 0, stop=False)
                    pe.matmul(dst, w_hi[:, q, j, 0:m], lo(k), start=False, stop=False)
                    mm = pe.matmul(dst, w_lo[:, q, j, 0:m], hi(k), start=False, stop=last and j == 3)
                mm.then_inc(quarters_done, 1)

            def acts(k):
                return act_hi[:, k], act_lo[:, k]

            def group(ph, i, u, hi, lo, n=T, m=P, extra=None, ready=None):
                g = ph.group(i, u)
                b = (ph.group0 + u) % 2
                wait(pe, banks_read, g - 1)
                dst = bank[b][0:m, 0:n]
                for q in range(ph.nq):
                    if extra and q == ph.nq - 1:
                        extra(dst)
                    if ready:
                        pe.wait_ge(ready[0], ready[1] + 4 * q + 4)
                    quarter(ph, i, u, q, dst, hi, lo, q == 0, q == ph.nq - 1, 4 * q, m)

            hi16, lo16 = (lambda k: act_hi[:, k]), (lambda k: act_lo[:, k])

            pe.wait_ge(small_landed, 16 * 9)
            pe.wait_ge(ident_made, 2)
            pe.transpose(bank[0][:, 0:116], small_rows[:], ident[0:116, 0:116]).then_inc(cols_turned, 1)
            for k in range(DK):
                if k == 0:
                    pe.wait_ge(x_scaled, TC)
                wait(pe, turned_lo, k - 3)
                for c in range(TC):
                    mm = pe.transpose(bank[4 + k % 4][:, c * P:(c + 1) * P], x_rows[:, c, k * P:(k + 1) * P], ident[:])
                mm.then_inc(turned, 1)
            pe.wait_ge(cols_ready, 1)

            def plain(i):
                for u in range(2):
                    group(ph, i, u, hi16, lo16)
            ph = PH["c"]
            def first(i):
                for u in range(2):
                    group(ph, i, u, hi16, lo16, ready=(turned_lo, 0) if isinstance(i, int) and u == 0 else None)
            runs(pe, ph.n // 2, first, peel=True)
            ph = PH["q"]
            runs(pe, ph.n // 2, plain)

            pe.wait_ge(w1_landed, 32)
            for s in range(2):
                pe.wait_ge(blocks_done, s + 1)
                for hh in range(2):
                    for k in range(16):
                        mm = pe.matmul(bank[4 + 2 * s + hh][:, 0:GROUPS * NCMP], w1[s][:, k, hh * P:(hh + 1) * P],
                                       blocks[s][:, k].rearrange("p g n -> p (g n)"), start=k == 0, stop=k == 15)
                    mm.then_inc(hid_done, 1)
            ph = PH["k"]
            runs(pe, ph.n // 2, plain)
            pe.wait_ge(sgu_landed, 16 * 2)
            pe.wait_ge(hid_act, 2)
            for hh in range(2):
                mm = pe.matmul(bank[2][0:HD, 0:GROUPS * NCMP], w2[:, 0, hh], hid_t[0][:, hh], start=hh == 0, stop=hh == 1)
            mm.then_inc(cmp_out, 1)
            pe.wait_ge(hid_act, 4)
            for g in range(GROUPS):
                for hh in range(2):
                    mm = pe.matmul(bank[3][0:NCMP, g * HD:(g + 1) * HD], hid_t[1][:, hh, g * NCMP:(g + 1) * NCMP],
                                   w2[:, 1, hh], start=hh == 0, stop=hh == 1)
            mm.then_inc(cmp_out, 1)

            ph = PH["v"]
            pe.wait_ge(cmp_ready, 2)
            def kv_values(i):
                for u in range(2):
                    n = i * 2 + u
                    group(ph, i, u, hi16, lo16)
                    pe.wait_ge(banks_read, ph.group(i, u) + 1)
                    wait(pe, kv_rows_done, n - 1)
                    for c in range(TC):
                        mm = pe.transpose(bank[2 + u][:, c * P:(c + 1) * P], vt[:, u, c * P:(c + 1) * P], ident[:])
                    mm.then_inc(kv_turned, 1)
            runs(pe, ph.n // 2, kv_values, peel=True)
            ph = PH["g"]
            group(ph, 0, 0, hi16, lo16, m=48)
            pe.wait_ge(banks_read, ph.groups_end())
            pe.wait_ge(kv_rows_done, 4)
            for c in range(TC):
                mm = pe.transpose(bank[2][:, c * 48:(c + 1) * 48], gate_t[:, c * P:(c + 1) * P], ident[0:48, 0:48])
            mm.then_inc(kv_turned, 1)

            pe.wait_ge(gates_done, 1)
            ph = PH["merge"]
            def attention(j):
                n0 = j * ITEMS
                for step in range(STEPS):
                    for k in QUARTERS_AT[step]:
                        p, q = k // 4, k % 4
                        if q == 0:
                            pe.wait_ge(banks_read, j * 8 + ph.group0 + p - 1)
                        quarter(ph, j * 4, p, q, bank[(ph.group0 + p) % 2][:], hi16, lo16, q == 0, q == 3, 4 * q)
                    if step < ITEMS:
                        pr, qi, e, b = items[step]
                        if step == 0:
                            pe.wait_ge(staged, j * (HPG + 1) + HPG + 1)
                        if step >= 2:
                            pe.wait_ge(exp_done, n0 + step - 1)
                        s = bank[2 + step % 2]
                        q = qs[:, 2 * pr + e, qi * P:(qi + 1) * P]
                        if b == 0:
                            pe.matmul(s[:, 0:NCMP], ident_b[:], cmp_mask_b[:, qi], start=True, stop=False)
                            pe.matmul(s[:, 0:NCMP], q, kc_t[:, ds(j * NCMP, NCMP)], start=False, stop=True).then_inc(qk_done, 1)
                        else:
                            here = slice(qi * P, (qi + 1) * P)
                            pe.matmul(s[:, here], ident_b[:], causal_b[:], start=True, stop=False)
                            mm = pe.matmul(s[:, here], q, k_t[:, b - 1, ds(j, 1), here], start=False, stop=True)
                            if qi > 0:
                                mm = pe.matmul(s[:, 0:qi * P], q, k_t[:, b - 1, ds(j, 1), 0:qi * P], start=True, stop=True)
                            mm.then_inc(qk_done, 1)
                    if 0 <= step - 1 < ITEMS:
                        t = step - 1
                        pr, qi, e, b = items[t]
                        pe.wait_ge(exp_done, n0 + t + 1)
                        if t >= 2:
                            pe.wait_ge(pt_copied, n0 + t - 1)
                        tb = bank[4 + t % 2]
                        if b == 0:
                            mm = pe.transpose(tb[0:NCMP, 0:P], prob[:, t % 3, 0:NCMP], ident[:])
                        else:
                            for kj in range(qi + 1):
                                mm = pe.transpose(tb[:, kj * P:(kj + 1) * P], prob[:, t % 3, kj * P:(kj + 1) * P], ident[:])
                        mm.then_inc(pt_done, 1)
                    if 0 <= step - 2 < ITEMS:
                        t = step - 2
                        pr, qi, e, b = items[t]
                        unit = t // 6
                        pe.wait_ge(pt_copied, n0 + t + 1)
                        if t % 6 == 0 and unit >= 1:
                            pe.wait_ge(o_scaled, j * UNITS + unit)
                        o = bank[6][:, (e * 3 + b) * HD:(e * 3 + b + 1) * HD]
                        if b == 0:
                            mm = pe.matmul(o, prob_t[0:NCMP, t % 3, 0], vcg[:], start=True, stop=True)
                        else:
                            for kj in range(qi + 1):
                                mm = pe.matmul(o, prob_t[:, t % 3, kj], v_kv[:, b - 1, kj, ds(j * HD, HD)], start=kj == 0, stop=kj == qi)
                        mm.then_inc(pv_done, 1)
                    if step >= OT_LAG and (step - OT_LAG) % 6 == 0:
                        unit = (step - OT_LAG) // 6
                        qi = unit % TC
                        pe.wait_ge(o_summed, j * UNITS + unit + 1)
                        if qi == 0 and unit >= TC:
                            pe.wait_ge(oa_lo_done, j * 2 + unit // TC)
                        pe.transpose(bank[7][:, qi * P:(qi + 1) * P], o_rows[:, unit % 2], ident[:]).then_inc(o_turned, 1)
            runs(pe, GROUPS, attention)

            pe.wait_ge(ws_masked, 1)
            for g in range(SG):
                mm = pe.transpose(bank[4 + g // 4][:, (g % 4) * P:(g % 4 + 1) * P], ws_rows[:, g], ident[:])
            mm.then_inc(ws_turned, 1)

            ph = PH["sv"]
            def turn_v(n, u):
                pe.wait_ge(banks_read, ph.group0 + n + 1)
                wait(pe, v_rows_done, n - 1)
                for c in range(TC):
                    mm = pe.transpose(bank[2 + u][:, c * P:(c + 1) * P], sv_t[:, u, c * P:(c + 1) * P], ident[:])
                mm.then_inc(v_turned, 1)
            def sgu_v(i):
                for u in range(2):
                    group(ph, i, u, hi16, lo16)
                    if not (isinstance(i, int) and i == 0 and u == 0):
                        turn_v(i * 2 + u - 1, 1 - u)
            runs(pe, ph.n // 2, sgu_v, peel=True)
            turn_v(ph.n - 1, 1)

            ph = PH["su"]
            pe.wait_ge(ws_ready, 2)
            def mix(n, u):
                pe.wait_ge(vn_done, n + 1)
                wait(pe, mix_copied, n - 1)
                if isinstance(n, int) and n < 2:
                    pe.wait_ge(v_rows_done, SG)
                for c in range(TC):
                    mm = pe.matmul(bank[2 + u][:, c * P:(c + 1) * P], vn[:, u, c], ws_t[:, ds(n, 1), :],
                                   start=True, stop=True)
                mm.then_inc(mix_done, 1)
            def sgu_u(i):
                for u in range(2):
                    group(ph, i, u, hi16, lo16)
                    if not (isinstance(i, int) and i == 0 and u == 0):
                        mix(i * 2 + u - 1, 1 - u)
            runs(pe, ph.n // 2, sgu_u, peel=True)
            mix(ph.n - 1, 1)

            pe.wait_ge(oa_lo_done, 8)
            pe.wait_ge(ob_lo_done, SG)
            ph = PH["ab"]
            def ab(i):
                for u in range(2):
                    for a, (h, l) in enumerate(((oa_hi, oa_lo), (ob_hi, ob_lo))):
                        wait(pe, banks_read, ph.group(i, u) + a - 1)
                        dst = bank[(ph.group0 + a) % 2][:]
                        for q in range(2):
                            quarter(ph, i, u, 2 * a + q, dst, lambda k: h[:, k], lambda k: l[:, k], q == 0, q == 1, 4 * q)
            runs(pe, ph.n // 2, ab)

            ph = PH["wo"]
            pe.wait_ge(merge_hi_done, DK)
            pe.wait_ge(merge_lo_done, DK)
            def wo(i):
                for u in range(2):
                    def residual(dst):
                        pe.wait_ge(xcol_landed[u], i * 16 + 16)
                        for c in range(TC):
                            pe.matmul(dst[:, c * P:(c + 1) * P], x_cols[:, u, c], ident[:], start=False, stop=False)
                    group(ph, i, u, hi16, lo16, extra=residual)
                    n = i * 2 + u
                    pe.wait_ge(mem_cols_done, n + 1)
                    wait(pe, mem_lo, n - 1)
                    for c in range(MC):
                        mm = pe.transpose(bank[2 + u][:, c * P:(c + 1) * P], mem_cols[:, u, c], ident[:])
                    mm.then_inc(mem_turned, 1)
            runs(pe, ph.n // 2, wo, peel=True)

            def norm_total(src, tiles):
                pe.wait_ge(summed, tiles)
                pe.matmul(bank[4][:], ones[:], src[:], start=True, stop=True).then_inc(norm_sum, 1)

            norm_total(sumsq, DK)
            pe.wait_ge(mem_lo, DK)
            hm_h, hm_l = (lambda k: hm_hi[:, k]), (lambda k: hm_lo[:, k])
            ph = PH["mk"]
            def mem_keys(i):
                for u in range(2):
                    group(ph, i, u, hm_h, hm_l, n=MEM)
            runs(pe, ph.n // 2, mem_keys)
            ph = PH["mv"]
            def mem_values(i):
                for u in range(2):
                    group(ph, i, u, hm_h, hm_l, n=MEM)
                    pe.wait_ge(banks_read, ph.group(i, u) + 1)
                    wait(pe, mv_ready, i * 2 + u - 1)
                    for c in range(MC):
                        mm = pe.transpose(bank[2 + u][:, c * P:(c + 1) * P], mv_t[:, u, c * P:(c + 1) * P], ident[:])
                    mm.then_inc(mvt_turned, 1)
            runs(pe, ph.n // 2, mem_values, peel=True)
            pe.wait_ge(xg_lo, DK)
            pe.wait_ge(mv_ready, 4)
            ph = PH["mq"]
            for step in range(M_STEPS):
                if step < 16:
                    h, q = divmod(step, 4)
                    i, u = ph.at(h)
                    if q == 0:
                        pe.wait_ge(banks_read, ph.group0 + h - 1)
                    quarter(ph, i, u, q, bank[(ph.group0 + h) % 2][:], hi16, lo16, q == 0, q == 3, 4 * q)
                t = step - M_LAG
                if 0 <= t < M_ITEMS:
                    h, qi = divmod(t, TC)
                    if qi == 0:
                        pe.wait_ge(banks_read, ph.group0 + h + 1)
                    wait(pe, m_exp, t - 1)
                    pe.matmul(bank[2 + t % 2][:, 0:MEM], mq_t[:, h, qi * P:(qi + 1) * P], mk_t[:, h], start=True, stop=True).then_inc(m_qk, 1)
                t = step - M_LAG - 1
                if 0 <= t < M_ITEMS:
                    pe.wait_ge(m_norm, t + 1)
                    wait(pe, m_ptc, t - 1)
                    for c in range(MC):
                        mm = pe.transpose(bank[4 + t % 2][:, c * P:(c + 1) * P], m_prob_n[:, t % 3, c * P:(c + 1) * P], ident[:])
                    mm.then_inc(m_pt, 1)
                t = step - M_LAG - 2
                if 0 <= t < M_ITEMS:
                    h, qi = divmod(t, TC)
                    pe.wait_ge(m_ptc, t + 1)
                    if qi == 0:
                        wait(pe, mo_lo_done, h - 1)
                    for c in range(MC):
                        mm = pe.matmul(bank[6 + h % 2][:, qi * P:(qi + 1) * P], mv_rows[:, c, h * P:(h + 1) * P],
                                       m_prob_t[:, t % 3, c], start=c == 0, stop=c == MC - 1)
                    mm.then_inc(m_pv, 1)
            pe.wait_ge(mo_lo_done, MH)
            ph = PH["mo"]
            def mo(i):
                for u in range(2):
                    for j in range(4):
                        wait(pe, banks_read, ph.group(i, u) + j - 1)
                        quarter(ph, i, u, j, bank[(ph.group0 + j) % 2][:], lambda k: mo_hi[:, k], lambda k: mo_lo[:, k], True, True, 0)
            runs(pe, ph.n // 2, mo)
            norm_total(sumsq, 2 * DK)

            def turn_out(n, u):
                pe.wait_ge(added, n + 3 * DK + 1)
                wait(pe, y_copied, n - 1)
                for t in range(TC):
                    mm = pe.transpose(bank[2 + u][:, t * P:(t + 1) * P], x_out[:, u, t * P:(t + 1) * P], ident[:])
                mm.then_inc(y_turned, 1)
            tiles = 0
            for c, nk in enumerate(FFN_CHUNKS):
                ph = PH[f"f{c}"]
                def fi(i):
                    for u in range(2):
                        group(ph, i, u, hi16, lo16, ready=(xg_lo, DK) if c == 0 and u == 0 and isinstance(i, int) else None)
                runs(pe, ph.n // 2, fi, peel=c == 0)
                tiles += nk
                pe.wait_ge(ff_hi_done, tiles)
                pe.wait_ge(ff_lo_done, tiles)
                ph = PH[f"o{c}"]
                last = c == len(FFN_CHUNKS) - 1
                def fo(i):
                    for u in range(2):
                        group(ph, i, u, lambda k: ff_hi[:, k], lambda k: ff_lo[:, k])
                        if last and not (isinstance(i, int) and i == 0 and u == 0):
                            turn_out(i * 2 + u - 1, 1 - u)
                runs(pe, ph.n // 2, fo, peel=last)
            turn_out(DK - 1, 1)
            pe.wait_ge(summed, 3 * DK)
            for c in range(TC):
                mm = pe.matmul(bank[4][:, c:c + 1], sumsq_f[:, c * P:(c + 1) * P], ones[:, 0:1], start=True, stop=True)
            mm.then_inc(norm_sum, 1)

        @block.vector
        def _(dve):
            def split(ph, i, u, width=P, quarters=None):
                s = ph.slot(u)
                for q in quarters or range(ph.nq):
                    if q == 0:
                        dve.wait_ge(raw_landed[s], ph.landed(i, u))
                    n = ph.quarter(i, u) + q
                    wait(dve, quarters_done, n - ph.nq + 1)
                    src = raw[:, s, 4 * q:4 * q + 4, 0:width]
                    dve.tensor_copy(w_hi[:, q, :, 0:width], src).then_inc(hi_done, 1)
                    dve.wait_ge(hi_done, n + 1)
                    dve.tensor_tensor(w_lo[:, q, :, 0:width], src, w_hi[:, q, :, 0:width].bitcast(F32), ALU.subtract).then_inc(split_done, 1)

            def split_all(ph, start=0, peel=False):
                def body(i):
                    for u in range(2):
                        split(ph, i, u)
                if start == 0:
                    runs(dve, ph.n // 2, body, peel)
                else:
                    with dve.Fori(start, ph.n // 2) as i:
                        body(i)

            dve.memset(ones[:], 1.0).then_inc(ones_made, 1)
            dve.memset(eps[:], EPS).then_inc(ones_made, 1)
            split(PH["c"], 0, 0)
            for c in range(TC):
                dve.wait_ge(rms_done, c + 1)
                dve.reciprocal(rstd[:, c:c + 1], ss[:, c:c + 1]).then_inc(rstd_done, 1)
                dve.wait_ge(rstd_done, c + 1)
                dve.tensor_scalar(x_rows[:, c], x_rows[:, c], rstd[:, c:c + 1], None, ALU.mult).then_inc(x_scaled, 1)
            dve.wait_ge(cols_ready, 1)
            for k in range(DK):
                dve.wait_ge(turned_hi, k + 1)
                dve.scalar_tensor_tensor(out=act_lo[:, k], in0=bank[4 + k % 4][:], scalar=cols[:, G_MIX + k:G_MIX + k + 1],
                                         in1=act_hi[:, k].bitcast(F32), op0=ALU.mult, op1=ALU.subtract).then_inc(turned_lo, 1)
            ph = PH["c"]
            split(ph, 0, 1)
            split_all(ph, start=1)
            for name in ("q", "k", "v"):
                split_all(PH[name])
            split(PH["g"], 0, 0, width=48)
            ph = PH["merge"]
            split(ph, 0, 0, quarters=range(AHEAD))

            dve.wait_ge(gates_masked, 1)
            def attention(j):
                n0 = j * ITEMS
                for step in range(STEPS):
                    if step < ITEMS:
                        pr, qi, e, b = items[step]
                        n = NCMP if b == 0 else (qi + 1) * P
                        dve.wait_ge(qk_done, n0 + step + 1)
                        if step >= 4:
                            dve.wait_ge(exp_done, n0 + step - 3)
                        dve.tensor_reduce(neg_max[:, step % 4:step % 4 + 1], bank[2 + step % 2][:, 0:n], AX.X, ALU.max, negate=True).then_inc(max_done, 1)
                    if 0 <= step - 1 < ITEMS:
                        t = step - 1
                        pr, qi, e, b = items[t]
                        dve.wait_ge(pt_done, n0 + t + 1)
                        if t >= 3:
                            dve.wait_ge(pv_done, n0 + t - 2)
                        if b == 0:
                            dve.tensor_copy(prob_t[0:NCMP, t % 3, 0], bank[4 + t % 2][0:NCMP, 0:P]).then_inc(pt_copied, 1)
                        else:
                            dve.tensor_copy(prob_t[:, t % 3, 0:qi + 1].rearrange("p k q -> p (k q)"),
                                            bank[4 + t % 2][:, 0:(qi + 1) * P]).then_inc(pt_copied, 1)
                    if step >= SUM_LAG and (step - SUM_LAG) % 6 == 0:
                        unit = (step - SUM_LAG) // 6
                        if unit < UNITS:
                            pr, qi = unit // TC, unit % TC
                            un = j * UNITS + unit
                            ub = unit % 2
                            dve.wait_ge(pv_done, n0 + 6 * unit + 6)
                            dve.reciprocal(coef[:, ub], den[:, ub]).then_inc(coef_step, 1)
                            dve.wait_ge(coef_step, un * 2 + 1)
                            dve.tensor_tensor(coef[:, ub], coef[:, ub], gates[:, qi, ds(j * 12 + 6 * pr, 6)], ALU.mult).then_inc(coef_step, 1)
                            dve.wait_ge(coef_step, un * 2 + 2)
                            dve.tensor_tensor(o_parts[:, ub].rearrange("p e b d -> p (e b) d"),
                                              bank[6][:, 0:6 * HD].rearrange("p (s d) -> p s d", d=HD),
                                              coef[:, ub].unsqueeze(2).broadcast_to([P, 6, HD]), ALU.mult).then_inc(o_scaled, 1)
                            dve.wait_ge(o_scaled, un + 1)
                            if unit >= 2:
                                dve.wait_ge(o_turned, un - 1)
                            dve.tensor_reduce(o_rows[:, ub].rearrange("p (e d) -> p e d", e=2), o_parts[:, ub].rearrange("p e b d -> p e d b"),
                                              AX.X, ALU.add).then_inc(o_summed, 1)
                    if step in (OT_LAG + 19, OT_LAG + 43):
                        pair = (step - OT_LAG - 19) // 24
                        dve.wait_ge(oa_hi_done, j * 2 + pair + 1)
                        dve.tensor_tensor(oa_lo[:, ds(j * 2 + pair, 1), :], bank[7][:], oa_hi[:, ds(j * 2 + pair, 1), :].bitcast(F32), ALU.subtract).then_inc(oa_lo_done, 1)
                    for k in QUARTERS_AT[step]:
                        k += AHEAD
                        split(ph, j * 4, k // 4, quarters=(k % 4,))
            runs(dve, GROUPS, attention)
            ph = PH["sv"]
            split(ph, 0, 0, quarters=range(AHEAD, 4))
            split(ph, 0, 1)
            split_all(ph, start=1)
            ph = PH["su"]
            split(ph, 0, 0)
            dve.wait_ge(v_rows_done, SG)
            for c in range(TC):
                for h in range(2):
                    dve.bn_stats(bn[:, c, h], v_rows[:, c, h * 512:(h + 1) * 512]).then_inc(ln_stats, 1)
            dve.wait_ge(ln_stats, 2 * TC)
            for c in range(TC):
                dve.bn_aggr(mv_stat[:, c], bn[:, c].rearrange("p a b -> p (a b)")).then_inc(ln_stats, 1)
            dve.wait_ge(ln_sqrt, 1)
            dve.reciprocal(ln_rstd[:], ln_shift[:]).then_inc(ln_ready, 1)
            dve.wait_ge(ln_ready, 1)
            dve.scalar_tensor_tensor(out=ln_shift[:], in0=mv_stat[:, :, 0], scalar=-1.0, in1=ln_rstd[:],
                                     op0=ALU.mult, op1=ALU.mult).then_inc(ln_ready, 1)
            split(ph, 0, 1)
            split_all(ph, start=1)
            ph = PH["ab"]
            split(ph, 0, 0)
            dve.wait_ge(mem_rms, 1)
            dve.reciprocal(rstd[:, 0:MC], rstd[:, 0:MC]).then_inc(mem_rstd, 1)
            split(ph, 0, 1)
            split_all(ph, start=1)
            ph = PH["wo"]
            def mem_low(n, u):
                dve.wait_ge(mem_hi, n + 1)
                dve.scalar_tensor_tensor(out=hm_lo[:, ds(n, 1), :], in0=bank[2 + u][:, 0:MEM],
                                         scalar=cols[:, ds(n + G_MEM, 1)], in1=hm_hi[:, ds(n, 1), :].bitcast(F32),
                                         op0=ALU.mult, op1=ALU.subtract).then_inc(mem_lo, 1)
            def wo(i):
                for u in range(2):
                    split(ph, i, u)
                    if not (isinstance(i, int) and i == 0 and u == 0):
                        mem_low(i * 2 + u - 1, 1 - u)
            runs(dve, ph.n // 2, wo, peel=True)

            def inverse(n, buf):
                dve.wait_ge(norm_root, n + 1)
                dve.reciprocal(buf[:], buf[:]).then_inc(norm_inv, 1)
                dve.wait_ge(norm_inv, n + 1)

            def normed(k, done, gain):
                wait(dve, xg_hi, done + k - 1)
                wait(dve, xg_lo, done + k - 1)
                dve.scalar_tensor_tensor(out=xg[:, k % 2], in0=xt[:, k], scalar=cols[:, gain + k:gain + k + 1],
                                         in1=rms_bc[:], op0=ALU.mult, op1=ALU.mult).then_inc(xg_done, 1)

            split(PH["mk"], 0, 0)
            mem_low(DK - 1, 1)
            inverse(0, rms_bc)
            k = 0
            for n in range(1, 8):
                for _ in range(3 if n < 3 else 2):
                    normed(k, 0, G_CROSS)
                    k += 1
                split(PH["mk" if n < 4 else "mv"], n % 4 // 2, n % 2)
            assert k == DK
            quarters = [(PH["mq"], p, q) for p in range(4) for q in range(4)] + [(PH["mo"], 0, q) for q in range(4)]
            def split_next():
                m, p, q = quarters.pop(0)
                split(m, *m.at(p), quarters=(q,))
            for _ in range(AHEAD):
                split_next()
            for step in range(M_STEPS):
                t = step - M_LAG
                if 0 <= t < M_ITEMS:
                    dve.wait_ge(m_qk, t + 1)
                    wait(dve, m_exp, t - 3)
                    dve.tensor_reduce(neg_max[:, t % 4:t % 4 + 1], bank[2 + t % 2][:, 0:MEM], AX.X, ALU.max, negate=True).then_inc(m_max, 1)
                    dve.wait_ge(m_exp, t + 1)
                    dve.reciprocal(coef[:, 0, t % 3:t % 3 + 1], den[:, 0, t % 3:t % 3 + 1]).then_inc(m_inv, 1)
                    dve.wait_ge(m_inv, t + 1)
                    wait(dve, m_pt, t - 2)
                    dve.tensor_scalar(m_prob_n[:, t % 3], m_prob[:, t % 3], coef[:, 0, t % 3:t % 3 + 1], None, ALU.mult).then_inc(m_norm, 1)
                t = step - M_LAG - 1
                if 0 <= t < M_ITEMS:
                    dve.wait_ge(m_pt, t + 1)
                    wait(dve, m_pv, t - 2)
                    dve.tensor_copy(m_prob_t[:, t % 3].rearrange("p c q -> p (c q)"), bank[4 + t % 2][:, 0:MEM]).then_inc(m_ptc, 1)
                t = step - M_LAG - 3
                if t >= 0 and t % TC == TC - 1:
                    h = t // TC
                    dve.wait_ge(mo_hi_done, h + 1)
                    dve.tensor_tensor(mo_lo[:, h], bank[6 + h % 2][:], mo_hi[:, h].bitcast(F32), ALU.subtract).then_inc(mo_lo_done, 1)
                if quarters and step < 16 + 4 - AHEAD:
                    split_next()
            assert not quarters
            split(PH["mo"], 0, 1)
            split_all(PH["mo"], start=1)
            split(PH["f0"], 0, 0)
            inverse(1, rms_bc)
            for k in range(DK):
                normed(k, DK, G_FFN)
            split(PH["f0"], 0, 1)
            split_all(PH["f0"], start=1)
            for name in ("o0", "f1", "o1", "f2", "o2"):
                split_all(PH[name])
            dve.wait_ge(norm_root, 3)
            dve.reciprocal(rstd[:], ss[:]).then_inc(rstd_done, 1)
            dve.wait_ge(rstd_done, TC + 1)
            dve.wait_ge(final_g_landed, 16)
            dve.wait_ge(y_copied, DK)
            for c in range(TC):
                dve.scalar_tensor_tensor(out=y_rows[:, c], in0=y_rows[:, c], scalar=rstd[:, c:c + 1], in1=final_g_bc[:],
                                         op0=ALU.mult, op1=ALU.mult).then_inc(y_done, 1)

        @block.scalar
        def _(act):
            for c in range(1, TC, 2):
                act.dma_start(x_rows[:, c], x_v[:, c]).then_inc(x_landed[c], 16)
            row = 0
            for g in (norm_mix_g[0], norm_cross_g[0], norm_mem_g[0], norm_ffn_g[0], norm_final_g):
                act.dma_start(small_rows[row:row + 16], g.rearrange("(k p) -> k p", p=P)).then_inc(small_landed, 16)
                row += 16
            for g in (cmp_pe_k[0], cmp_pe_v[0]):
                act.dma_start(small_rows[row:row + 16], g.rearrange("(k a) d -> k (a d)", a=2)).then_inc(small_landed, 16)
                row += 16
            for g in (cmp_k_b1[0], cmp_v_b1[0]):
                act.dma_start(small_rows[row:row + 2], g.rearrange("(k p) -> k p", p=P)).then_inc(small_landed, 16)
                row += 2
            for s, w in enumerate((cmp_k_w2, cmp_v_w2)):
                act.dma_start(w2[:, s], w[0].rearrange("(k p) n -> p k n", p=P)).then_inc(sgu_landed, 16)

            for c in range(TC):
                act.wait_ge(x_landed[c], 16)
                wait(act, sq_done, c)
                act.activation(junk[:], x_rows[:, c], ACT.Square,
                               accum_out=ss[:, c:c + 1]).then_inc(sq_done, 1)
            act.wait_ge(ones_made, 2)
            for c in range(TC):
                act.wait_ge(sq_done, c + 1)
                act.activation(ss[:, c:c + 1], ss[:, c:c + 1], ACT.Sqrt, scale=1.0 / D, bias=eps[:]).then_inc(rms_done, 1)
            act.wait_ge(cols_turned, 1)
            act.activation(cols[:], bank[0][:, 0:116], ACT.Copy).then_inc(cols_ready, 1)
            act.wait_ge(cols_ready, 1)
            for k in range(DK):
                act.wait_ge(turned, k + 1)
                act.activation(act_hi[:, k], bank[4 + k % 4][:], ACT.Copy, scale=cols[:, G_MIX + k:G_MIX + k + 1]).then_inc(turned_hi, 1)
            def result(ph, i, u, g=0, upto=None):
                q = ph.nq if upto is None else upto
                act.wait_ge(quarters_done, ph.quarter(i, u) + q)
                return bank[(ph.group0 + ph.ng * u + g) % 2]

            ph = PH["c"]
            def cmp_streams(i):
                for u in range(2):
                    src = result(ph, i, u)
                    for g in range(2):
                        act.activation(kv_src[0:HD, ds(i, 1), 2 * u + g, :], src[g * HD:(g + 1) * HD, :], ACT.Copy)
                        a = act.activation(kv_src[HD:P, ds(i, 1), 2 * u + g, 0:T - 1], src[g * HD:(g + 1) * HD, 1:T], ACT.Copy)
                    a.then_inc(banks_read, 1)
            runs(act, ph.n // 2, cmp_streams)
            ph = PH["q"]
            def queries(i):
                for u in range(2):
                    act.activation(q_t[:, ds(i * 2 + u, 1), :], result(ph, i, u)[:], ACT.Copy, scale=HD ** -0.5).then_inc(banks_read, 1)
            runs(act, ph.n // 2, queries)
            for s in range(2):
                for hh in range(2):
                    act.wait_ge(hid_done, 2 * s + hh + 1)
                    act.activation(hid_t[s][:, hh], bank[4 + 2 * s + hh][:, 0:GROUPS * NCMP], ACT.Gelu_apprx_tanh,
                                   bias=cols[:, B1_K + 2 * s + hh:B1_K + 2 * s + hh + 1]).then_inc(hid_act, 1)
            ph = PH["k"]
            def keys(i):
                for u in range(2):
                    src = result(ph, i, u)
                    for g in range(2):
                        a = act.activation(k_t[:, ds(i, 1), 2 * u + g, :], src[g * HD:(g + 1) * HD, :], ACT.Copy)
                    a.then_inc(banks_read, 1)
            runs(act, ph.n // 2, keys)
            act.wait_ge(cmp_out, 1)
            act.activation(kc_t[:], bank[2][0:HD, 0:GROUPS * NCMP], ACT.Copy).then_inc(cmp_ready, 1)
            act.wait_ge(cmp_out, 2)
            act.activation(vc[:].rearrange("n g d -> n (g d)"), bank[3][0:NCMP, 0:GROUPS * HD], ACT.Copy).then_inc(cmp_ready, 1)
            ph = PH["v"]
            def values(i):
                for u in range(2):
                    n = i * 2 + u
                    src = result(ph, i, u)
                    wait(act, kv_turned, n - 1)
                    act.activation(vt[:, u], src[:], ACT.Copy).then_inc(banks_read, 1)
                    act.wait_ge(kv_turned, n + 1)
                    act.activation(v_kv[:, ds(i, 1), :, u * P:(u + 1) * P], bank[2 + u][:].rearrange("p (c f) -> p c f", c=TC), ACT.Copy).then_inc(kv_rows_done, 1)
            runs(act, ph.n // 2, values, peel=True)
            ph = PH["g"]
            act.activation(gate_t[:], result(ph, 0, 0)[0:48, :], ACT.Copy).then_inc(banks_read, 1)
            act.wait_ge(kv_turned, 5)
            act.activation(gates[:].rearrange("p c g -> p (c g)"), bank[2][:, 0:TC * 48], ACT.Sigmoid).then_inc(gates_done, 1)

            ph = PH["merge"]
            def attention(j):
                n0 = j * ITEMS
                act.activation(vcg[:], vc[:, ds(j, 1), :].rearrange("n a d -> n (a d)"), ACT.Copy).then_inc(staged, 1)
                for pr in range(2):
                    for e in range(2):
                        act.activation(qs[:, 2 * pr + e], q_t[e * HD:(e + 1) * HD, ds(j * 2 + pr, 1), :], ACT.Copy).then_inc(staged, 1)
                for step in range(STEPS):
                    if step < ITEMS:
                        pr, qi, e, b = items[step]
                        n = NCMP if b == 0 else (qi + 1) * P
                        unit = step // 6
                        act.wait_ge(max_done, n0 + step + 1)
                        if step >= 3:
                            act.wait_ge(pt_done, n0 + step - 2)
                        if step % 6 == 0 and unit >= 2:
                            act.wait_ge(o_scaled, j * UNITS + unit - 1)
                        act.activation(prob[:, step % 3, 0:n], bank[2 + step % 2][:, 0:n], ACT.Exp,
                                       bias=neg_max[:, step % 4:step % 4 + 1],
                                       accum_out=den[:, unit % 2, e * 3 + b:e * 3 + b + 1]).then_inc(exp_done, 1)
                    if step in (OT_LAG + 18, OT_LAG + 42):
                        pair = (step - OT_LAG - 18) // 24
                        act.wait_ge(o_turned, j * UNITS + TC * pair + TC)
                        act.activation(oa_hi[:, ds(j * 2 + pair, 1), :], bank[7][:], ACT.Copy).then_inc(oa_hi_done, 1)
                    for k in (QUARTERS_AT[step - 1] if step else []) + (QUARTERS_AT[step] if step == STEPS - 1 else []):
                        if k % 4 == 3:
                            p = k // 4
                            act.wait_ge(quarters_done, j * 32 + ph.quarter0 + k + 1)
                            if p >= 2:
                                act.wait_ge(gate_stored[p % 2], j * 64 + 16 * (p // 2))
                            act.activation(gate_out[:, p % 2], bank[(ph.group0 + p) % 2][:], ACT.Copy).then_inc(banks_read, 1)
                            act.wait_ge(banks_read, j * 8 + ph.group0 + p + 1)
                            act.dma_start(merge_dram[ds((j * 8 + p) * P, P), :], gate_out[:, p % 2]).then_inc(gate_stored[p % 2], 16)
                for b in range(2):
                    act.wait_ge(gate_stored[b], j * 64 + 64)
            runs(act, GROUPS, attention)

            act.wait_ge(oa_lo_done, 8)
            act.dma_start(ws_rows[:], sgu_ws[0].rearrange("g t s -> t g s")).then_inc(ws_landed, 16)
            act.wait_ge(ws_turned, 1)
            for h in range(2):
                act.activation(ws_t[:, 4 * h:4 * h + 4].rearrange("p g t -> p (g t)"), bank[4 + h][:], ACT.Copy).then_inc(ws_ready, 1)
            ph = PH["sv"]
            def v_out(n, u):
                act.wait_ge(v_turned, n + 1)
                act.activation(v_rows[:, :, ds(n * P, P)], bank[2 + u][:].rearrange("p (c f) -> p c f", c=TC), ACT.Copy).then_inc(v_rows_done, 1)
            def sgu_v(i):
                for u in range(2):
                    n = i * 2 + u
                    src = result(ph, i, u)
                    wait(act, v_turned, n - 1)
                    act.activation(sv_t[:, u], src[:], ACT.Gelu_apprx_tanh).then_inc(banks_read, 1)
                    if not (isinstance(i, int) and n == 0):
                        v_out(n - 1, 1 - u)
            runs(act, ph.n // 2, sgu_v, peel=True)
            v_out(ph.n - 1, 1)
            act.wait_ge(ln_stats, 3 * TC)
            act.activation(ln_shift[:], mv_stat[:, :, 1], ACT.Sqrt, bias=eps[:]).then_inc(ln_sqrt, 1)
            act.wait_ge(ln_ready, 2)

            ph = PH["su"]
            def mix_out(n, u):
                act.wait_ge(mix_done, n + 1)
                wait(act, ob_done, n)
                act.activation(mixed[:].rearrange("p c t -> p (c t)"), bank[2 + u][:], ACT.Copy).then_inc(mix_copied, 1)
                act.wait_ge(ob_done, n + 1)
                act.activation(ob_hi[:, ds(n, 1), :], ob[:], ACT.Copy).then_inc(ob_hi_done, 1)
            def rows_in(n, u):
                for r, src in enumerate((sgu_ln_g[0], sgu_ln_b[0], sgu_b[0].rearrange("g t -> (g t)"))):
                    act.dma_start(rows_bc[:, u, r], src[ds(n * P, P)].partition_broadcast(P)).then_inc(rows_landed[u], 16)
            def sgu_u(i):
                for u in range(2):
                    n = i * 2 + u
                    wait(act, vn_done, n - 1)
                    for c in range(TC):
                        a = act.activation(vz[:, u, c], v_rows[:, c, ds(n * P, P)], ACT.Identity,
                                           scale=ln_rstd[:, c:c + 1], bias=ln_shift[:, c:c + 1])
                    a.then_inc(vz_done, 1)
                    src = result(ph, i, u)
                    wait(act, ob_done, n - 1)
                    act.activation(ut[:, u], src[:], ACT.Gelu_apprx_tanh).then_inc(banks_read, 1)
                    if not (isinstance(i, int) and n == 0):
                        mix_out(n - 1, 1 - u)
                    if not (isinstance(i, int) and n in (0, SG - 1)):
                        rows_in(n + 1, 1 - u)
            rows_in(0, 0)
            rows_in(1, 1)
            runs(act, ph.n // 2 - 1, sgu_u, peel=True)
            sgu_u(ph.n // 2 - 1)
            mix_out(ph.n - 1, 1)

            act.wait_ge(mem_landed, 16)
            for c in range(MC):
                wait(act, mem_sq, c)
                act.activation(mem_junk[:], mem_rows[:, c], ACT.Square, accum_out=ss[:, c:c + 1]).then_inc(mem_sq, 1)
            act.wait_ge(mem_sq, MC)
            act.activation(rstd[:, 0:MC], ss[:, 0:MC], ACT.Sqrt, scale=1.0 / D, bias=eps[:]).then_inc(mem_rms, 1)

            ph = PH["ab"]
            def merge_hi(n, u):
                act.wait_ge(merge_done, n + 1)
                act.activation(act_hi[:, ds(n, 1), :], merged[:, u], ACT.Copy).then_inc(merge_hi_done, 1)
            def ab(i):
                for u in range(2):
                    n = i * 2 + u
                    act.wait_ge(gates_landed[u], i * 32 + 32)
                    act.activation(gate_in[:, u], gate_in[:, u], ACT.Sigmoid).then_inc(gates_open, 1)
                    src = result(ph, i, u, 0, 2)
                    wait(act, merge_done, n - 1)
                    act.activation(pa[:, u], src[:], ACT.Copy).then_inc(banks_read, 1)
                    if not (isinstance(i, int) and n == 0):
                        merge_hi(n - 1, 1 - u)
                    src = result(ph, i, u, 1, 4)
                    act.activation(pb[:, u], src[:], ACT.Copy).then_inc(banks_read, 1)
            runs(act, ph.n // 2, ab, peel=True)
            merge_hi(ph.n - 1, 1)

            ph = PH["wo"]
            act.wait_ge(mem_rstd, 1)
            def wo(i):
                for u in range(2):
                    n = i * 2 + u
                    wait(act, mem_turned, n - 1)
                    for c in range(MC):
                        a = act.activation(mem_cols[:, u, c], mem_rows[:, c, ds(n * P, P)], ACT.Copy, scale=rstd[:, c:c + 1])
                    a.then_inc(mem_cols_done, 1)
                    src = result(ph, i, u)
                    wait(act, summed, n - 1)
                    act.activation(sq[:, u], src[:], ACT.Square).then_inc(squared, 1)
                    act.activation(xt[:, ds(n, 1), :], src[:], ACT.Copy).then_inc(banks_read, 1)
                    act.wait_ge(mem_turned, n + 1)
                    act.activation(hm_hi[:, ds(n, 1), :], bank[2 + u][:, 0:MEM], ACT.Copy, scale=cols[:, ds(n + G_MEM, 1)]).then_inc(mem_hi, 1)
            runs(act, ph.n // 2, wo, peel=True)

            def root(n, buf):
                act.wait_ge(norm_sum, n + 1)
                act.activation(buf[:], bank[4][:], ACT.Sqrt, scale=1.0 / D, bias=eps[:]).then_inc(norm_root, 1)

            def split_hi(k, done):
                act.wait_ge(xg_done, done + k + 1)
                act.activation(act_hi[:, k], xg[:, k % 2], ACT.Copy).then_inc(xg_hi, 1)

            root(0, rms_bc)
            k = 0
            for n in range(8):
                if n > 0:
                    for _ in range(3 if n < 3 else 2):
                        split_hi(k, 0)
                        k += 1
                ph = PH["mk" if n < 4 else "mv"]
                i, u = n % 4 // 2, n % 2
                src = result(ph, i, u)
                if n < 4:
                    act.activation(mk_t[:, n], src[:, 0:MEM], ACT.Copy).then_inc(banks_read, 1)
                else:
                    wait(act, mvt_turned, n - 5)
                    act.activation(mv_t[:, u], src[:, 0:MEM], ACT.Copy).then_inc(banks_read, 1)
                    act.wait_ge(mvt_turned, n - 3)
                    act.activation(mv_rows[:, :, (n - 4) * P:(n - 3) * P], bank[2 + u][:, 0:MEM].rearrange("p (c f) -> p c f", c=MC), ACT.Copy).then_inc(mv_ready, 1)
            ph = PH["mq"]
            for step in range(M_STEPS + 1):
                if step in (4, 8, 12, 16):
                    h = step // 4 - 1
                    act.activation(mq_t[:, h], result(ph, h // 2, h % 2)[:], ACT.Copy, scale=P ** -0.5).then_inc(banks_read, 1)
                t = step - M_LAG
                if 0 <= t < M_ITEMS:
                    act.wait_ge(m_max, t + 1)
                    wait(act, m_norm, t - 2)
                    act.activation(m_prob[:, t % 3], bank[2 + t % 2][:, 0:MEM], ACT.Exp, bias=neg_max[:, t % 4:t % 4 + 1],
                                   accum_out=den[:, 0, t % 3:t % 3 + 1]).then_inc(m_exp, 1)
                t = step - M_LAG - 3
                if t >= 0 and t % TC == TC - 1:
                    h = t // TC
                    act.wait_ge(m_pv, TC * (h + 1))
                    act.activation(mo_hi[:, h], bank[6 + h % 2][:], ACT.Copy).then_inc(mo_hi_done, 1)

            def add_out(ph, i, u, g, n, tile, total):
                src = result(ph, i, u, g, g + 1 if ph.ng > 1 else None)
                wait(act, added, n - 1)
                act.activation(add_in[:, g % 2 if ph.ng > 1 else u], src[:], ACT.Copy).then_inc(banks_read, 1)

            def square(n, tile, b, buf, sq0):
                act.wait_ge(added, n + 1)
                wait(act, summed, sq0 - 1)
                act.activation(buf, xt[:, ds(tile, 1), :], ACT.Square).then_inc(squared, 1)

            ph = PH["mo"]
            def mo(i):
                for u in range(2):
                    for j in range(4):
                        n = (i * 2 + u) * 4 + j
                        add_out(ph, i, u, j, n, n, DK)
                        if not (isinstance(i, int) and n == 0):
                            square(n - 1, n - 1, 1 - j % 2, sq[:, 1 - j % 2], DK + n - 1)
            runs(act, ph.n // 2, mo, peel=True)
            square(DK - 1, DK - 1, 1, sq[:, 1], 2 * DK - 1)
            root(1, rms_bc)
            for k in range(DK):
                split_hi(k, DK)
            tiles = 0
            n_add = DK
            for c, nk in enumerate(FFN_CHUNKS):
                ph = PH[f"f{c}"]
                act.wait_ge(added, n_add)
                def fi(i):
                    src = result(ph, i, 0)
                    wait(act, ff_done, tiles + i)
                    act.activation(gated[:], src[:], ACT.Silu).then_inc(banks_read, 1)
                    src = result(ph, i, 1)
                    act.activation(up[:], src[:], ACT.Copy).then_inc(banks_read, 1)
                    act.wait_ge(ff_done, tiles + i + 1)
                    act.activation(ff_hi[:, ds(i, 1), :], ff[:], ACT.Copy).then_inc(ff_hi_done, 1)
                runs(act, nk, fi, peel=c == 0)
                tiles += nk
                ph = PH[f"o{c}"]
                last = c == len(FFN_CHUNKS) - 1
                def y_out(n, u):
                    act.wait_ge(y_turned, n + 1)
                    act.activation(y_rows[:, :, ds(n * P, P)], bank[2 + u][:].rearrange("p (c f) -> p c f", c=TC), ACT.Copy).then_inc(y_copied, 1)
                def fo(i):
                    for u in range(2):
                        n = i * 2 + u
                        src = result(ph, i, u)
                        wait(act, added, n_add + n - 1)
                        act.activation(add_in[:, u], src[:], ACT.Copy).then_inc(banks_read, 1)
                        if last:
                            act.wait_ge(added, n_add + n + 1)
                            wait(act, summed, 2 * DK + n)
                            act.activation(ff[:], x_out[:, u], ACT.Square).then_inc(squared, 1)
                            if not (isinstance(i, int) and n == 0):
                                y_out(n - 1, 1 - u)
                if last:
                    act.wait_ge(ff_lo_done, FK)
                    act.dma_start(final_g_bc[:], norm_final_g.partition_broadcast(P)).then_inc(final_g_landed, 16)
                runs(act, ph.n // 2, fo, peel=last)
                n_add += DK
            y_out(DK - 1, 1)
            act.wait_ge(norm_sum, 3)
            act.activation(ss[:], bank[4][:, 0:TC], ACT.Sqrt, scale=1.0 / D, bias=eps[:]).then_inc(norm_root, 1)

        @block.gpsimd
        def _(pool):
            pool.memset(ident[:], 0.0).then_inc(ident_zero, 1)
            pool.memset(ident_b[:], 0.0).then_inc(ident_zero, 1)
            pool.wait_ge(ident_zero, 2)
            for m in (ident, ident_b):
                pool.affine_select(out=m[:], in_=m[:], compare_op=ALU.not_equal, fill=1.0, base=0,
                                   pattern=[[-1, P]], channel_multiplier=1).then_inc(ident_made, 1)
            pool.memset(causal_b[:], 0.0).then_inc(masks_zero, 1)
            pool.memset(cmp_mask_b[:], 0.0).then_inc(masks_zero, 1)
            pool.memset(valid[:], 1.0).then_inc(masks_zero, 1)
            pool.wait_ge(masks_zero, 3)
            pool.affine_select(out=causal_b[:], in_=causal_b[:], compare_op=ALU.is_ge, fill=MASKED, base=0,
                               pattern=[[-1, P]], channel_multiplier=1).then_inc(masks_made, 1)
            pool.affine_select(out=cmp_mask_b[:], in_=cmp_mask_b[:], compare_op=ALU.is_ge, fill=MASKED, base=1 - CMP_LEN,
                               pattern=[[P, TC], [-CMP_STEP, NCMP]], channel_multiplier=1).then_inc(masks_made, 1)
            pool.affine_select(out=valid[:], in_=valid[:], compare_op=ALU.is_ge, fill=0.0, base=1 - CMP_LEN,
                               pattern=[[0, 1]], channel_multiplier=1).then_inc(masks_made, 1)
            pool.wait_ge(banks_read, PH["c"].groups_end())
            for s in range(2):
                for g in range(GROUPS):
                    src = kv_src[:, s, g].rearrange("p (n k a) -> p a k n", k=8, a=2)[:, 0]
                    for h in range(2):
                        pe_col = (PE_K, PE_V)[s] + 8 * h
                        a = pool.tensor_tensor(blocks[s][:, 8 * h:8 * h + 8, g], src[:, :, h:h + NCMP],
                                               cols[:, pe_col:pe_col + 8].unsqueeze(2).broadcast_to([P, 8, NCMP]), ALU.add)
                a.then_inc(blocks_done, 1)
            pool.wait_ge(gates_done, 1)
            g0 = gates[:, 0].rearrange("p (h b) -> p b h", b=3)[:, 0]
            pool.tensor_scalar(g0, g0, valid[:], None, ALU.mult).then_inc(gates_masked, 1)

            pool.wait_ge(ws_landed, 16)
            pool.affine_select(out=ws_rows[:], in_=ws_rows[:], compare_op=ALU.is_ge, fill=0.0, base=0,
                               pattern=[[0, SG], [-1, P]], channel_multiplier=1).then_inc(ws_masked, 1)

            ph = PH["su"]
            def gate_out_tile(n, u):
                pool.wait_ge(mix_copied, n + 1)
                pool.tensor_tensor(mixed[:], mixed[:], rows_bc[:, u, 2].unsqueeze(1).broadcast_to([P, TC, P]), ALU.add).then_inc(ob_step, 1)
                pool.wait_ge(ob_step, n + 1)
                wait(pool, ob_lo_done, n)
                pool.tensor_tensor(ob[:], mixed[:].rearrange("p c t -> p (c t)"), ut[:, u], ALU.mult).then_inc(ob_done, 1)
                pool.wait_ge(ob_hi_done, n + 1)
                pool.tensor_tensor(ob_lo[:, ds(n, 1), :], ob[:], ob_hi[:, ds(n, 1), :].bitcast(F32), ALU.subtract).then_inc(ob_lo_done, 1)
            def sgu_u(i):
                for u in range(2):
                    n = i * 2 + u
                    pool.wait_ge(rows_landed[u], i * 48 + 48)
                    pool.wait_ge(vz_done, n + 1)
                    wait(pool, mix_done, n - 1)
                    pool.tensor_tensor(vz[:, u], vz[:, u], rows_bc[:, u, 0].unsqueeze(1).broadcast_to([P, TC, P]), ALU.mult).then_inc(vn_step, 1)
                    pool.wait_ge(vn_step, n + 1)
                    pool.tensor_tensor(vn[:, u], vz[:, u], rows_bc[:, u, 1].unsqueeze(1).broadcast_to([P, TC, P]), ALU.add).then_inc(vn_done, 1)
                    if not (isinstance(i, int) and n == 0):
                        gate_out_tile(n - 1, 1 - u)
            runs(pool, ph.n // 2, sgu_u, peel=True)
            gate_out_tile(ph.n - 1, 1)

            ph = PH["ab"]
            def ab(i):
                for u in range(2):
                    n = i * 2 + u
                    pool.wait_ge(gates_open, n + 1)
                    pool.wait_ge(banks_read, ph.group(i, u) + 2)
                    pool.tensor_tensor(pa[:, u], pa[:, u], gate_in[:, u, 0], ALU.mult).then_inc(merge_step, 1)
                    pool.tensor_tensor(pb[:, u], pb[:, u], gate_in[:, u, 1], ALU.mult).then_inc(merge_step, 1)
                    pool.wait_ge(merge_step, n * 2 + 2)
                    pool.tensor_tensor(merged[:, u], pa[:, u], pb[:, u], ALU.add).then_inc(merge_done, 1)
                    pool.wait_ge(merge_hi_done, n + 1)
                    pool.tensor_tensor(act_lo[:, ds(n, 1), :], merged[:, u], act_hi[:, ds(n, 1), :].bitcast(F32), ALU.subtract).then_inc(merge_lo_done, 1)
            runs(pool, ph.n // 2, ab)

            def clear(buf, n):
                pool.memset(buf[:], 0.0).then_inc(sumsq_zero, 1)
                pool.wait_ge(sumsq_zero, n)

            def total(buf, sqr, n):
                pool.wait_ge(squared, n + 1)
                wait(pool, summed, n)
                pool.tensor_tensor(buf[:], buf[:], sqr, ALU.add).then_inc(summed, 1)

            def split_lo(k, done):
                pool.wait_ge(xg_hi, done + k + 1)
                pool.tensor_tensor(act_lo[:, k], xg[:, k % 2], act_hi[:, k].bitcast(F32), ALU.subtract).then_inc(xg_lo, 1)

            clear(sumsq, 1)
            def wo(i):
                for u in range(2):
                    total(sumsq, sq[:, u], i * 2 + u)
            runs(pool, DK // 2, wo, peel=True)
            for k in range(DK):
                split_lo(k, 0)

            pool.wait_ge(norm_sum, 1)
            clear(sumsq, 2)
            ph = PH["mo"]
            def mo(i):
                for u in range(2):
                    for j in range(4):
                        n = (i * 2 + u) * 4 + j
                        pool.wait_ge(banks_read, ph.group(i, u) + j + 1)
                        pool.tensor_tensor(xt[:, ds(n, 1), :], xt[:, ds(n, 1), :], add_in[:, j % 2], ALU.add).then_inc(added, 1)
                        if not (isinstance(i, int) and n == 0):
                            total(sumsq, sq[:, 1 - j % 2], n - 1 + DK)
            runs(pool, ph.n // 2, mo, peel=True)
            total(sumsq, sq[:, 1], 2 * DK - 1)
            for k in range(DK):
                split_lo(k, DK)

            clear(sumsq_f, 3)
            tiles = 0
            for c, nk in enumerate(FFN_CHUNKS):
                ph = PH[f"f{c}"]
                def fi(i):
                    pool.wait_ge(banks_read, ph.group(i, 1) + 1)
                    wait(pool, ff_lo_done, i + tiles)
                    pool.tensor_tensor(ff[:], gated[:], up[:], ALU.mult).then_inc(ff_done, 1)
                    pool.wait_ge(ff_hi_done, i + tiles + 1)
                    pool.tensor_tensor(ff_lo[:, ds(i, 1), :], ff[:], ff_hi[:, ds(i, 1), :].bitcast(F32), ALU.subtract).then_inc(ff_lo_done, 1)
                runs(pool, nk, fi, peel=c == 0)
                tiles += nk
                ph = PH[f"o{c}"]
                last = c == len(FFN_CHUNKS) - 1
                def fo(i):
                    for u in range(2):
                        n = i * 2 + u
                        pool.wait_ge(banks_read, ph.group(i, u) + 1)
                        if last:
                            wait(pool, y_turned, n - 1)
                        pool.tensor_tensor(x_out[:, u] if last else xt[:, ds(n, 1), :], xt[:, ds(n, 1), :].rearrange("p a t -> p (a t)") if last else xt[:, ds(n, 1), :],
                                           add_in[:, u], ALU.add).then_inc(added, 1)
                        if last:
                            total(sumsq_f, ff[:], n + 2 * DK)
                runs(pool, ph.n // 2, fo, peel=last)


_INS = ["x", "mem", "norm_mix_g", "w_in", "cmp_pe_k", "cmp_k_w1", "cmp_k_b1", "cmp_k_w2", "cmp_pe_v", "cmp_v_w1",
        "cmp_v_b1", "cmp_v_w2", "sgu_ln_g", "sgu_ln_b", "sgu_ws", "sgu_b", "w_proj_a", "w_proj_b", "w_mix_out",
        "norm_cross_g", "norm_mem_g", "w_mq", "w_mkv", "w_mo", "norm_ffn_g", "w_ffn_in", "w_ffn_out", "norm_final_g"]
_OUTS = [((1, T, D), "float32")]


def kernel(**inputs):
    import numpy as _np
    import concourse.bacc as _bacc
    from concourse import mybir as _mybir
    from concourse.bass_utils import run_bass_kernel_spmd as _run

    nc = _bacc.Bacc("TRN2", target_bir_lowering=False, num_devices=1)
    arrays, args = {}, []
    for name in _INS:
        a = _np.ascontiguousarray(inputs[name])
        arrays[f"in_{name}_dram"] = a
        args.append(nc.dram_tensor(f"in_{name}_dram", a.shape, _mybir.dt.from_np(a.dtype), kind="ExternalInput").ap())
    for i, (shape, dtype) in enumerate(_OUTS):
        dt = _mybir.dt.from_np(_np.dtype(dtype))
        args.append(nc.dram_tensor(f"out_{i}_dram", shape, dt, kind="ExternalOutput").ap())
    build(nc, *args)
    r = _run(nc, [arrays], core_ids=[0])
    got = tuple(r.results[0][f"out_{i}_dram"] for i in range(len(_OUTS)))
    return got[0]
```

```python
import concourse.bass as bass
from concourse import mybir
from contextlib import ExitStack

F32 = mybir.dt.float32
F32R = mybir.dt.float32r
BF16 = mybir.dt.bfloat16
ACT = mybir.ActivationFunctionType
ALU = mybir.AluOpType
AX = mybir.AxisListType

P = 128
T = 512
TC = T // P
D = 2048
DK = D // P
MEM = 256
MC = MEM // P
HEADS, GROUPS, HD = 16, 4, 64
HPG = HEADS // GROUPS
CMP_LEN, CMP_STEP = 32, 16
NCMP = (T - CMP_LEN) // CMP_STEP + 1
CMP_HID = 256
SG = 8
MH = 4
FF = (8 * D + 3 * 256 - 1) // (3 * 256) * 256
FK = FF // P
FFN_CHUNKS = (16, 16, 12)
EPS = 1e-6
MASKED = -1e30
KIB = 1024

C_Q, C_KV = 0, 1024
C_NSA_GATE = C_KV + 6 * 256
C_U = C_NSA_GATE + 48
C_V = C_U + 1024
C_MERGE = C_V + 1024

assert sum(FFN_CHUNKS) == FK and T // 64 <= 16 and T <= 512


class Phase:

    def __init__(self, prev, panels, quarters=4, groups=1, dmas=1):
        self.n, self.nq, self.ng, self.nd = panels, quarters, groups, dmas
        if prev is None:
            self.panel0 = self.quarter0 = self.group0 = 0
            self.landed0 = (0, 0)
        else:
            self.panel0 = prev.panel0 + prev.n
            self.quarter0 = prev.quarter0 + prev.n * prev.nq
            self.group0 = prev.group0 + prev.n * prev.ng
            used = [sum(1 for k in range(prev.n) if (prev.panel0 + k) % 2 == s) for s in (0, 1)]
            self.landed0 = tuple(prev.landed0[s] + 16 * prev.nd * used[s] for s in (0, 1))
        self.first = prev is None

    def slot(self, u):
        return (self.panel0 + u) % 2

    def landed(self, i, u):
        return self.landed0[self.slot(u)] + 16 * self.nd * (i + u // 2 + 1)

    def quarter(self, i, u):
        return self.quarter0 + self.nq * (2 * i + u)

    def group(self, i, u):
        return self.group0 + self.ng * (2 * i + u)

    def at(self, p):
        return p // 2, p % 2

    def end(self):
        return self.quarter0 + self.n * self.nq

    def groups_end(self):
        return self.group0 + self.n * self.ng


def step_cost(items, step, t_lag, pv_lag):
    cost = 0
    for lag, fixed, per_tile in ((0, 1, 4), (t_lag, 0, 4), (pv_lag, 0, 2)):
        if 0 <= step - lag < len(items):
            pr, qi, e, b = items[step - lag]
            cost += fixed + per_tile * (qi + 1 if b else 1)
    return cost * P // 2


def spread(tiles, costs):
    each = 3 * T
    total = sum(costs) + tiles * each
    at, left, spent = [], list(range(tiles)), 0
    for step, cost in enumerate(costs):
        spent += cost
        goal = total * (step + 1) / len(costs)
        n = 0 if step < len(costs) - 1 else len(left)
        while n < len(left) and spent + n * each < goal:
            n += 1
        spent += n * each
        at.append(left[:n])
        left = left[n:]
    return at


def plan():
    ph, prev = {}, None
    for name, args in (
        ("c", (4,)), ("q", (8,)), ("k", (4,)), ("v", (4,)), ("g", (1,)), ("merge", (32,)),
        ("sv", (8,)), ("su", (8,)), ("ab", (16, 4, 2, 2)), ("wo", (16,)), ("mk", (4,)), ("mv", (4,)),
        ("mq", (4,)), ("mo", (4, 4, 4, 4)),
    ):
        prev = ph[name] = Phase(prev, *args)
    for c, nk in enumerate(FFN_CHUNKS):
        prev = ph[f"f{c}"] = Phase(prev, 2 * nk)
        prev = ph[f"o{c}"] = Phase(prev, DK, nk // 4)
    return ph


def build(nc, x, mem, norm_mix_g, w_in, cmp_pe_k, cmp_k_w1, cmp_k_b1, cmp_k_w2, cmp_pe_v, cmp_v_w1,
          cmp_v_b1, cmp_v_w2, sgu_ln_g, sgu_ln_b, sgu_ws, sgu_b, w_proj_a, w_proj_b, w_mix_out,
          norm_cross_g, norm_mem_g, w_mq, w_mkv, w_mo, norm_ffn_g, w_ffn_in, w_ffn_out,
          norm_final_g, out):
    PH = plan()
    ds = bass.ds
    with ExitStack() as ctx:
        def sem(name):
            return ctx.enter_context(nc.semaphore(name))

        base = (nc.sbuf_base + 63) // 64 * 64
        A = base + 32 * KIB
        B = A + 64 * KIB
        B2 = B + 32 * KIB
        C = B + 64 * KIB
        K = C + 40 * KIB

        def at(name, shape, dt, offset):
            return nc.alloc_sbuf_tensor_at(name, shape, dt, offset=offset)

        raw = at("raw", [P, 2, 16, P], F32, base)
        w_hi = at("w_hi", [P, 4, 4, P], F32R, base + 16 * KIB)
        w_lo = at("w_lo", [P, 4, 4, P], F32R, base + 24 * KIB)

        act_hi = at("act_hi", [P, DK, T], F32R, A)
        act_lo = at("act_lo", [P, DK, T], F32R, A + 32 * KIB)

        x_rows = at("x_rows", [P, TC, D], F32, B)
        junk = at("junk", [P, 2, D], F32, B2)
        small_rows = at("small_rows", [116, P], F32, C)
        kv_src = at("kv_src", [P, 2, GROUPS, T], F32, B2)
        blocks = [at(f"blocks_{s}", [P, 16, GROUPS, NCMP], F32, B2 + (16 + 8 * s) * KIB) for s in range(2)]
        w1 = [at(f"w1_{s}", [P, 16, CMP_HID], F32, B + 16 * KIB * s) for s in range(2)]
        hid_t = [at(f"hid_t_{s}", [P, 2, GROUPS * NCMP], F32, C + (16 + s) * KIB) for s in range(2)]
        w2 = at("w2", [P, 2, 2, HD], F32, C + 18 * KIB)
        vt = at("vt", [P, 2, T], F32, B2)
        gate_t = at("gate_t", [48, T], F32, B2 + 4 * KIB)
        q_t = at("q_t", [P, 8, T], F32, C)
        v_kv = at("v_kv", [P, 2, TC, 256], F32, C + 16 * KIB)
        k_t = at("k_t", [HD, 2, GROUPS, T], F32, C + 24 * KIB)
        qs = at("qs", [HD, HPG, T], F32, B)
        prob = at("prob", [P, 3, T], F32, B + 8 * KIB)
        prob_t = at("prob_t", [P, 3, TC, P], F32, B + 14 * KIB)
        gate_out = at("gate_out", [P, 2, T], F32, B + 20 * KIB)
        o_parts = at("o_parts", [P, 2, 2, 3, HD], F32, B + 24 * KIB)
        o_rows = at("o_rows", [P, 2, P], F32, B + 27 * KIB)
        oa_hi = at("oa_hi", [P, 8, T], F32R, B2)
        oa_lo = at("oa_lo", [P, 8, T], F32R, B2 + 16 * KIB)
        ws_rows = at("ws_rows", [P, SG, P], F32, B)
        ob_hi = at("ob_hi", [P, SG, T], F32R, B)
        ob_lo = at("ob_lo", [P, SG, T], F32R, B + 16 * KIB)
        v_rows = at("v_rows", [P, TC, 1024], F32, C)
        sv_t = at("sv_t", [P, 2, T], F32, C + 16 * KIB)
        ut = at("ut", [P, 2, T], F32, C + 16 * KIB)
        vz = at("vz", [P, 2, TC, P], F32, C + 20 * KIB)
        vn = at("vn", [P, 2, TC, P], F32, C + 24 * KIB)
        mixed = at("mixed", [P, TC, P], F32, C + 28 * KIB)
        ob = at("ob", [P, T], F32, C + 30 * KIB)
        ws_t = at("ws_t", [P, SG, P], F32, C + 32 * KIB)
        rows_bc = at("rows_bc", [P, 2, 3, P], F32, C + 36 * KIB)
        gate_in = at("gate_in", [P, 2, 2, T], F32, C)
        pa = at("pa", [P, 2, T], F32, C + 8 * KIB)
        pb = at("pb", [P, 2, T], F32, C + 12 * KIB)
        merged = at("merged", [P, 2, T], F32, C + 16 * KIB)
        mem_rows = at("mem_rows", [P, MC, D], F32, C + 20 * KIB)
        x_cols = at("x_cols", [P, 2, TC, P], F32, C + 36 * KIB)
        mem_cols = at("mem_cols", [P, 2, MC, P], F32, C + 8 * KIB)
        xt = at("xt", [P, DK, T], F32, B)
        sq = at("sq", [P, 2, T], F32, C)
        sumsq = at("sumsq", [P, T], F32, C + 4 * KIB)
        rms_bc = at("rms_bc", [P, T], F32, C + 6 * KIB)
        xg = at("xg", [P, 2, T], F32, C + 8 * KIB)
        hm_hi = at("hm_hi", [P, DK, MEM], F32R, B2)
        hm_lo = at("hm_lo", [P, DK, MEM], F32R, B2 + 16 * KIB)
        mq_t = at("mq_t", [P, MH, T], F32, C + 12 * KIB)
        mk_t = at("mk_t", [P, MH, MEM], F32, C + 20 * KIB)
        mv_rows = at("mv_rows", [P, MC, 512], F32, C + 24 * KIB)
        mv_t = at("mv_t", [P, 2, MEM], F32, C + 28 * KIB)
        add_in = at("add_in", [P, 2, T], F32, C + 32 * KIB)
        mo_hi = at("mo_hi", [P, MH, T], F32R, B2)
        mo_lo = at("mo_lo", [P, MH, T], F32R, B2 + 8 * KIB)
        mem_junk = at("mem_junk", [P, D], F32, A + 48 * KIB)
        m_prob = at("m_prob", [P, 3, MEM], F32, B2 + 16 * KIB)
        m_prob_n = at("m_prob_n", [P, 3, MEM], F32, B2 + 20 * KIB)
        m_prob_t = at("m_prob_t", [P, 3, MC, P], F32, B2 + 24 * KIB)
        ff_hi = at("ff_hi", [P, 16, T], F32R, B2)
        ff_lo = at("ff_lo", [P, 16, T], F32R, C)
        gated = at("gated", [P, T], F32, C + 32 * KIB)
        up = at("up", [P, T], F32, C + 34 * KIB)
        ff = at("ff", [P, T], F32, C + 36 * KIB)
        sumsq_f = at("sumsq_f", [P, T], F32, C + 38 * KIB)
        y_rows = at("y_rows", [P, TC, D], F32, A)
        final_g_bc = at("final_g_bc", [P, D], F32, A + 32 * KIB)
        x_out = at("x_out", [P, 2, T], F32, A + 40 * KIB)

        spot = [K]

        def const(name, shape, dt=F32):
            size = mybir.dt.size(dt)
            for n in shape[1:]:
                size *= n
            t = at(name, shape, dt, spot[0])
            spot[0] += (size + 31) // 32 * 32
            return t

        ident = const("ident", [P, P])
        ones = const("ones", [P, P])
        ident_b = const("ident_b", [P, P], BF16)
        causal_b = const("causal_b", [P, P], BF16)
        cmp_mask_b = const("cmp_mask_b", [P, TC, NCMP], BF16)
        valid = const("valid", [P, 1])
        eps = const("eps", [P, 1])
        cols = const("cols", [P, 116])
        ss = const("ss", [P, TC])
        rstd = const("rstd", [P, TC])
        bn = const("bn", [P, TC, 2, 6])
        mv_stat = const("mv_stat", [P, TC, 2])
        ln_rstd = const("ln_rstd", [P, TC])
        ln_shift = const("ln_shift", [P, TC])
        gates = const("gates", [P, TC, 48])
        kc_t = const("kc_t", [HD, GROUPS * NCMP])
        vc = const("vc", [NCMP, GROUPS, HD])
        vcg = const("vcg", [NCMP, HD])
        ffn_rms_bc = const("ffn_rms_bc", [P, T])
        neg_max = const("neg_max", [P, 4])
        den = const("den", [P, 2, 6])
        coef = const("coef", [P, 2, 6])
        assert spot[0] <= nc.sbuf_usable_end, spot[0]
        G_MIX, G_CROSS, G_MEM, G_FFN, G_FINAL, PE_K, PE_V, B1_K, B1_V = 0, 16, 32, 48, 64, 80, 96, 112, 114

        bank = [ctx.enter_context(nc.psum_tensor(f"bank{b}", [P, T], F32)) for b in range(8)]
        merge_dram = nc.dram_tensor("merge_gates", [2 * DK * P, T], F32, kind="Internal").ap()

        raw_landed = [sem("raw_landed0"), sem("raw_landed1")]
        hi_done = sem("hi_done")
        split_done = sem("split_done")
        quarters_done = sem("quarters_done")
        banks_read = sem("banks_read")
        ones_made = sem("ones_made")
        ident_zero = sem("ident_zero")
        ident_made = sem("ident_made")
        masks_zero = sem("masks_zero")
        masks_made = sem("masks_made")
        x_landed = [sem(f"x_landed{c}") for c in range(TC)]
        small_landed = sem("small_landed")
        sgu_landed = sem("sgu_landed")
        sq_done = sem("sq_done")
        sq_dve = sem("sq_dve")
        rms_done = sem("rms_done")
        rstd_done = sem("rstd_done")
        x_scaled = sem("x_scaled")
        turned = sem("turned")
        turned_hi = sem("turned_hi")
        turned_lo = sem("turned_lo")
        cols_turned = sem("cols_turned")
        cols_ready = sem("cols_ready")
        ws_masked = sem("ws_masked")
        ws_turned = sem("ws_turned")
        ws_ready = sem("ws_ready")
        gate_stored = [sem("gate_stored0"), sem("gate_stored1")]
        v_turned = sem("v_turned")
        v_rows_done = sem("v_rows_done")
        ln_stats = sem("ln_stats")
        ln_sqrt = sem("ln_sqrt")
        ln_ready = sem("ln_ready")
        vz_done = sem("vz_done")
        vn_step = sem("vn_step")
        vn_done = sem("vn_done")
        mix_done = sem("mix_done")
        mix_copied = sem("mix_copied")
        ob_step = sem("ob_step")
        ob_done = sem("ob_done")
        ob_hi_done = sem("ob_hi_done")
        ob_lo_done = sem("ob_lo_done")
        kv_turned = sem("kv_turned")
        kv_rows_done = sem("kv_rows_done")
        gates_done = sem("gates_done")
        gates_masked = sem("gates_masked")
        w1_landed = sem("w1_landed")
        blocks_done = sem("blocks_done")
        hid_done = sem("hid_done")
        hid_act = sem("hid_act")
        cmp_out = sem("cmp_out")
        cmp_ready = sem("cmp_ready")
        staged = sem("staged")
        rows_landed = [sem("rows_landed0"), sem("rows_landed1")]
        ws_landed = sem("ws_landed")
        mem_cols_done = sem("mem_cols_done")
        gates_open = sem("gates_open")
        final_g_landed = sem("final_g_landed")
        sumsq_zero = sem("sumsq_zero")
        qk_done = sem("qk_done")
        max_done = sem("max_done")
        exp_done = sem("exp_done")
        pt_done = sem("pt_done")
        pt_copied = sem("pt_copied")
        pv_done = sem("pv_done")
        coef_step = sem("coef_step")
        o_scaled = sem("o_scaled")
        o_summed = sem("o_summed")
        o_turned = sem("o_turned")
        oa_hi_done = sem("oa_hi_done")
        oa_lo_done = sem("oa_lo_done")
        gates_landed = [sem("gates_landed0"), sem("gates_landed1")]
        merge_step = sem("merge_step")
        merge_done = sem("merge_done")
        merge_hi_done = sem("merge_hi_done")
        merge_lo_done = sem("merge_lo_done")
        mem_landed = sem("mem_landed")
        mem_sq = sem("mem_sq")
        mem_rms = sem("mem_rms")
        mem_rstd = sem("mem_rstd")
        mem_turned = sem("mem_turned")
        mem_hi = sem("mem_hi")
        mem_lo = sem("mem_lo")
        xcol_landed = [sem("xcol_landed0"), sem("xcol_landed1")]
        squared = sem("squared")
        summed = sem("summed")
        norm_sum = sem("norm_sum")
        norm_root = sem("norm_root")
        norm_inv = sem("norm_inv")
        xg_done = sem("xg_done")
        xg_hi = sem("xg_hi")
        xg_lo = sem("xg_lo")
        mvt_turned = sem("mvt_turned")
        mv_ready = sem("mv_ready")
        m_qk = sem("m_qk")
        m_max = sem("m_max")
        m_exp = sem("m_exp")
        m_inv = sem("m_inv")
        m_norm = sem("m_norm")
        m_pt = sem("m_pt")
        m_ptc = sem("m_ptc")
        m_pv = sem("m_pv")
        mo_hi_done = sem("mo_hi_done")
        mo_lo_done = sem("mo_lo_done")
        copied = sem("copied")
        added = sem("added")
        gate_scaled = sem("gate_scaled")
        gate_silu = sem("gate_silu")
        ff_done = sem("ff_done")
        ff_hi_done = sem("ff_hi_done")
        ff_lo_done = sem("ff_lo_done")
        y_done = sem("y_done")
        y_turned = sem("y_turned")
        y_copied = sem("y_copied")
        stored = sem("stored")

        block = ctx.enter_context(nc.Block())

        def wait(eng, s, value):
            if not isinstance(value, int) or value > 0:
                eng.wait_ge(s, value)

        def runs(eng, n, body, peel=False):
            if peel:
                body(0)
            if n - peel > 0:
                with eng.Fori(1 if peel else 0, n) as i:
                    body(i)

        items = [(pr, qi, e, b) for pr in range(2) for qi in range(TC) for e in range(2) for b in (1, 2, 0)]
        ITEMS = len(items)
        UNITS = ITEMS // 6
        T_LAG, PV_LAG = 2, 4
        SUM_LAG, OT_LAG = PV_LAG + 6, PV_LAG + 8
        STEPS = ITEMS - 6 + OT_LAG + 2
        GATE_TILES = 8 * DK
        HEAD_START = 3 * 3 * T
        TILES_AT = spread(GATE_TILES, [step_cost(items, step, T_LAG, PV_LAG) - (0 if step else HEAD_START) for step in range(STEPS)])
        QUARTERS_AT = [[k // 4 for k in tiles if k % 4 == 3] for tiles in TILES_AT]
        AHEAD = 3
        M_ITEMS, M_LAG = MH * TC, 4
        M_T_LAG, M_PV_LAG = M_LAG + 2, M_LAG + 3
        M_STEPS = M_ITEMS + M_PV_LAG + 1
        NORMED_AT = (0, 0, 2, 2, 2, 2, 2, 2)

        w_in_v = w_in[0].rearrange("(k p) n -> p k n", p=P)
        wa_v = w_proj_a[0].rearrange("(k p) n -> p k n", p=P)
        wb_v = w_proj_b[0].rearrange("(k p) n -> p k n", p=P)
        wo_v = w_mix_out[0].rearrange("(k p) n -> p k n", p=P)
        mq_v = w_mq[0].rearrange("(k p) n -> p k n", p=P)
        mkv_v = w_mkv[0].rearrange("(k p) n -> p k n", p=P)
        mo_v = w_mo[0].rearrange("(k p) n -> p k n", p=P)
        fi_v = w_ffn_in[0].rearrange("(k p) n -> p k n", p=P)
        fo_v = w_ffn_out[0].rearrange("(k p) n -> p k n", p=P)
        x_v = x[0].rearrange("(c p) n -> p c n", p=P)
        out_v = out[0].rearrange("(c p) n -> p c n", p=P)

        @block.sync
        def _(sp):
            def panel(ph, i, u, parts):
                s = ph.slot(u)
                wait(sp, split_done, ph.quarter(i, u) - ph.nq)
                for k0, k1, src in parts:
                    sp.dma_start(raw[:, s, k0:k1, 0:src.shape[2]], src).then_inc(raw_landed[s], 16)

            def columns(ph, view, col, width=P, step=2 * P, apart=P, n=None, peel=False):
                def body(i):
                    for u in range(min(2, ph.n)):
                        panel(ph, i, u, [(0, 16, view[:, :, ds(i * step + u * apart + col, width)])])
                runs(sp, n or ph.n // 2, body, peel)

            for c in range(0, TC, 2):
                sp.dma_start(x_rows[:, c], x_v[:, c]).then_inc(x_landed[c], 16)
            columns(PH["c"], w_in_v, C_KV, peel=True)
            sp.wait_ge(turned, DK)
            for s, w in enumerate((cmp_k_w1, cmp_v_w1)):
                sp.dma_start(w1[s][:], w[0].rearrange("(k p) n -> p k n", p=P)).then_inc(w1_landed, 16)
            columns(PH["q"], w_in_v, C_Q)
            columns(PH["k"], w_in_v, C_KV + 2 * 256, step=2 * 256)
            columns(PH["v"], w_in_v, C_KV + 3 * 256, step=2 * 256)
            panel(PH["g"], 0, 0, [(0, 16, w_in_v[:, :, C_NSA_GATE:C_NSA_GATE + 48])])
            columns(PH["merge"], w_in_v, C_MERGE)
            columns(PH["sv"], w_in_v, C_V)
            columns(PH["su"], w_in_v, C_U)

            ph = PH["ab"]
            def ab(i):
                for u in range(2):
                    n = i * 2 + u
                    panel(ph, i, u, [(0, 8, wa_v[:, :, ds(n * P, P)]), (8, 16, wb_v[:, :, ds(n * P, P)])])
                if isinstance(i, int):
                    sp.wait_ge(ob_lo_done, SG)
                    for b in range(2):
                        sp.wait_ge(gate_stored[b], 16 * DK)
                for u in range(2):
                    n = i * 2 + u
                    wait(sp, merge_done, n - 1)
                    for b in range(2):
                        sp.dma_start(gate_in[:, u, b], merge_dram[ds(i * 2 * P + u * P + b * DK * P, P), :]).then_inc(gates_landed[u], 16)
                if isinstance(i, int):
                    sp.dma_start(mem_rows[:], mem[0].rearrange("(c p) n -> p c n", p=P)).then_inc(mem_landed, 16)
            runs(sp, ph.n // 2, ab, peel=True)

            ph = PH["wo"]
            def wo(i):
                for u in range(2):
                    n = i * 2 + u
                    panel(ph, i, u, [(0, 16, wo_v[:, :, ds(n * P, P)])])
                    wait(sp, quarters_done, ph.quarter(i, u) - ph.nq)
                    sp.dma_start(x_cols[:, u], x_v[:, :, ds(n * P, P)]).then_inc(xcol_landed[u], 16)
            runs(sp, ph.n // 2, wo, peel=True)
            columns(PH["mk"], mkv_v, 0)
            columns(PH["mv"], mkv_v, 512)
            columns(PH["mq"], mq_v, 0)
            ph = PH["mo"]
            def mo(i):
                for u in range(2):
                    panel(ph, i, u, [(4 * j, 4 * j + 4, mo_v[:, :, ds((i * 2 + u) * 512 + j * P, P)]) for j in range(4)])
            runs(sp, ph.n // 2, mo)
            t0 = 0
            for c, nk in enumerate(FFN_CHUNKS):
                columns(PH[f"f{c}"], fi_v, t0 * P, step=P, apart=FF)
                ph = PH[f"o{c}"]
                def fo(i, ph=ph, t0=t0, nk=nk):
                    for u in range(2):
                        panel(ph, i, u, [(0, nk, fo_v[:, t0:t0 + nk, ds((i * 2 + u) * P, P)])])
                runs(sp, ph.n // 2, fo)
                t0 += nk
            for c in range(TC):
                sp.wait_ge(y_done, c + 1)
                sp.dma_start(out_v[:, c], y_rows[:, c]).then_inc(stored, 16)
            sp.wait_ge(stored, 16 * TC)

        @block.tensor
        def _(pe):
            def products(q, j, dst, hi, lo, first, last, m=P):
                pe.matmul(dst, w_hi[:, q, j, 0:m], hi, start=first, stop=False)
                pe.matmul(dst, w_hi[:, q, j, 0:m], lo, start=False, stop=False)
                return pe.matmul(dst, w_lo[:, q, j, 0:m], hi, start=False, stop=last)

            def quarter(ph, i, u, q, dst, hi, lo, first, last, k0, m=P):
                pe.wait_ge(split_done, ph.quarter(i, u) + q + 1)
                for j in range(4):
                    k = k0 + j
                    mm = products(q, j, dst, hi(k), lo(k), first and j == 0, last and j == 3, m)
                mm.then_inc(quarters_done, 1)

            def acts(k):
                return act_hi[:, k], act_lo[:, k]

            def group(ph, i, u, hi, lo, n=T, m=P, extra=None, ready=None):
                g = ph.group(i, u)
                b = (ph.group0 + u) % 2
                wait(pe, banks_read, g - 1)
                dst = bank[b][0:m, 0:n]
                for q in range(ph.nq):
                    if extra and q == ph.nq - 1:
                        extra(dst)
                    if ready:
                        pe.wait_ge(ready[0], ready[1] + 4 * q + 4)
                    quarter(ph, i, u, q, dst, hi, lo, q == 0, q == ph.nq - 1, 4 * q, m)

            hi16, lo16 = (lambda k: act_hi[:, k]), (lambda k: act_lo[:, k])

            pe.wait_ge(small_landed, 16 * 9)
            pe.wait_ge(ident_made, 2)
            pe.transpose(bank[0][:, 0:116], small_rows[:], ident[0:116, 0:116]).then_inc(cols_turned, 1)
            for k in range(DK):
                if k == 0:
                    pe.wait_ge(x_scaled, TC)
                wait(pe, turned_lo, k - 3)
                for c in range(TC):
                    mm = pe.transpose(bank[4 + k % 4][:, c * P:(c + 1) * P], x_rows[:, c, k * P:(k + 1) * P], ident[:])
                mm.then_inc(turned, 1)
            pe.wait_ge(cols_ready, 1)

            def plain(i):
                for u in range(2):
                    group(ph, i, u, hi16, lo16)
            ph = PH["c"]
            def first(i):
                for u in range(2):
                    group(ph, i, u, hi16, lo16, ready=(turned_lo, 0) if isinstance(i, int) and u == 0 else None)
            runs(pe, ph.n // 2, first, peel=True)
            ph = PH["q"]
            runs(pe, ph.n // 2, plain)

            pe.wait_ge(w1_landed, 32)
            for s in range(2):
                pe.wait_ge(blocks_done, s + 1)
                for hh in range(2):
                    for k in range(16):
                        mm = pe.matmul(bank[4 + 2 * s + hh][:, 0:GROUPS * NCMP], w1[s][:, k, hh * P:(hh + 1) * P],
                                       blocks[s][:, k].rearrange("p g n -> p (g n)"), start=k == 0, stop=k == 15)
                    mm.then_inc(hid_done, 1)
            ph = PH["k"]
            runs(pe, ph.n // 2, plain)
            pe.wait_ge(sgu_landed, 16 * 2)
            pe.wait_ge(hid_act, 2)
            for hh in range(2):
                mm = pe.matmul(bank[2][0:HD, 0:GROUPS * NCMP], w2[:, 0, hh], hid_t[0][:, hh], start=hh == 0, stop=hh == 1)
            mm.then_inc(cmp_out, 1)
            pe.wait_ge(hid_act, 4)
            for g in range(GROUPS):
                for hh in range(2):
                    mm = pe.matmul(bank[3][0:NCMP, g * HD:(g + 1) * HD], hid_t[1][:, hh, g * NCMP:(g + 1) * NCMP],
                                   w2[:, 1, hh], start=hh == 0, stop=hh == 1)
            mm.then_inc(cmp_out, 1)

            ph = PH["v"]
            pe.wait_ge(cmp_ready, 2)
            def kv_values(i):
                for u in range(2):
                    n = i * 2 + u
                    group(ph, i, u, hi16, lo16)
                    if not (isinstance(i, int) and n == 0):
                        turn_values(n - 1, 1 - u)
            def turn_values(n, u):
                pe.wait_ge(banks_read, PH["v"].group0 + n + 1)
                wait(pe, kv_rows_done, n - 1)
                for c in range(TC):
                    mm = pe.transpose(bank[2 + u][:, c * P:(c + 1) * P], vt[:, u, c * P:(c + 1) * P], ident[:])
                mm.then_inc(kv_turned, 1)
            runs(pe, ph.n // 2, kv_values, peel=True)
            ph = PH["g"]
            group(ph, 0, 0, hi16, lo16, m=48)
            turn_values(3, 1)
            pe.wait_ge(banks_read, ph.groups_end())
            pe.wait_ge(kv_rows_done, 4)
            for c in range(TC):
                mm = pe.transpose(bank[2][:, c * 48:(c + 1) * 48], gate_t[:, c * P:(c + 1) * P], ident[0:48, 0:48])
            mm.then_inc(kv_turned, 1)

            pe.wait_ge(gates_done, 1)
            ph = PH["merge"]
            def attention(j):
                n0 = j * ITEMS
                def gate_tiles(tiles):
                    for k in tiles:
                        p, t = divmod(k, DK)
                        if t == 0:
                            pe.wait_ge(banks_read, j * 8 + ph.group0 + p - 1)
                        if t % 4 == 0:
                            pe.wait_ge(split_done, ph.quarter(j * 4, p) + t // 4 + 1)
                        mm = products(t // 4, t % 4, bank[(ph.group0 + p) % 2][:], act_hi[:, t], act_lo[:, t], t == 0, t == DK - 1)
                        if t % 4 == 3:
                            mm.then_inc(quarters_done, 1)
                for step in range(STEPS):
                    tiles = TILES_AT[step]
                    third = (len(tiles) + 2) // 3 if step else len(tiles)
                    gate_tiles(tiles[:third])
                    if step < ITEMS:
                        pr, qi, e, b = items[step]
                        if step == 0:
                            pe.wait_ge(staged, j * (HPG + 1) + 3)
                        if step == ITEMS // 2:
                            pe.wait_ge(staged, j * (HPG + 1) + 5)
                        if step >= 2:
                            pe.wait_ge(exp_done, n0 + step - 1)
                        s = bank[2 + step % 2]
                        q = qs[:, 2 * pr + e, qi * P:(qi + 1) * P]
                        if b == 0:
                            pe.matmul(s[:, 0:NCMP], ident_b[:], cmp_mask_b[:, qi], start=True, stop=False)
                            pe.matmul(s[:, 0:NCMP], q, kc_t[:, ds(j * NCMP, NCMP)], start=False, stop=True).then_inc(qk_done, 1)
                        else:
                            here = slice(qi * P, (qi + 1) * P)
                            pe.matmul(s[:, here], ident_b[:], causal_b[:], start=True, stop=False)
                            mm = pe.matmul(s[:, here], q, k_t[:, b - 1, ds(j, 1), here], start=False, stop=True)
                            if qi > 0:
                                mm = pe.matmul(s[:, 0:qi * P], q, k_t[:, b - 1, ds(j, 1), 0:qi * P], start=True, stop=True)
                            mm.then_inc(qk_done, 1)
                    gate_tiles(tiles[third:2 * third])
                    if 0 <= step - T_LAG < ITEMS:
                        t = step - T_LAG
                        pr, qi, e, b = items[t]
                        pe.wait_ge(exp_done, n0 + t + 1)
                        if t >= 2:
                            pe.wait_ge(pt_copied, n0 + t - 1)
                        tb = bank[4 + t % 2]
                        if b == 0:
                            mm = pe.transpose(tb[0:NCMP, 0:P], prob[:, t % 3, 0:NCMP], ident[:])
                        else:
                            for kj in range(qi + 1):
                                mm = pe.transpose(tb[:, kj * P:(kj + 1) * P], prob[:, t % 3, kj * P:(kj + 1) * P], ident[:])
                        mm.then_inc(pt_done, 1)
                    gate_tiles(tiles[2 * third:])
                    if 0 <= step - PV_LAG < ITEMS:
                        t = step - PV_LAG
                        pr, qi, e, b = items[t]
                        unit = t // 6
                        pe.wait_ge(pt_copied, n0 + t + 1)
                        if t % 6 == 0 and unit >= 2:
                            pe.wait_ge(o_scaled, j * UNITS + unit - 1)
                        o = bank[6 + unit % 2][:, (e * 3 + b) * HD:(e * 3 + b + 1) * HD]
                        if b == 0:
                            mm = pe.matmul(o, prob_t[0:NCMP, t % 3, 0], vcg[:], start=True, stop=True)
                        else:
                            for kj in range(qi + 1):
                                mm = pe.matmul(o, prob_t[:, t % 3, kj], v_kv[:, b - 1, kj, ds(j * HD, HD)], start=kj == 0, stop=kj == qi)
                        mm.then_inc(pv_done, 1)
                    if step >= OT_LAG and (step - OT_LAG) % 6 == 0:
                        unit = (step - OT_LAG) // 6
                        qi = unit % TC
                        pe.wait_ge(o_summed, j * UNITS + unit + 1)
                        if unit >= 2:
                            pe.wait_ge(oa_lo_done, j * UNITS + unit - 1)
                        pe.transpose(bank[6 + unit % 2][:, 6 * HD:6 * HD + P], o_rows[:, unit % 2], ident[:]).then_inc(o_turned, 1)
            runs(pe, GROUPS, attention)

            ph = PH["sv"]
            def turn_v(n, u):
                pe.wait_ge(banks_read, ph.group0 + n + 1)
                wait(pe, v_rows_done, n - 1)
                for c in range(TC):
                    mm = pe.transpose(bank[2 + u][:, c * P:(c + 1) * P], sv_t[:, u, c * P:(c + 1) * P], ident[:])
                mm.then_inc(v_turned, 1)
            def sgu_v(i):
                for u in range(2):
                    group(ph, i, u, hi16, lo16)
                    if not (isinstance(i, int) and i == 0 and u == 0):
                        turn_v(i * 2 + u - 1, 1 - u)
            sgu_v(0)
            pe.wait_ge(ws_masked, 1)
            for g in range(SG):
                mm = pe.transpose(bank[4 + g // 4][:, (g % 4) * P:(g % 4 + 1) * P], ws_rows[:, g], ident[:])
            mm.then_inc(ws_turned, 1)
            with pe.Fori(1, ph.n // 2) as i:
                sgu_v(i)
            turn_v(ph.n - 1, 1)

            ph = PH["su"]
            pe.wait_ge(ws_ready, 2)
            def mix(n, u):
                pe.wait_ge(vn_done, n + 1)
                wait(pe, mix_copied, n - 1)
                if isinstance(n, int) and n < 2:
                    pe.wait_ge(v_rows_done, SG)
                for c in range(TC):
                    mm = pe.matmul(bank[2 + u][:, c * P:(c + 1) * P], vn[:, u, c], ws_t[:, ds(n, 1), :],
                                   start=True, stop=True)
                mm.then_inc(mix_done, 1)
            def sgu_u(i):
                for u in range(2):
                    group(ph, i, u, hi16, lo16)
                    if not (isinstance(i, int) and i == 0 and u == 0):
                        mix(i * 2 + u - 1, 1 - u)
            runs(pe, ph.n // 2, sgu_u, peel=True)
            mix(ph.n - 1, 1)

            pe.wait_ge(oa_lo_done, GROUPS * UNITS)
            ph = PH["ab"]
            def ab(i):
                for u in range(2):
                    for a, (h, l) in enumerate(((oa_hi, oa_lo), (ob_hi, ob_lo))):
                        wait(pe, banks_read, ph.group(i, u) + a - 1)
                        dst = bank[(ph.group0 + a) % 2][:]
                        for q in range(2):
                            if isinstance(i, int) and u == 0 and a == 1:
                                pe.wait_ge(ob_lo_done, 4 * q + 4)
                            quarter(ph, i, u, 2 * a + q, dst, lambda k: h[:, k], lambda k: l[:, k], q == 0, q == 1, 4 * q)
            runs(pe, ph.n // 2, ab, peel=True)

            ph = PH["wo"]
            def wo(i):
                for u in range(2):
                    def residual(dst):
                        pe.wait_ge(xcol_landed[u], i * 16 + 16)
                        for c in range(TC):
                            pe.matmul(dst[:, c * P:(c + 1) * P], x_cols[:, u, c], ident[:], start=False, stop=False)
                    group(ph, i, u, hi16, lo16, extra=residual,
                          ready=(merge_lo_done, 0) if isinstance(i, int) and u == 0 else None)
                    n = i * 2 + u
                    pe.wait_ge(mem_cols_done, n + 1)
                    wait(pe, mem_lo, n - 1)
                    for c in range(MC):
                        mm = pe.transpose(bank[2 + u][:, c * P:(c + 1) * P], mem_cols[:, u, c], ident[:])
                    mm.then_inc(mem_turned, 1)
            runs(pe, ph.n // 2, wo, peel=True)

            def norm_total(src, tiles):
                pe.wait_ge(summed, tiles)
                pe.matmul(bank[4][:], ones[:], src[:], start=True, stop=True).then_inc(norm_sum, 1)

            pe.wait_ge(mem_lo, DK)
            hm_h, hm_l = (lambda k: hm_hi[:, k]), (lambda k: hm_lo[:, k])
            ph = PH["mk"]
            def mem_keys(i):
                for u in range(2):
                    group(ph, i, u, hm_h, hm_l, n=MEM)
            group(ph, 0, 0, hm_h, hm_l, n=MEM)
            norm_total(sumsq, DK)
            group(ph, 0, 1, hm_h, hm_l, n=MEM)
            mem_keys(1)
            ph = PH["mv"]
            def mem_values(i):
                for u in range(2):
                    group(ph, i, u, hm_h, hm_l, n=MEM)
                    pe.wait_ge(banks_read, ph.group(i, u) + 1)
                    wait(pe, mv_ready, i * 2 + u - 1)
                    for c in range(MC):
                        mm = pe.transpose(bank[2 + u][:, c * P:(c + 1) * P], mv_t[:, u, c * P:(c + 1) * P], ident[:])
                    mm.then_inc(mvt_turned, 1)
            runs(pe, ph.n // 2, mem_values, peel=True)
            ph = PH["mq"]
            for step in range(M_STEPS):
                if step < 16:
                    h, q = divmod(step, 4)
                    i, u = ph.at(h)
                    if q == 0:
                        pe.wait_ge(banks_read, ph.group0 + h - 1)
                    if h == 0:
                        pe.wait_ge(xg_lo, 4 * q + 4)
                    quarter(ph, i, u, q, bank[(ph.group0 + h) % 2][:], hi16, lo16, q == 0, q == 3, 4 * q)
                t = step - M_LAG
                if 0 <= t < M_ITEMS:
                    h, qi = divmod(t, TC)
                    if qi == 0:
                        pe.wait_ge(banks_read, ph.group0 + h + 1)
                    wait(pe, m_exp, t - 1)
                    pe.matmul(bank[2 + t % 2][:, 0:MEM], mq_t[:, h, qi * P:(qi + 1) * P], mk_t[:, h], start=True, stop=True).then_inc(m_qk, 1)
                t = step - M_T_LAG
                if 0 <= t < M_ITEMS:
                    pe.wait_ge(m_norm, t + 1)
                    wait(pe, m_ptc, t - 1)
                    for c in range(MC):
                        mm = pe.transpose(bank[4 + t % 2][:, c * P:(c + 1) * P], m_prob_n[:, t % 3, c * P:(c + 1) * P], ident[:])
                    mm.then_inc(m_pt, 1)
                t = step - M_PV_LAG
                if 0 <= t < M_ITEMS:
                    h, qi = divmod(t, TC)
                    if t == 0:
                        pe.wait_ge(mv_ready, 4)
                    pe.wait_ge(m_ptc, t + 1)
                    if qi == 0:
                        wait(pe, mo_lo_done, h - 1)
                    for c in range(MC):
                        mm = pe.matmul(bank[6 + h % 2][:, qi * P:(qi + 1) * P], mv_rows[:, c, h * P:(h + 1) * P],
                                       m_prob_t[:, t % 3, c], start=c == 0, stop=c == MC - 1)
                    mm.then_inc(m_pv, 1)
            pe.wait_ge(mo_lo_done, MH)
            ph = PH["mo"]
            def mo(i):
                for u in range(2):
                    for j in range(4):
                        wait(pe, banks_read, ph.group(i, u) + j - 1)
                        quarter(ph, i, u, j, bank[(ph.group0 + j) % 2][:], lambda k: mo_hi[:, k], lambda k: mo_lo[:, k], True, True, 0)
            runs(pe, ph.n // 2, mo)

            def turn_out(n, u):
                pe.wait_ge(added, n + 3 * DK + 1)
                wait(pe, y_copied, n - 1)
                for t in range(TC):
                    mm = pe.transpose(bank[2 + u][:, t * P:(t + 1) * P], x_out[:, u, t * P:(t + 1) * P], ident[:])
                mm.then_inc(y_turned, 1)
            tiles = 0
            for c, nk in enumerate(FFN_CHUNKS):
                ph = PH[f"f{c}"]
                def fi(i):
                    for u in range(2):
                        group(ph, i, u, hi16, lo16, ready=(xg_lo, DK) if c == 0 and u == 0 and isinstance(i, int) else None)
                        if c == 0 and u == 0 and isinstance(i, int):
                            norm_total(sumsq, 2 * DK)
                runs(pe, ph.n // 2, fi, peel=c == 0)
                tiles += nk
                ph = PH[f"o{c}"]
                last = c == len(FFN_CHUNKS) - 1
                def fo(i):
                    for u in range(2):
                        group(ph, i, u, lambda k: ff_hi[:, k], lambda k: ff_lo[:, k],
                              ready=(ff_lo_done, tiles - nk) if isinstance(i, int) and u == 0 else None)
                        if last and not (isinstance(i, int) and i == 0 and u == 0):
                            turn_out(i * 2 + u - 1, 1 - u)
                runs(pe, ph.n // 2, fo, peel=True)
            turn_out(DK - 1, 1)
            pe.wait_ge(summed, 3 * DK)
            for c in range(TC):
                mm = pe.matmul(bank[4][:, c:c + 1], sumsq_f[:, c * P:(c + 1) * P], ones[:, 0:1], start=True, stop=True)
            mm.then_inc(norm_sum, 1)

        @block.vector
        def _(dve):
            def split(ph, i, u, width=P, quarters=None):
                s = ph.slot(u)
                for q in quarters or range(ph.nq):
                    if q == 0:
                        dve.wait_ge(raw_landed[s], ph.landed(i, u))
                    n = ph.quarter(i, u) + q
                    wait(dve, quarters_done, n - ph.nq + 1)
                    src = raw[:, s, 4 * q:4 * q + 4, 0:width]
                    dve.tensor_copy(w_hi[:, q, :, 0:width], src).then_inc(hi_done, 1)
                    dve.wait_ge(hi_done, n + 1)
                    dve.tensor_tensor(w_lo[:, q, :, 0:width], src, w_hi[:, q, :, 0:width].bitcast(F32), ALU.subtract).then_inc(split_done, 1)

            def split_all(ph, start=0, peel=False):
                def body(i):
                    for u in range(2):
                        split(ph, i, u)
                if start == 0:
                    runs(dve, ph.n // 2, body, peel)
                else:
                    with dve.Fori(start, ph.n // 2) as i:
                        body(i)

            dve.memset(ones[:], 1.0).then_inc(ones_made, 1)
            dve.memset(eps[:], EPS).then_inc(ones_made, 1)
            for c in range(TC // 2, TC):
                dve.wait_ge(x_landed[c], 16)
                wait(dve, sq_dve, c - TC // 2)
                dve.tensor_tensor_reduce(out=junk[:, 1], in0=x_rows[:, c], in1=x_rows[:, c], scale=1.0, scalar=0.0,
                                         op0=ALU.mult, op1=ALU.add, accum_out=ss[:, c:c + 1]).then_inc(sq_dve, 1)
            dve.wait_ge(rms_done, 1)
            dve.reciprocal(rstd[:], ss[:]).then_inc(rstd_done, 1)
            dve.wait_ge(rstd_done, 1)
            for c in range(TC // 2):
                dve.tensor_scalar(x_rows[:, c], x_rows[:, c], rstd[:, c:c + 1], None, ALU.mult).then_inc(x_scaled, 1)
            split(PH["c"], 0, 0, quarters=(0,))
            dve.wait_ge(cols_ready, 1)
            for k in range(DK):
                if k in (4, 8, 12):
                    split(PH["c"], 0, 0, quarters=(k // 4,))
                dve.wait_ge(turned_hi, k + 1)
                dve.scalar_tensor_tensor(out=act_lo[:, k], in0=bank[4 + k % 4][:], scalar=cols[:, G_MIX + k:G_MIX + k + 1],
                                         in1=act_hi[:, k].bitcast(F32), op0=ALU.mult, op1=ALU.subtract).then_inc(turned_lo, 1)
            ph = PH["c"]
            split(ph, 0, 1)
            split_all(ph, start=1)
            for name in ("q", "k", "v"):
                split_all(PH[name])
            split(PH["g"], 0, 0, width=48)
            ph = PH["merge"]
            split(ph, 0, 0, quarters=range(AHEAD))

            dve.wait_ge(gates_masked, 1)
            def attention(j):
                n0 = j * ITEMS
                for step in range(STEPS):
                    if step < ITEMS:
                        pr, qi, e, b = items[step]
                        n = NCMP if b == 0 else (qi + 1) * P
                        dve.wait_ge(qk_done, n0 + step + 1)
                        if step >= 4:
                            dve.wait_ge(exp_done, n0 + step - 3)
                        dve.tensor_reduce(neg_max[:, step % 4:step % 4 + 1], bank[2 + step % 2][:, 0:n], AX.X, ALU.max, negate=True).then_inc(max_done, 1)
                    if 0 <= step - T_LAG < ITEMS:
                        t = step - T_LAG
                        pr, qi, e, b = items[t]
                        dve.wait_ge(pt_done, n0 + t + 1)
                        if t >= 3:
                            dve.wait_ge(pv_done, n0 + t - 2)
                        if b == 0:
                            dve.tensor_copy(prob_t[0:NCMP, t % 3, 0], bank[4 + t % 2][0:NCMP, 0:P]).then_inc(pt_copied, 1)
                        else:
                            dve.tensor_copy(prob_t[:, t % 3, 0:qi + 1].rearrange("p k q -> p (k q)"),
                                            bank[4 + t % 2][:, 0:(qi + 1) * P]).then_inc(pt_copied, 1)
                    if step >= SUM_LAG and (step - SUM_LAG) % 6 == 0:
                        unit = (step - SUM_LAG) // 6
                        if unit < UNITS:
                            pr, qi = unit // TC, unit % TC
                            un = j * UNITS + unit
                            ub = unit % 2
                            dve.wait_ge(pv_done, n0 + 6 * unit + 6)
                            dve.reciprocal(coef[:, ub], den[:, ub]).then_inc(coef_step, 1)
                            dve.wait_ge(coef_step, un * 2 + 1)
                            dve.tensor_tensor(coef[:, ub], coef[:, ub], gates[:, qi, ds(j * 12 + 6 * pr, 6)], ALU.mult).then_inc(coef_step, 1)
                            dve.wait_ge(coef_step, un * 2 + 2)
                            dve.tensor_tensor(o_parts[:, ub].rearrange("p e b d -> p (e b) d"),
                                              bank[6 + ub][:, 0:6 * HD].rearrange("p (s d) -> p s d", d=HD),
                                              coef[:, ub].unsqueeze(2).broadcast_to([P, 6, HD]), ALU.mult).then_inc(o_scaled, 1)
                            dve.wait_ge(o_scaled, un + 1)
                            if unit >= 2:
                                dve.wait_ge(o_turned, un - 1)
                            dve.tensor_reduce(o_rows[:, ub].rearrange("p (e d) -> p e d", e=2), o_parts[:, ub].rearrange("p e b d -> p e d b"),
                                              AX.X, ALU.add).then_inc(o_summed, 1)
                    if step > OT_LAG and (step - OT_LAG - 1) % 6 == 0:
                        unit = (step - OT_LAG - 1) // 6
                        place = oa_lo[:, ds(j * 2 + unit // TC, 1), unit % TC * P:(unit % TC + 1) * P]
                        high = oa_hi[:, ds(j * 2 + unit // TC, 1), unit % TC * P:(unit % TC + 1) * P]
                        dve.wait_ge(oa_hi_done, j * UNITS + unit + 1)
                        dve.tensor_tensor(place, bank[6 + unit % 2][:, 6 * HD:6 * HD + P], high.bitcast(F32), ALU.subtract).then_inc(oa_lo_done, 1)
                    for k in QUARTERS_AT[step]:
                        k += AHEAD
                        split(ph, j * 4, k // 4, quarters=(k % 4,))
            runs(dve, GROUPS, attention)
            ph = PH["sv"]
            split(ph, 0, 0, quarters=range(AHEAD, 4))
            split(ph, 0, 1)
            split_all(ph, start=1)
            ph = PH["su"]
            split(ph, 0, 0)
            dve.wait_ge(v_rows_done, SG)
            for c in range(TC):
                for h in range(2):
                    dve.bn_stats(bn[:, c, h], v_rows[:, c, h * 512:(h + 1) * 512]).then_inc(ln_stats, 1)
            dve.wait_ge(ln_stats, 2 * TC)
            for c in range(TC):
                dve.bn_aggr(mv_stat[:, c], bn[:, c].rearrange("p a b -> p (a b)")).then_inc(ln_stats, 1)
            dve.wait_ge(ln_sqrt, 1)
            dve.reciprocal(ln_rstd[:], ln_shift[:]).then_inc(ln_ready, 1)
            dve.wait_ge(ln_ready, 1)
            dve.scalar_tensor_tensor(out=ln_shift[:], in0=mv_stat[:, :, 0], scalar=-1.0, in1=ln_rstd[:],
                                     op0=ALU.mult, op1=ALU.mult).then_inc(ln_ready, 1)
            split(ph, 0, 1)
            split_all(ph, start=1)
            split_all(PH["ab"])
            dve.wait_ge(mem_rms, 1)
            dve.reciprocal(rstd[:, 0:MC], rstd[:, 0:MC]).then_inc(mem_rstd, 1)
            ph = PH["wo"]
            def mem_low(n, u):
                dve.wait_ge(mem_hi, n + 1)
                dve.scalar_tensor_tensor(out=hm_lo[:, ds(n, 1), :], in0=bank[2 + u][:, 0:MEM],
                                         scalar=cols[:, ds(n + G_MEM, 1)], in1=hm_hi[:, ds(n, 1), :].bitcast(F32),
                                         op0=ALU.mult, op1=ALU.subtract).then_inc(mem_lo, 1)
            def wo(i):
                for u in range(2):
                    split(ph, i, u)
                    if not (isinstance(i, int) and i == 0 and u == 0):
                        mem_low(i * 2 + u - 1, 1 - u)
            runs(dve, ph.n // 2, wo, peel=True)

            def inverse(n, buf):
                dve.wait_ge(norm_root, n + 1)
                dve.reciprocal(buf[:], buf[:]).then_inc(norm_inv, 1)
                dve.wait_ge(norm_inv, n + 1)

            def normed(k, done, gain):
                wait(dve, xg_hi, done + k - 1)
                wait(dve, xg_lo, done + k - 1)
                dve.scalar_tensor_tensor(out=xg[:, k % 2], in0=xt[:, k], scalar=cols[:, gain + k:gain + k + 1],
                                         in1=rms_bc[:], op0=ALU.mult, op1=ALU.mult).then_inc(xg_done, 1)

            split(PH["mk"], 0, 0)
            mem_low(DK - 1, 1)
            split(PH["mk"], 0, 1)
            inverse(0, rms_bc)
            k = 0
            for n in range(2, 8):
                for _ in range(NORMED_AT[n]):
                    normed(k, 0, G_CROSS)
                    k += 1
                split(PH["mk" if n < 4 else "mv"], n % 4 // 2, n % 2)
            quarters = [(PH["mq"], p, q) for p in range(4) for q in range(4)] + [(PH["mo"], 0, q) for q in range(4)]
            def split_next():
                m, p, q = quarters.pop(0)
                split(m, *m.at(p), quarters=(q,))
            for _ in range(AHEAD):
                split_next()
            while k < DK:
                normed(k, 0, G_CROSS)
                k += 1
            for step in range(M_STEPS):
                t = step - M_LAG
                if 0 <= t < M_ITEMS:
                    dve.wait_ge(m_qk, t + 1)
                    wait(dve, m_exp, t - 3)
                    dve.tensor_reduce(neg_max[:, t % 4:t % 4 + 1], bank[2 + t % 2][:, 0:MEM], AX.X, ALU.max, negate=True).then_inc(m_max, 1)
                    dve.wait_ge(m_exp, t + 1)
                    dve.reciprocal(coef[:, 0, t % 3:t % 3 + 1], den[:, 0, t % 3:t % 3 + 1]).then_inc(m_inv, 1)
                    dve.wait_ge(m_inv, t + 1)
                    wait(dve, m_pt, t - 2)
                    dve.tensor_scalar(m_prob_n[:, t % 3], m_prob[:, t % 3], coef[:, 0, t % 3:t % 3 + 1], None, ALU.mult).then_inc(m_norm, 1)
                t = step - M_T_LAG
                if 0 <= t < M_ITEMS:
                    dve.wait_ge(m_pt, t + 1)
                    wait(dve, m_pv, t - 2)
                    dve.tensor_copy(m_prob_t[:, t % 3].rearrange("p c q -> p (c q)"), bank[4 + t % 2][:, 0:MEM]).then_inc(m_ptc, 1)
                t = step - M_PV_LAG - 1
                if t >= 0 and t % TC == TC - 1:
                    h = t // TC
                    dve.wait_ge(mo_hi_done, h + 1)
                    dve.tensor_tensor(mo_lo[:, h], bank[6 + h % 2][:], mo_hi[:, h].bitcast(F32), ALU.subtract).then_inc(mo_lo_done, 1)
                if quarters and step < 16 + 4 - AHEAD:
                    split_next()
            assert not quarters
            def gained_low(n):
                dve.wait_ge(xg_hi, DK + n + 1)
                dve.scalar_tensor_tensor(out=act_lo[:, ds(n, 1), :], in0=xt[:, ds(n, 1), :], scalar=cols[:, ds(n + G_FFN, 1)],
                                         in1=act_hi[:, ds(n, 1), :].bitcast(F32), op0=ALU.mult, op1=ALU.subtract).then_inc(xg_lo, 1)
            split(PH["mo"], 0, 1)
            def mo(i):
                for u in range(2):
                    for q in range(4):
                        split(PH["mo"], i, u, quarters=(q,))
                        gained_low((i * 2 + u - 2) * 4 + q)
            with dve.Fori(1, PH["mo"].n // 2) as i:
                mo(i)
            for u in range(2):
                for q in range(4):
                    if u == 1:
                        gained_low(DK - 4 + q)
                    split(PH["f0"], 0, u, quarters=(q,))
                    if u == 0:
                        gained_low(DK - 8 + q)
            inverse(1, ffn_rms_bc)
            split_all(PH["f0"], start=1)
            for name in ("o0", "f1", "o1", "f2", "o2"):
                split_all(PH[name])
            dve.wait_ge(norm_root, 3)
            dve.reciprocal(rstd[:], ss[:]).then_inc(rstd_done, 1)
            dve.wait_ge(rstd_done, 2)
            dve.wait_ge(final_g_landed, 16)
            dve.wait_ge(y_copied, DK)
            for c in range(TC):
                dve.scalar_tensor_tensor(out=y_rows[:, c], in0=y_rows[:, c], scalar=rstd[:, c:c + 1], in1=final_g_bc[:],
                                         op0=ALU.mult, op1=ALU.mult).then_inc(y_done, 1)

        @block.scalar
        def _(act):
            for c in range(1, TC, 2):
                act.dma_start(x_rows[:, c], x_v[:, c]).then_inc(x_landed[c], 16)
            row = 0
            for g in (norm_mix_g[0], norm_cross_g[0], norm_mem_g[0], norm_ffn_g[0], norm_final_g):
                act.dma_start(small_rows[row:row + 16], g.rearrange("(k p) -> k p", p=P)).then_inc(small_landed, 16)
                row += 16
            for g in (cmp_pe_k[0], cmp_pe_v[0]):
                act.dma_start(small_rows[row:row + 16], g.rearrange("(k a) d -> k (a d)", a=2)).then_inc(small_landed, 16)
                row += 16
            for g in (cmp_k_b1[0], cmp_v_b1[0]):
                act.dma_start(small_rows[row:row + 2], g.rearrange("(k p) -> k p", p=P)).then_inc(small_landed, 16)
                row += 2
            for s, w in enumerate((cmp_k_w2, cmp_v_w2)):
                act.dma_start(w2[:, s], w[0].rearrange("(k p) n -> p k n", p=P)).then_inc(sgu_landed, 16)

            for c in range(TC // 2):
                act.wait_ge(x_landed[c], 16)
                wait(act, sq_done, c)
                act.activation(junk[:, 0], x_rows[:, c], ACT.Square,
                               accum_out=ss[:, c:c + 1]).then_inc(sq_done, 1)
            act.wait_ge(ones_made, 2)
            act.wait_ge(sq_done, TC // 2)
            act.wait_ge(sq_dve, TC // 2)
            act.activation(ss[:], ss[:], ACT.Sqrt, scale=1.0 / D, bias=eps[:]).then_inc(rms_done, 1)
            act.wait_ge(rstd_done, 1)
            for c in range(TC // 2, TC):
                act.activation(x_rows[:, c], x_rows[:, c], ACT.Copy, scale=rstd[:, c:c + 1]).then_inc(x_scaled, 1)
            act.wait_ge(cols_turned, 1)
            act.activation(cols[:], bank[0][:, 0:116], ACT.Copy).then_inc(cols_ready, 1)
            act.wait_ge(cols_ready, 1)
            for k in range(DK):
                act.wait_ge(turned, k + 1)
                act.activation(act_hi[:, k], bank[4 + k % 4][:], ACT.Copy, scale=cols[:, G_MIX + k:G_MIX + k + 1]).then_inc(turned_hi, 1)
            def result(ph, i, u, g=0, upto=None):
                q = ph.nq if upto is None else upto
                act.wait_ge(quarters_done, ph.quarter(i, u) + q)
                return bank[(ph.group0 + ph.ng * u + g) % 2]

            ph = PH["c"]
            def cmp_streams(i):
                for u in range(2):
                    src = result(ph, i, u)
                    for g in range(2):
                        act.activation(kv_src[0:HD, ds(i, 1), 2 * u + g, :], src[g * HD:(g + 1) * HD, :], ACT.Copy)
                        a = act.activation(kv_src[HD:P, ds(i, 1), 2 * u + g, 0:T - 1], src[g * HD:(g + 1) * HD, 1:T], ACT.Copy)
                    a.then_inc(banks_read, 1)
            runs(act, ph.n // 2, cmp_streams)
            ph = PH["q"]
            def queries(i):
                for u in range(2):
                    act.activation(q_t[:, ds(i * 2 + u, 1), :], result(ph, i, u)[:], ACT.Copy, scale=HD ** -0.5).then_inc(banks_read, 1)
            runs(act, ph.n // 2, queries)
            for s in range(2):
                for hh in range(2):
                    act.wait_ge(hid_done, 2 * s + hh + 1)
                    act.activation(hid_t[s][:, hh], bank[4 + 2 * s + hh][:, 0:GROUPS * NCMP], ACT.Gelu_apprx_tanh,
                                   bias=cols[:, B1_K + 2 * s + hh:B1_K + 2 * s + hh + 1]).then_inc(hid_act, 1)
            ph = PH["k"]
            def keys(i):
                for u in range(2):
                    src = result(ph, i, u)
                    for g in range(2):
                        a = act.activation(k_t[:, ds(i, 1), 2 * u + g, :], src[g * HD:(g + 1) * HD, :], ACT.Copy)
                    a.then_inc(banks_read, 1)
            runs(act, ph.n // 2, keys)
            act.wait_ge(cmp_out, 1)
            act.activation(kc_t[:], bank[2][0:HD, 0:GROUPS * NCMP], ACT.Copy).then_inc(cmp_ready, 1)
            act.wait_ge(cmp_out, 2)
            act.activation(vc[:].rearrange("n g d -> n (g d)"), bank[3][0:NCMP, 0:GROUPS * HD], ACT.Copy).then_inc(cmp_ready, 1)
            ph = PH["v"]
            def values(i):
                for u in range(2):
                    n = i * 2 + u
                    src = result(ph, i, u)
                    wait(act, kv_turned, n - 1)
                    act.activation(vt[:, u], src[:], ACT.Copy).then_inc(banks_read, 1)
                    if u == 1:
                        value_rows(n - 1, i, 0)
                    elif not (isinstance(i, int) and n == 0):
                        value_rows(n - 1, i - 1, 1)
            def value_rows(n, i, u):
                act.wait_ge(kv_turned, n + 1)
                dst = v_kv[:, i] if isinstance(i, int) else v_kv[:, ds(i, 1)].rearrange("p a c f -> p (a c) f")
                act.activation(dst[:, :, u * P:(u + 1) * P], bank[2 + u][:].rearrange("p (c f) -> p c f", c=TC), ACT.Copy).then_inc(kv_rows_done, 1)
            runs(act, ph.n // 2, values, peel=True)
            ph = PH["g"]
            act.activation(gate_t[:], result(ph, 0, 0)[0:48, :], ACT.Copy).then_inc(banks_read, 1)
            value_rows(3, 1, 1)
            act.wait_ge(kv_turned, 5)
            act.activation(gates[:].rearrange("p c g -> p (c g)"), bank[2][:, 0:TC * 48], ACT.Sigmoid).then_inc(gates_done, 1)

            ph = PH["merge"]
            def attention(j):
                n0 = j * ITEMS
                for pr in range(2):
                    if pr == 1:
                        act.activation(vcg[:], vc[:, ds(j, 1), :].rearrange("n a d -> n (a d)"), ACT.Copy).then_inc(staged, 1)
                    for e in range(2):
                        act.activation(qs[:, 2 * pr + e], q_t[e * HD:(e + 1) * HD, ds(j * 2 + pr, 1), :], ACT.Copy).then_inc(staged, 1)
                for step in range(STEPS):
                    if step < ITEMS:
                        pr, qi, e, b = items[step]
                        n = NCMP if b == 0 else (qi + 1) * P
                        unit = step // 6
                        act.wait_ge(max_done, n0 + step + 1)
                        if step >= 3:
                            act.wait_ge(pt_done, n0 + step - 2)
                        if step % 6 == 0 and unit >= 2:
                            act.wait_ge(o_scaled, j * UNITS + unit - 1)
                        act.activation(prob[:, step % 3, 0:n], bank[2 + step % 2][:, 0:n], ACT.Exp,
                                       bias=neg_max[:, step % 4:step % 4 + 1],
                                       accum_out=den[:, unit % 2, e * 3 + b:e * 3 + b + 1]).then_inc(exp_done, 1)
                    if step >= OT_LAG and (step - OT_LAG) % 6 == 0:
                        unit = (step - OT_LAG) // 6
                        act.wait_ge(o_turned, j * UNITS + unit + 1)
                        act.activation(oa_hi[:, ds(j * 2 + unit // TC, 1), unit % TC * P:(unit % TC + 1) * P],
                                       bank[6 + unit % 2][:, 6 * HD:6 * HD + P], ACT.Copy).then_inc(oa_hi_done, 1)
                    for k in (QUARTERS_AT[step - 1] if step else []) + (QUARTERS_AT[step] if step == STEPS - 1 else []):
                        if k % 4 == 3:
                            p = k // 4
                            act.wait_ge(quarters_done, j * 32 + ph.quarter0 + k + 1)
                            wait(act, gate_stored[p % 2], j * 64 + 16 * (p // 2))
                            act.activation(gate_out[:, p % 2], bank[(ph.group0 + p) % 2][:], ACT.Copy).then_inc(banks_read, 1)
                            act.wait_ge(banks_read, j * 8 + ph.group0 + p + 1)
                            act.dma_start(merge_dram[ds((j * 8 + p) * P, P), :], gate_out[:, p % 2]).then_inc(gate_stored[p % 2], 16)
            runs(act, GROUPS, attention, peel=True)

            act.wait_ge(oa_lo_done, GROUPS * UNITS)
            act.dma_start(ws_rows[:], sgu_ws[0].rearrange("g t s -> t g s")).then_inc(ws_landed, 16)
            ph = PH["sv"]
            def v_out(n, u):
                act.wait_ge(v_turned, n + 1)
                act.activation(v_rows[:, :, ds(n * P, P)], bank[2 + u][:].rearrange("p (c f) -> p c f", c=TC), ACT.Copy).then_inc(v_rows_done, 1)
            def sgu_v(i):
                for u in range(2):
                    n = i * 2 + u
                    src = result(ph, i, u)
                    wait(act, v_turned, n - 1)
                    act.activation(sv_t[:, u], src[:], ACT.Gelu_apprx_tanh).then_inc(banks_read, 1)
                    if not (isinstance(i, int) and n == 0):
                        v_out(n - 1, 1 - u)
            sgu_v(0)
            act.wait_ge(ws_turned, 1)
            for h in range(2):
                act.activation(ws_t[:, 4 * h:4 * h + 4].rearrange("p g t -> p (g t)"), bank[4 + h][:], ACT.Copy).then_inc(ws_ready, 1)
            with act.Fori(1, ph.n // 2) as i:
                sgu_v(i)
            v_out(ph.n - 1, 1)
            act.wait_ge(ln_stats, 3 * TC)
            act.activation(ln_shift[:], mv_stat[:, :, 1], ACT.Sqrt, bias=eps[:]).then_inc(ln_sqrt, 1)
            act.wait_ge(ln_ready, 2)

            ph = PH["su"]
            def mix_out(n, u):
                act.wait_ge(mix_done, n + 1)
                wait(act, ob_done, n)
                act.activation(mixed[:].rearrange("p c t -> p (c t)"), bank[2 + u][:], ACT.Copy).then_inc(mix_copied, 1)
                act.wait_ge(ob_done, n + 1)
                act.activation(ob_hi[:, ds(n, 1), :], ob[:], ACT.Copy).then_inc(ob_hi_done, 1)
            def rows_in(n, u):
                for r, src in enumerate((sgu_ln_g[0], sgu_ln_b[0], sgu_b[0].rearrange("g t -> (g t)"))):
                    act.dma_start(rows_bc[:, u, r], src[ds(n * P, P)].partition_broadcast(P)).then_inc(rows_landed[u], 16)
            def sgu_u(i):
                for u in range(2):
                    n = i * 2 + u
                    wait(act, vn_done, n - 1)
                    for c in range(TC):
                        a = act.activation(vz[:, u, c], v_rows[:, c, ds(n * P, P)], ACT.Identity,
                                           scale=ln_rstd[:, c:c + 1], bias=ln_shift[:, c:c + 1])
                    a.then_inc(vz_done, 1)
                    src = result(ph, i, u)
                    wait(act, ob_done, n - 1)
                    act.activation(ut[:, u], src[:], ACT.Gelu_apprx_tanh).then_inc(banks_read, 1)
                    if not (isinstance(i, int) and n == 0):
                        mix_out(n - 1, 1 - u)
                    if not (isinstance(i, int) and n in (0, SG - 1)):
                        rows_in(n + 1, 1 - u)
            rows_in(0, 0)
            rows_in(1, 1)
            runs(act, ph.n // 2 - 1, sgu_u, peel=True)
            sgu_u(ph.n // 2 - 1)
            mix_out(ph.n - 1, 1)

            ph = PH["ab"]
            def merge_hi(n, u):
                act.wait_ge(merge_done, n + 1)
                act.activation(act_hi[:, ds(n, 1), :], merged[:, u], ACT.Copy).then_inc(merge_hi_done, 1)
            def ab(i):
                for u in range(2):
                    n = i * 2 + u
                    src = result(ph, i, u, 0, 2)
                    wait(act, merge_done, n - 1)
                    act.activation(pa[:, u], src[:], ACT.Copy).then_inc(banks_read, 1)
                    if not (isinstance(i, int) and n == 0):
                        merge_hi(n - 1, 1 - u)
                    src = result(ph, i, u, 1, 4)
                    act.activation(pb[:, u], src[:], ACT.Copy).then_inc(banks_read, 1)
                    act.wait_ge(gates_landed[u], i * 32 + 32)
                    act.activation(gate_in[:, u], gate_in[:, u], ACT.Sigmoid).then_inc(gates_open, 1)
            ab(0)
            ab(1)
            act.wait_ge(mem_landed, 16)
            for c in range(MC):
                wait(act, mem_sq, c)
                act.activation(mem_junk[:], mem_rows[:, c], ACT.Square, accum_out=ss[:, c:c + 1]).then_inc(mem_sq, 1)
            act.wait_ge(mem_sq, MC)
            act.activation(rstd[:, 0:MC], ss[:, 0:MC], ACT.Sqrt, scale=1.0 / D, bias=eps[:]).then_inc(mem_rms, 1)
            with act.Fori(2, ph.n // 2) as i:
                ab(i)
            merge_hi(ph.n - 1, 1)

            ph = PH["wo"]
            act.wait_ge(mem_rstd, 1)
            def wo(i):
                for u in range(2):
                    n = i * 2 + u
                    wait(act, mem_turned, n - 1)
                    for c in range(MC):
                        a = act.activation(mem_cols[:, u, c], mem_rows[:, c, ds(n * P, P)], ACT.Copy, scale=rstd[:, c:c + 1])
                    a.then_inc(mem_cols_done, 1)
                    src = result(ph, i, u)
                    wait(act, summed, n - 1)
                    act.activation(sq[:, u], src[:], ACT.Square).then_inc(squared, 1)
                    act.activation(xt[:, ds(n, 1), :], src[:], ACT.Copy).then_inc(banks_read, 1)
                    act.wait_ge(mem_turned, n + 1)
                    act.activation(hm_hi[:, ds(n, 1), :], bank[2 + u][:, 0:MEM], ACT.Copy, scale=cols[:, ds(n + G_MEM, 1)]).then_inc(mem_hi, 1)
            runs(act, ph.n // 2, wo, peel=True)

            def root(n, buf):
                act.wait_ge(norm_sum, n + 1)
                act.activation(buf[:], bank[4][:], ACT.Sqrt, scale=1.0 / D, bias=eps[:]).then_inc(norm_root, 1)

            def split_hi(k, done):
                act.wait_ge(xg_done, done + k + 1)
                act.activation(act_hi[:, k], xg[:, k % 2], ACT.Copy).then_inc(xg_hi, 1)

            k = 0
            for n in range(8):
                if n == 1:
                    root(0, rms_bc)
                for _ in range(NORMED_AT[n]):
                    split_hi(k, 0)
                    k += 1
                ph = PH["mk" if n < 4 else "mv"]
                i, u = n % 4 // 2, n % 2
                src = result(ph, i, u)
                if n < 4:
                    act.activation(mk_t[:, n], src[:, 0:MEM], ACT.Copy).then_inc(banks_read, 1)
                else:
                    wait(act, mvt_turned, n - 5)
                    act.activation(mv_t[:, u], src[:, 0:MEM], ACT.Copy).then_inc(banks_read, 1)
                    act.wait_ge(mvt_turned, n - 3)
                    act.activation(mv_rows[:, :, (n - 4) * P:(n - 3) * P], bank[2 + u][:, 0:MEM].rearrange("p (c f) -> p c f", c=MC), ACT.Copy).then_inc(mv_ready, 1)
            while k < DK:
                split_hi(k, 0)
                k += 1
            ph = PH["mq"]
            for step in range(M_STEPS + 1):
                if step in (4, 8, 12, 16):
                    h = step // 4 - 1
                    act.activation(mq_t[:, h], result(ph, h // 2, h % 2)[:], ACT.Copy, scale=P ** -0.5).then_inc(banks_read, 1)
                t = step - M_LAG
                if 0 <= t < M_ITEMS:
                    act.wait_ge(m_max, t + 1)
                    wait(act, m_norm, t - 2)
                    act.activation(m_prob[:, t % 3], bank[2 + t % 2][:, 0:MEM], ACT.Exp, bias=neg_max[:, t % 4:t % 4 + 1],
                                   accum_out=den[:, 0, t % 3:t % 3 + 1]).then_inc(m_exp, 1)
                t = step - M_PV_LAG - 1
                if t >= 0 and t % TC == TC - 1:
                    h = t // TC
                    act.wait_ge(m_pv, TC * (h + 1))
                    act.activation(mo_hi[:, h], bank[6 + h % 2][:], ACT.Copy).then_inc(mo_hi_done, 1)

            def add_out(ph, i, u, g, n, tile, total):
                src = result(ph, i, u, g, g + 1 if ph.ng > 1 else None)
                wait(act, added, n - 1)
                act.activation(add_in[:, g % 2 if ph.ng > 1 else u], src[:], ACT.Copy).then_inc(banks_read, 1)

            def square(n, tile, b, buf, sq0):
                act.wait_ge(added, n + 1)
                wait(act, summed, sq0 - 1)
                act.activation(buf, xt[:, ds(tile, 1), :], ACT.Square).then_inc(squared, 1)

            def gained_high(n):
                act.activation(act_hi[:, ds(n, 1), :], xt[:, ds(n, 1), :], ACT.Copy, scale=cols[:, ds(n + G_FFN, 1)]).then_inc(xg_hi, 1)

            ph = PH["mo"]
            def mo(i):
                for u in range(2):
                    for j in range(4):
                        n = (i * 2 + u) * 4 + j
                        add_out(ph, i, u, j, n, n, DK)
                        if not (isinstance(i, int) and n == 0):
                            square(n - 1, n - 1, 1 - j % 2, sq[:, 1 - j % 2], DK + n - 1)
                            gained_high(n - 1)
            runs(act, ph.n // 2, mo, peel=True)
            square(DK - 1, DK - 1, 1, sq[:, 1], 2 * DK - 1)
            gained_high(DK - 1)
            root(1, ffn_rms_bc)
            tiles = 0
            n_add = DK
            for c, nk in enumerate(FFN_CHUNKS):
                ph = PH[f"f{c}"]
                act.wait_ge(added, n_add)
                def fi(i):
                    src = result(ph, i, 0)
                    wait(act, ff_done, tiles + i)
                    act.activation(gated[:], src[:], ACT.Copy).then_inc(banks_read, 1)
                    act.wait_ge(gate_scaled, 2 * (tiles + i) + 1)
                    act.activation(gated[:], gated[:], ACT.Silu).then_inc(gate_silu, 1)
                    src = result(ph, i, 1)
                    act.activation(up[:], src[:], ACT.Copy).then_inc(banks_read, 1)
                    act.wait_ge(ff_done, tiles + i + 1)
                    act.activation(ff_hi[:, ds(i, 1), :], ff[:], ACT.Copy).then_inc(ff_hi_done, 1)
                runs(act, nk, fi, peel=c == 0)
                tiles += nk
                ph = PH[f"o{c}"]
                last = c == len(FFN_CHUNKS) - 1
                def y_out(n, u):
                    act.wait_ge(y_turned, n + 1)
                    act.activation(y_rows[:, :, ds(n * P, P)], bank[2 + u][:].rearrange("p (c f) -> p c f", c=TC), ACT.Copy).then_inc(y_copied, 1)
                def fo(i):
                    for u in range(2):
                        n = i * 2 + u
                        src = result(ph, i, u)
                        wait(act, added, n_add + n - 1)
                        act.activation(add_in[:, u], src[:], ACT.Copy).then_inc(banks_read, 1)
                        if last:
                            act.wait_ge(added, n_add + n + 1)
                            wait(act, summed, 2 * DK + n)
                            act.activation(ff[:], x_out[:, u], ACT.Square).then_inc(squared, 1)
                            if not (isinstance(i, int) and n == 0):
                                y_out(n - 1, 1 - u)
                if last:
                    act.wait_ge(ff_lo_done, FK)
                    act.dma_start(final_g_bc[:], norm_final_g.partition_broadcast(P)).then_inc(final_g_landed, 16)
                runs(act, ph.n // 2, fo, peel=last)
                n_add += DK
            y_out(DK - 1, 1)
            act.wait_ge(norm_sum, 3)
            act.activation(ss[:], bank[4][:, 0:TC], ACT.Sqrt, scale=1.0 / D, bias=eps[:]).then_inc(norm_root, 1)

        @block.gpsimd
        def _(pool):
            pool.memset(ident[:], 0.0).then_inc(ident_zero, 1)
            pool.memset(ident_b[:], 0.0).then_inc(ident_zero, 1)
            pool.wait_ge(ident_zero, 2)
            for m in (ident, ident_b):
                pool.affine_select(out=m[:], in_=m[:], compare_op=ALU.not_equal, fill=1.0, base=0,
                                   pattern=[[-1, P]], channel_multiplier=1).then_inc(ident_made, 1)
            pool.memset(causal_b[:], 0.0).then_inc(masks_zero, 1)
            pool.memset(cmp_mask_b[:], 0.0).then_inc(masks_zero, 1)
            pool.memset(valid[:], 1.0).then_inc(masks_zero, 1)
            pool.wait_ge(masks_zero, 3)
            pool.affine_select(out=causal_b[:], in_=causal_b[:], compare_op=ALU.is_ge, fill=MASKED, base=0,
                               pattern=[[-1, P]], channel_multiplier=1).then_inc(masks_made, 1)
            pool.affine_select(out=cmp_mask_b[:], in_=cmp_mask_b[:], compare_op=ALU.is_ge, fill=MASKED, base=1 - CMP_LEN,
                               pattern=[[P, TC], [-CMP_STEP, NCMP]], channel_multiplier=1).then_inc(masks_made, 1)
            pool.affine_select(out=valid[:], in_=valid[:], compare_op=ALU.is_ge, fill=0.0, base=1 - CMP_LEN,
                               pattern=[[0, 1]], channel_multiplier=1).then_inc(masks_made, 1)
            pool.wait_ge(banks_read, PH["c"].groups_end())
            for s in range(2):
                for g in range(GROUPS):
                    src = kv_src[:, s, g].rearrange("p (n k a) -> p a k n", k=8, a=2)[:, 0]
                    for h in range(2):
                        pe_col = (PE_K, PE_V)[s] + 8 * h
                        a = pool.tensor_tensor(blocks[s][:, 8 * h:8 * h + 8, g], src[:, :, h:h + NCMP],
                                               cols[:, pe_col:pe_col + 8].unsqueeze(2).broadcast_to([P, 8, NCMP]), ALU.add)
                a.then_inc(blocks_done, 1)
            pool.wait_ge(gates_done, 1)
            g0 = gates[:, 0].rearrange("p (h b) -> p b h", b=3)[:, 0]
            pool.tensor_scalar(g0, g0, valid[:], None, ALU.mult).then_inc(gates_masked, 1)

            pool.wait_ge(ws_landed, 16)
            pool.affine_select(out=ws_rows[:], in_=ws_rows[:], compare_op=ALU.is_ge, fill=0.0, base=0,
                               pattern=[[0, SG], [-1, P]], channel_multiplier=1).then_inc(ws_masked, 1)

            ph = PH["su"]
            def gate_out_tile(n, u):
                pool.wait_ge(mix_copied, n + 1)
                pool.tensor_tensor(mixed[:], mixed[:], rows_bc[:, u, 2].unsqueeze(1).broadcast_to([P, TC, P]), ALU.add).then_inc(ob_step, 1)
                pool.wait_ge(ob_step, n + 1)
                wait(pool, ob_lo_done, n)
                pool.tensor_tensor(ob[:], mixed[:].rearrange("p c t -> p (c t)"), ut[:, u], ALU.mult).then_inc(ob_done, 1)
                pool.wait_ge(ob_hi_done, n + 1)
                pool.tensor_tensor(ob_lo[:, ds(n, 1), :], ob[:], ob_hi[:, ds(n, 1), :].bitcast(F32), ALU.subtract).then_inc(ob_lo_done, 1)
            def sgu_u(i):
                for u in range(2):
                    n = i * 2 + u
                    pool.wait_ge(rows_landed[u], i * 48 + 48)
                    pool.wait_ge(vz_done, n + 1)
                    wait(pool, mix_done, n - 1)
                    pool.tensor_tensor(vz[:, u], vz[:, u], rows_bc[:, u, 0].unsqueeze(1).broadcast_to([P, TC, P]), ALU.mult).then_inc(vn_step, 1)
                    pool.wait_ge(vn_step, n + 1)
                    pool.tensor_tensor(vn[:, u], vz[:, u], rows_bc[:, u, 1].unsqueeze(1).broadcast_to([P, TC, P]), ALU.add).then_inc(vn_done, 1)
                    if not (isinstance(i, int) and n == 0):
                        gate_out_tile(n - 1, 1 - u)
            runs(pool, ph.n // 2, sgu_u, peel=True)
            gate_out_tile(ph.n - 1, 1)

            ph = PH["ab"]
            def ab(i):
                for u in range(2):
                    n = i * 2 + u
                    pool.wait_ge(gates_open, n + 1)
                    pool.wait_ge(banks_read, ph.group(i, u) + 2)
                    pool.tensor_tensor(pa[:, u], pa[:, u], gate_in[:, u, 0], ALU.mult).then_inc(merge_step, 1)
                    pool.tensor_tensor(pb[:, u], pb[:, u], gate_in[:, u, 1], ALU.mult).then_inc(merge_step, 1)
                    pool.wait_ge(merge_step, n * 2 + 2)
                    pool.tensor_tensor(merged[:, u], pa[:, u], pb[:, u], ALU.add).then_inc(merge_done, 1)
                    pool.wait_ge(merge_hi_done, n + 1)
                    pool.tensor_tensor(act_lo[:, ds(n, 1), :], merged[:, u], act_hi[:, ds(n, 1), :].bitcast(F32), ALU.subtract).then_inc(merge_lo_done, 1)
            runs(pool, ph.n // 2, ab)

            def clear(buf, n):
                pool.memset(buf[:], 0.0).then_inc(sumsq_zero, 1)
                pool.wait_ge(sumsq_zero, n)

            def total(buf, sqr, n):
                pool.wait_ge(squared, n + 1)
                wait(pool, summed, n)
                pool.tensor_tensor(buf[:], buf[:], sqr, ALU.add).then_inc(summed, 1)

            def split_lo(k, done):
                pool.wait_ge(xg_hi, done + k + 1)
                pool.tensor_tensor(act_lo[:, k], xg[:, k % 2], act_hi[:, k].bitcast(F32), ALU.subtract).then_inc(xg_lo, 1)

            clear(sumsq, 1)
            def wo(i):
                for u in range(2):
                    total(sumsq, sq[:, u], i * 2 + u)
            runs(pool, DK // 2, wo, peel=True)
            for k in range(DK):
                split_lo(k, 0)

            pool.wait_ge(norm_sum, 1)
            clear(sumsq, 2)
            ph = PH["mo"]
            def mo(i):
                for u in range(2):
                    for j in range(4):
                        n = (i * 2 + u) * 4 + j
                        pool.wait_ge(banks_read, ph.group(i, u) + j + 1)
                        pool.tensor_tensor(xt[:, ds(n, 1), :], xt[:, ds(n, 1), :], add_in[:, j % 2], ALU.add).then_inc(added, 1)
                        if not (isinstance(i, int) and n == 0):
                            total(sumsq, sq[:, 1 - j % 2], n - 1 + DK)
            runs(pool, ph.n // 2, mo, peel=True)
            total(sumsq, sq[:, 1], 2 * DK - 1)

            clear(sumsq_f, 3)
            pool.wait_ge(norm_inv, 2)
            tiles = 0
            for c, nk in enumerate(FFN_CHUNKS):
                ph = PH[f"f{c}"]
                def fi(i):
                    pool.wait_ge(banks_read, ph.group(i, 0) + 1)
                    pool.tensor_tensor(gated[:], gated[:], ffn_rms_bc[:], ALU.mult).then_inc(gate_scaled, 1)
                    pool.wait_ge(gate_silu, tiles + i + 1)
                    pool.tensor_tensor(gated[:], gated[:], ffn_rms_bc[:], ALU.mult).then_inc(gate_scaled, 1)
                    pool.wait_ge(banks_read, ph.group(i, 1) + 1)
                    pool.wait_ge(gate_scaled, 2 * (tiles + i) + 2)
                    wait(pool, ff_lo_done, i + tiles)
                    pool.tensor_tensor(ff[:], gated[:], up[:], ALU.mult).then_inc(ff_done, 1)
                    pool.wait_ge(ff_hi_done, i + tiles + 1)
                    pool.tensor_tensor(ff_lo[:, ds(i, 1), :], ff[:], ff_hi[:, ds(i, 1), :].bitcast(F32), ALU.subtract).then_inc(ff_lo_done, 1)
                runs(pool, nk, fi, peel=c == 0)
                tiles += nk
                ph = PH[f"o{c}"]
                last = c == len(FFN_CHUNKS) - 1
                def fo(i):
                    for u in range(2):
                        n = i * 2 + u
                        pool.wait_ge(banks_read, ph.group(i, u) + 1)
                        if last:
                            wait(pool, y_turned, n - 1)
                        pool.tensor_tensor(x_out[:, u] if last else xt[:, ds(n, 1), :], xt[:, ds(n, 1), :].rearrange("p a t -> p (a t)") if last else xt[:, ds(n, 1), :],
                                           add_in[:, u], ALU.add).then_inc(added, 1)
                        if last:
                            total(sumsq_f, ff[:], n + 2 * DK)
                runs(pool, ph.n // 2, fo, peel=last)


_INS = ["x", "mem", "norm_mix_g", "w_in", "cmp_pe_k", "cmp_k_w1", "cmp_k_b1", "cmp_k_w2", "cmp_pe_v", "cmp_v_w1",
        "cmp_v_b1", "cmp_v_w2", "sgu_ln_g", "sgu_ln_b", "sgu_ws", "sgu_b", "w_proj_a", "w_proj_b", "w_mix_out",
        "norm_cross_g", "norm_mem_g", "w_mq", "w_mkv", "w_mo", "norm_ffn_g", "w_ffn_in", "w_ffn_out", "norm_final_g"]
_OUTS = [((1, T, D), "float32")]


def kernel(**inputs):
    import numpy as _np
    import concourse.bacc as _bacc
    from concourse import mybir as _mybir
    from concourse.bass_utils import run_bass_kernel_spmd as _run

    nc = _bacc.Bacc("TRN2", target_bir_lowering=False, num_devices=1)
    arrays, args = {}, []
    for name in _INS:
        a = _np.ascontiguousarray(inputs[name])
        arrays[f"in_{name}_dram"] = a
        args.append(nc.dram_tensor(f"in_{name}_dram", a.shape, _mybir.dt.from_np(a.dtype), kind="ExternalInput").ap())
    for i, (shape, dtype) in enumerate(_OUTS):
        dt = _mybir.dt.from_np(_np.dtype(dtype))
        args.append(nc.dram_tensor(f"out_{i}_dram", shape, dt, kind="ExternalOutput").ap())
    build(nc, *args)
    r = _run(nc, [arrays], core_ids=[0])
    got = tuple(r.results[0][f"out_{i}_dram"] for i in range(len(_OUTS)))
    return got[0]
```
